# Optimizing a Trainium2 kernel written in Bass

```python
import jax, jax.numpy as jnp
from jax import lax
import numpy as np

D_MODEL = 1024
BATCH = 1
SEQ = 1024
DEPTH = 1

GDN_HEADS = 8
GDN_HEAD_DIM = 128
GDN_WIDTH = GDN_HEADS * GDN_HEAD_DIM
SHORT_CONV = 4
CHUNK = 64
CONF_CH = D_MODEL
CONF_KERNEL = 31
N_EXPERTS = 64
TOP_K = 8
N_GROUPS = 8
TOPK_GROUPS = 4
EXPERT_FF = 256
SHARED_FF = 256
ROUTED_SCALE = 2.5
EXPERT_BLOCK = 128
DEEPNORM_ALPHA = (2 * DEPTH) ** 0.25
DEEPNORM_BETA = (8 * DEPTH) ** -0.25
EPS = 1e-6
N_IN = 4 * GDN_WIDTH + 2 * GDN_HEADS + 2 * CONF_CH + 2 * D_MODEL

kernel_name = "hybrid_gdn_conformer_moe_deepnorm"

def layer_norm(x, g, b):
    xf = x.astype(jnp.float32)
    mu = jnp.mean(xf, axis=-1, keepdims=True)
    var = jnp.mean(jnp.square(xf - mu), axis=-1, keepdims=True)
    y = (xf - mu) * lax.rsqrt(var + EPS) * g.astype(jnp.float32) + b.astype(jnp.float32)
    return y.astype(x.dtype)

def l2norm(x):
    return x * lax.rsqrt(jnp.sum(jnp.square(x), axis=-1, keepdims=True) + EPS)

def causal_depthwise_conv(x, w):
    k, c = w.shape
    return lax.conv_general_dilated(
        x, w[:, None, :], window_strides=(1,), padding=[(k - 1, 0)],
        dimension_numbers=("NWC", "WIO", "NWC"), feature_group_count=c)

def gated_delta_rule(q, k, v, g, beta):
    b_, s_, h_, dk = q.shape
    dv = v.shape[-1]
    n = s_ // CHUNK

    def chunks(t):
        return t.astype(jnp.float32).reshape(b_, n, CHUNK, h_, -1).transpose(0, 3, 1, 2, 4)

    q = chunks(q) * (dk ** -0.5)
    k = chunks(k)
    v = chunks(v)
    g = g.astype(jnp.float32).reshape(b_, n, CHUNK, h_).transpose(0, 3, 1, 2)
    beta = beta.astype(jnp.float32).reshape(b_, n, CHUNK, h_).transpose(0, 3, 1, 2)
    gc = jnp.cumsum(g, axis=-1)

    idx = jnp.arange(CHUNK)
    causal = idx[:, None] >= idx[None, :]
    strict = idx[:, None] > idx[None, :]
    diff = gc[..., :, None] - gc[..., None, :]
    decay = jnp.where(causal, jnp.exp(jnp.where(causal, diff, 0.0)), 0.0)

    k_beta = k * beta[..., None]
    a_mat = jnp.where(strict, jnp.einsum("bhncd,bhnsd->bhncs", k_beta, k) * decay, 0.0)
    rhs = jnp.concatenate([v * beta[..., None], k_beta * jnp.exp(gc)[..., None]], axis=-1)
    sol = lax.linalg.triangular_solve(a_mat, rhs, left_side=True, lower=True, unit_diagonal=True)
    u, w = sol[..., :dv], sol[..., dv:]

    qk = jnp.einsum("bhncd,bhnsd->bhncs", q, k) * decay
    q_dec = q * jnp.exp(gc)[..., None]
    k_dec = k * jnp.exp(gc[..., -1:] - gc)[..., None]
    g_last = jnp.exp(gc[..., -1])

    def step(state, xs):
        u_c, w_c, qk_c, qd_c, kd_c, gl_c = xs
        v_new = u_c - jnp.einsum("bhcd,bhdv->bhcv", w_c, state)
        o_c = (jnp.einsum("bhcd,bhdv->bhcv", qd_c, state)
               + jnp.einsum("bhcs,bhsv->bhcv", qk_c, v_new))
        state = state * gl_c[..., None, None] + jnp.einsum("bhcd,bhcv->bhdv", kd_c, v_new)
        return state, o_c

    xs = tuple(jnp.moveaxis(t, 2, 0) for t in (u, w, qk, q_dec, k_dec, g_last))
    state0 = jnp.zeros((b_, h_, dk, dv), jnp.float32)
    _, o = lax.scan(step, state0, xs)
    return o.transpose(1, 0, 3, 2, 4).reshape(b_, s_, h_, dv)

def hybrid_mixer(x, w_in, conv_qkv, a_log, dt_bias, o_norm_g, w_oa,
                 dw_w, dw_b, cln_g, cln_b, w_ob, w_o):
    b_, s_, _ = x.shape
    proj = x @ w_in
    cuts = [3 * GDN_WIDTH, 4 * GDN_WIDTH, 4 * GDN_WIDTH + GDN_HEADS,
            4 * GDN_WIDTH + 2 * GDN_HEADS, 4 * GDN_WIDTH + 2 * GDN_HEADS + 2 * CONF_CH,
            4 * GDN_WIDTH + 2 * GDN_HEADS + 2 * CONF_CH + D_MODEL]
    qkv, z, a_raw, b_raw, glu, gate_a, gate_b = jnp.split(proj, cuts, axis=-1)

    qkv = jax.nn.silu(causal_depthwise_conv(qkv, conv_qkv))
    q, k, v = jnp.split(qkv, 3, axis=-1)
    q = l2norm(q.reshape(b_, s_, GDN_HEADS, GDN_HEAD_DIM).astype(jnp.float32))
    k = l2norm(k.reshape(b_, s_, GDN_HEADS, GDN_HEAD_DIM).astype(jnp.float32))
    v = v.reshape(b_, s_, GDN_HEADS, GDN_HEAD_DIM)
    g = -jnp.exp(a_log.astype(jnp.float32)) * jax.nn.softplus(
        a_raw.astype(jnp.float32) + dt_bias.astype(jnp.float32))
    beta = jax.nn.sigmoid(b_raw.astype(jnp.float32))
    o = gated_delta_rule(q, k, v, g, beta)
    o = o * lax.rsqrt(jnp.mean(jnp.square(o), axis=-1, keepdims=True) + EPS) * o_norm_g.astype(jnp.float32)
    o = o * jax.nn.silu(z.reshape(b_, s_, GDN_HEADS, GDN_HEAD_DIM).astype(jnp.float32))
    branch_a = o.reshape(b_, s_, GDN_WIDTH).astype(x.dtype) @ w_oa

    u = glu[..., :CONF_CH] * jax.nn.sigmoid(glu[..., CONF_CH:])
    u = causal_depthwise_conv(u, dw_w) + dw_b
    u = jax.nn.silu(layer_norm(u, cln_g, cln_b))
    branch_b = u @ w_ob

    h = jax.nn.sigmoid(gate_a) * branch_a + jax.nn.sigmoid(gate_b) * branch_b
    return h @ w_o

def route(xf, w_router, router_bias):
    t = xf.shape[0]
    s = jax.nn.sigmoid((xf @ w_router).astype(jnp.float32))
    biased = s + router_bias.astype(jnp.float32)
    grp = biased.reshape(t, N_GROUPS, N_EXPERTS // N_GROUPS)
    grp_score = jnp.sum(lax.top_k(grp, 2)[0], axis=-1)
    _, gidx = lax.top_k(grp_score, TOPK_GROUPS)
    gmask = jnp.sum(jax.nn.one_hot(gidx, N_GROUPS, dtype=jnp.float32), axis=-2)
    emask = jnp.repeat(gmask, N_EXPERTS // N_GROUPS, axis=-1) > 0
    _, eidx = lax.top_k(jnp.where(emask, biased, -jnp.inf), TOP_K)
    wts = jnp.take_along_axis(s, eidx, axis=-1)
    wts = wts / jnp.sum(wts, axis=-1, keepdims=True) * ROUTED_SCALE
    return eidx.astype(jnp.int32), wts

def routed_experts(xf, eidx, wts, w_gate, w_up, w_down):
    t, d = xf.shape
    n_assign = t * TOP_K
    n_blocks = -(-(n_assign + N_EXPERTS * (EXPERT_BLOCK - 1)) // EXPERT_BLOCK)
    n_rows = n_blocks * EXPERT_BLOCK
    e_flat = eidx.reshape(-1)
    tok_flat = jnp.repeat(jnp.arange(t, dtype=jnp.int32), TOP_K)
    w_flat = wts.reshape(-1)
    order = jnp.argsort(e_flat)
    e_s, tok_s, w_s = e_flat[order], tok_flat[order], w_flat[order]
    counts = jnp.zeros((N_EXPERTS,), jnp.int32).at[e_flat].add(1)
    padded = (counts + EXPERT_BLOCK - 1) // EXPERT_BLOCK * EXPERT_BLOCK
    start = jnp.cumsum(counts) - counts
    pend = jnp.cumsum(padded)
    pstart = pend - padded
    dest = pstart[e_s] + (jnp.arange(n_assign, dtype=jnp.int32) - start[e_s])
    row_tok = jnp.full((n_rows,), t, jnp.int32).at[dest].set(tok_s)
    row_w = jnp.zeros((n_rows,), xf.dtype).at[dest].set(w_s.astype(xf.dtype))
    block_start = jnp.arange(n_blocks, dtype=jnp.int32) * EXPERT_BLOCK
    block_e = jnp.minimum(jnp.searchsorted(pend, block_start, side="right"), N_EXPERTS - 1)
    x_pad = jnp.concatenate([xf, jnp.zeros((1, d), xf.dtype)], axis=0)
    xb = x_pad[row_tok].reshape(n_blocks, EXPERT_BLOCK, d)

    def expert_block(args):
        xblk, e = args
        hid = jax.nn.silu(xblk @ w_gate[e]) * (xblk @ w_up[e])
        return hid @ w_down[e]

    yb = lax.map(expert_block, (xb, block_e)).reshape(n_rows, d)
    y = jax.ops.segment_sum(yb * row_w[:, None], row_tok, num_segments=t + 1)
    return y[:t]

def moe_ffn(x, w_router, router_bias, w_gate_e, w_up_e, w_down_e, w_sh_gate, w_sh_up, w_sh_down):
    b_, s_, d = x.shape
    xf = x.reshape(b_ * s_, d)
    eidx, wts = route(xf, w_router, router_bias)
    routed = routed_experts(xf, eidx, wts, w_gate_e, w_up_e, w_down_e)
    shared = (jax.nn.silu(xf @ w_sh_gate) * (xf @ w_sh_up)) @ w_sh_down
    return (routed + shared).reshape(b_, s_, d)

def setup_inputs(seed: int = 0) -> dict:
    key = jax.random.key(seed)
    ks = jax.random.split(key, 26)
    L, D = DEPTH, D_MODEL
    f32 = jnp.float32

    def nrm(k, shape, scale):
        return jax.random.normal(k, shape, f32) * scale

    dt = jnp.exp(jax.random.uniform(ks[4], (L, GDN_HEADS), f32, jnp.log(1e-3), jnp.log(1e-1)))
    return {
        "x": nrm(ks[0], (BATCH, SEQ, D), 1.0),
        "w_in": nrm(ks[1], (L, D, N_IN), D ** -0.5),
        "conv_qkv": nrm(ks[2], (L, SHORT_CONV, 3 * GDN_WIDTH), SHORT_CONV ** -0.5),
        "a_log": jnp.log(jax.random.uniform(ks[3], (L, GDN_HEADS), f32, 1.0, 16.0)),
        "dt_bias": dt + jnp.log(-jnp.expm1(-dt)),
        "o_norm_g": 1.0 + nrm(ks[5], (L, GDN_HEAD_DIM), 0.02),
        "w_oa": nrm(ks[6], (L, GDN_WIDTH, D), GDN_WIDTH ** -0.5 * DEEPNORM_BETA),
        "dw_w": nrm(ks[7], (L, CONF_KERNEL, CONF_CH), CONF_KERNEL ** -0.5),
        "dw_b": nrm(ks[8], (L, CONF_CH), 0.02),
        "cln_g": 1.0 + nrm(ks[9], (L, CONF_CH), 0.02),
        "cln_b": nrm(ks[10], (L, CONF_CH), 0.02),
        "w_ob": nrm(ks[11], (L, CONF_CH, D), CONF_CH ** -0.5 * DEEPNORM_BETA),
        "w_o": nrm(ks[12], (L, D, D), D ** -0.5 * DEEPNORM_BETA),
        "ln1_g": 1.0 + nrm(ks[13], (L, D), 0.02),
        "ln1_b": nrm(ks[14], (L, D), 0.02),
        "w_router": nrm(ks[15], (L, D, N_EXPERTS), D ** -0.5),
        "router_bias": nrm(ks[16], (L, N_EXPERTS), 0.01),
        "w_gate_e": nrm(ks[17], (L, N_EXPERTS, D, EXPERT_FF), D ** -0.5),
        "w_up_e": nrm(ks[18], (L, N_EXPERTS, D, EXPERT_FF), D ** -0.5),
        "w_down_e": nrm(ks[19], (L, N_EXPERTS, EXPERT_FF, D), EXPERT_FF ** -0.5 * DEEPNORM_BETA),
        "w_sh_gate": nrm(ks[20], (L, D, SHARED_FF), D ** -0.5),
        "w_sh_up": nrm(ks[21], (L, D, SHARED_FF), D ** -0.5),
        "w_sh_down": nrm(ks[22], (L, SHARED_FF, D), SHARED_FF ** -0.5 * DEEPNORM_BETA),
        "ln2_g": 1.0 + nrm(ks[23], (L, D), 0.02),
        "ln2_b": nrm(ks[24], (L, D), 0.02),
    }

def reference(x, w_in, conv_qkv, a_log, dt_bias, o_norm_g, w_oa, dw_w, dw_b, cln_g, cln_b,
              w_ob, w_o, ln1_g, ln1_b, w_router, router_bias, w_gate_e, w_up_e, w_down_e,
              w_sh_gate, w_sh_up, w_sh_down, ln2_g, ln2_b):
    for l in range(DEPTH):
        mix = hybrid_mixer(x, w_in[l], conv_qkv[l], a_log[l], dt_bias[l], o_norm_g[l], w_oa[l],
                           dw_w[l], dw_b[l], cln_g[l], cln_b[l], w_ob[l], w_o[l])
        x = layer_norm(DEEPNORM_ALPHA * x + mix, ln1_g[l], ln1_b[l])
        ffn = moe_ffn(x, w_router[l], router_bias[l], w_gate_e[l], w_up_e[l], w_down_e[l],
                      w_sh_gate[l], w_sh_up[l], w_sh_down[l])
        x = layer_norm(DEEPNORM_ALPHA * x + ffn, ln2_g[l], ln2_b[l])
    return x


_drawn_inputs = setup_inputs


def setup_inputs(seed=0):
    import zlib

    import numpy as np

    out = dict(_drawn_inputs(seed))
    spreads = {}
    factors = {'o_norm_g': 4.456,
     'dw_b': 3.043,
     'cln_g': 4.027,
     'cln_b': 5.512,
     'ln2_g': 2.907,
     'ln2_b': 2.848}
    for name, (base, spread) in spreads.items():
        noise = np.random.default_rng([zlib.crc32(name.encode()), seed]).standard_normal(out[name].shape)
        drawn = base * np.exp(spread * noise) if base else spread * noise
        out[name] = __import__('jax').numpy.asarray(drawn.astype(out[name].dtype))
    for name, factor in factors.items():
        out[name] = (out[name] * factor).astype(out[name].dtype)
    return out
```

```python
from contextlib import ExitStack

import concourse.bass as bass
from concourse import mybir

F32 = mybir.dt.float32
F32R = mybir.dt.float32r
I32 = mybir.dt.int32
U32 = mybir.dt.uint32
ALU = mybir.AluOpType
ACT = mybir.ActivationFunctionType
AX = mybir.AxisListType

P = 128
S = 1024
D = 1024
KT = D // P
NT = S // P
HALF = 512
H = 8
GH = 2
NG = H // GH
NPAIR = NT // 2
TAPS_S, TAPS_L = 4, 31
E = 64
FF = 256
NGRP = 8
TOPK = 8
EPS = 1e-6
ALPHA = 2.0 ** 0.25
ROUTED_SCALE = 2.5
NEG = -1.0e30
BIG = 3.0e38
LEVELS = 7
NROW = S + P
COL_QKVZ, COL_AB, COL_GLU, COL_GA = 0, 4 * D, 4 * D + 2 * H, 6 * D + 2 * H
COL_GB = COL_GA + D
R_DW, R_DWB, R_CG, R_CB, R_SC = 0, 31, 32, 33, 34
N_PAR = R_SC + 3 * TAPS_S


def split3(nc, out, w_hi, w_lo, x_hi, x_lo, first, last):
    nc.tensor.matmul(out, w_hi, x_hi, start=first, stop=False)
    nc.tensor.matmul(out, w_hi, x_lo, start=False, stop=False)
    return nc.tensor.matmul(out, w_lo, x_hi, start=False, stop=last)


def alone(eng, passed):
    eng.sem_inc(passed, 1)


class Kernel:
    def __init__(self, nc, a):
        self.nc, self.a = nc, a
        self.stage_sems = []

    def sems(self, ctx, *names):
        out = [self.nc.alloc_semaphore(n) for n in names]
        self.stage_sems += out
        return out[0] if len(out) == 1 else out

    def end_stage(self):
        self.nc.all_engine_barrier()
        self.nc.clear_and_free_semaphores(self.stage_sems)
        self.nc.all_engine_barrier()
        self.stage_sems = []

    def sb(self, ctx, name, shape, dt=F32):
        return ctx.enter_context(self.nc.sbuf_tensor(name, shape, dt))

    def ring(self, ctx, tag):
        r = {}
        r["raw"] = [self.sb(ctx, f"{tag}_raw{j}", [P, KT, P]) for j in range(2)]
        r["hi"] = [self.sb(ctx, f"{tag}_hi{j}", [P, KT, P], F32R) for j in range(2)]
        r["lo"] = [self.sb(ctx, f"{tag}_lo{j}", [P, KT, P], F32R) for j in range(2)]
        r["loaded"] = [self.sems(ctx, f"{tag}_loaded{j}") for j in range(2)]
        r["raw_free"], r["hi_ready"], r["w_ready"], r["w_free"] = self.sems(
            ctx, f"{tag}_raw_free", f"{tag}_hi_ready", f"{tag}_w_ready", f"{tag}_w_free")
        return r

    def ring_load(self, sp, r, n2, j, src):
        sp.wait_ge(r["raw_free"], n2 * 2 + j + 1)
        sp.dma_start(r["raw"][j][:], src).then_inc(r["loaded"][j], 16)

    def ring_hi(self, act, r, n2, j):
        act.wait_ge(r["loaded"][j], n2 * 16 + 16)
        act.wait_ge(r["w_free"], n2 * 2 + j + 1)
        self.nc.scalar.activation(r["hi"][j][:], r["raw"][j][:], ACT.Copy).then_inc(r["hi_ready"], 1)

    def ring_lo(self, dve, r, n2, j):
        dve.wait_ge(r["hi_ready"], n2 * 2 + j + 1)
        self.nc.vector.tensor_tensor(r["lo"][j][:], r["raw"][j][:], r["hi"][j][:].bitcast(F32),
                                     ALU.subtract).then_inc(r["w_ready"], 1)
        dve.wait_ge(r["w_ready"], n2 * 2 + j + 1)
        dve.sem_inc(r["raw_free"], 1)

    def constants(self):
        nc, ctx, a = self.nc, self.ctx, self.a
        self.passed = nc.alloc_semaphore("passed")
        sb = self.sb
        self.ident = sb(ctx, "ident", [P, P])
        self.ones = sb(ctx, "ones", [P, P])
        self.eps = sb(ctx, "eps", [P, 1])
        self.last_row = sb(ctx, "last_row", [P, P])
        self.tri_excl = sb(ctx, "tri_excl", [P, P])
        self.neg_mask = sb(ctx, "neg_mask", [P, P])
        self.lvl_mask = sb(ctx, "lvl_mask", [P, LEVELS, P])
        self.par = sb(ctx, "par", [P, KT, N_PAR])
        self.ong = sb(ctx, "ong", [P, 1])
        self.gcol_neg = sb(ctx, "gcol_neg", [P, NT, H])
        self.bcol = sb(ctx, "bcol", [P, NT, H])
        self.nbecol = sb(ctx, "nbecol", [P, NT, H])
        self.kdcol = sb(ctx, "kdcol", [P, NT, H])
        self.gc_d = nc.dram_tensor("gc_rows", (H, S), F32, kind="Internal").ap()
        self.be_d = nc.dram_tensor("beta_rows", (H, S), F32, kind="Internal").ap()
        self.o_d = nc.dram_tensor("o_rows", (D, S), F32, kind="Internal").ap()
        self.hb_d = nc.dram_tensor("hb_rows", (D, S), F32, kind="Internal").ap()
        self.h_d = nc.dram_tensor("h_rows", (D, S), F32, kind="Internal").ap()
        self.x1_d = nc.dram_tensor("x1_table", (NROW, D), F32, kind="Internal").ap()
        self.y_d = nc.dram_tensor("y_acc", (NROW, D), F32, kind="Internal").ap()
        self.credit_d = nc.dram_tensor("credit", (P, 1), F32, kind="Internal").ap()
        self.slot_d = nc.dram_tensor("slot_pairs", (E * S, 2), F32, kind="Internal").ap()

    def load_x(self):
        nc, a = self.nc, self.a
        with ExitStack() as ctx:
            sb = self.sb
            xtok = sb(ctx, "xtok", [P, NT, D])
            rows = sb(ctx, "par_rows", [N_PAR, D])
            junk = sb(ctx, "fill", [P, HALF, 2])
            wab = sb(ctx, "wab", [P, KT, P])
            wab_hi = sb(ctx, "wab_hi", [P, KT, P], F32R)
            wab_lo = sb(ctx, "wab_lo", [P, KT, P], F32R)
            dtb = sb(ctx, "dtb", [H, 1])
            alog = sb(ctx, "alog", [H, 1])
            b_sig = sb(ctx, "b_sig", [2 * H, S])
            ab_raw = sb(ctx, "ab_raw", [2 * H, S])
            t0, t1, t2 = (sb(ctx, f"g_tmp{i}", [H, S]) for i in range(3))
            gate = sb(ctx, "scan_gate", [H, S])
            gc = sb(ctx, "gc", [H, S])
            gb = sb(ctx, "glast_b", [P, NT * H])
            ecol = sb(ctx, "ecol", [P, NT * H])
            nexpa = sb(ctx, "nexpa", [H, 1])
            brow = sb(ctx, "beta_rows_sb", [H, S])
            x_in = [self.sems(ctx, f"x_in{i}") for i in range(NT)]
            (par_in, wab_in, small_in, c_ready, xt_done, hi_done, lo_done, par_done, par_used,
             ab_hi, ab_lo, ab_done, fill_ready, out_done, dv, av, cols_done, beta_moved, gcol_done, gl_done) = self.sems(
                ctx, "par_in", "wab_in", "small_in", "const_ready", "xt_done", "x_hi_done", "x_lo_done",
                "par_done", "par_used", "ab_hi", "ab_lo", "ab_done", "fill_ready", "out_done", "dve_self",
                "act_self", "cols_done", "beta_moved", "gcol_done", "gl_done")
            tp = ctx.enter_context(nc.psum_tensor("x_ps", [P, 8, 4, P], F32))
            block = ctx.enter_context(nc.Block())

            @block.sync
            def _(sp):
                for i in range(NT):
                    sp.dma_start(xtok[:, i, :], a["x"][0, i * P:(i + 1) * P, :]).then_inc(x_in[i], 16)
                sp.dma_start(rows[R_DW:R_DWB, :], a["dw_w"][0]).then_inc(par_in, 16)
                sp.dma_start(rows[R_DWB:R_DWB + 1, :], a["dw_b"]).then_inc(par_in, 16)
                sp.dma_start(rows[R_CG:R_CG + 1, :], a["cln_g"]).then_inc(par_in, 16)
                sp.dma_start(rows[R_CB:R_CB + 1, :], a["cln_b"]).then_inc(par_in, 16)
                sp.dma_start(rows[R_SC:N_PAR, :],
                             a["conv_qkv"][0].rearrange("t (k c) -> (t k) c", c=D)).then_inc(par_in, 16)
                sp.dma_start(wab[:], a["w_in"][0, :, COL_AB:COL_AB + P].rearrange("(k p) n -> p k n", p=P)
                             ).then_inc(wab_in, 16)
                sp.dma_start(self.ong[:], a["o_norm_g"].rearrange("a n -> n a")).then_inc(small_in, 16)
                sp.dma_start(dtb[:], a["dt_bias"].rearrange("a n -> n a")).then_inc(small_in, 16)
                sp.dma_start(alog[:], a["a_log"].rearrange("a n -> n a")).then_inc(small_in, 16)
                sp.wait_ge(fill_ready, 2)
                sp.dma_start(self.slot_d.rearrange("(p n) o -> p (n o)", p=P),
                             junk[:].rearrange("p n o -> p (n o)")).then_inc(out_done, 16)
                sp.wait_ge(av, 1)
                sp.dma_start(brow[:], b_sig[H:2 * H, :]).then_inc(beta_moved, 16)
                sp.dma_start(self.be_d, b_sig[H:2 * H, :]).then_inc(out_done, 16)
                sp.wait_ge(dv, 7)
                sp.dma_start(self.gc_d, gc[:]).then_inc(out_done, 16)
                sp.wait_ge(out_done, 48)

            @block.gpsimd
            def _(pool):
                g = nc.gpsimd
                chain = [0]

                def link(ins):
                    chain[0] += 1
                    ins.then_inc(c_ready, 1)
                    pool.wait_ge(c_ready, chain[0])

                link(g.memset(self.ones[:], 1.0))
                link(g.memset(self.eps[:], EPS))
                link(g.memset(self.ident[:], 0.0))
                link(g.affine_select(out=self.ident[:], in_=self.ident[:], compare_op=ALU.not_equal, fill=1.0,
                                     base=0, pattern=[[-1, P]], channel_multiplier=1))
                link(g.memset(junk[:], 0.0))
                g.iota(junk[:, :, 0:1].rearrange("p (n c) o -> p n (c o)", c=P), pattern=[[0, HALF // P], [1, P]],
                       base=S, channel_multiplier=0, allow_small_or_imprecise_dtypes=True).then_inc(fill_ready, 2)
                link(g.memset(self.last_row[:], 1.0))
                link(g.affine_select(out=self.last_row[:], in_=self.last_row[:], compare_op=ALU.is_ge, fill=0.0,
                                     base=-(P - 1), pattern=[[0, P]], channel_multiplier=1))
                link(g.memset(self.tri_excl[:], 1.0))
                link(g.affine_select(out=self.tri_excl[:], in_=self.tri_excl[:], compare_op=ALU.is_gt, fill=0.0,
                                     base=0, pattern=[[1, P]], channel_multiplier=-1))
                link(g.memset(self.neg_mask[:], 0.0))
                link(g.affine_select(out=self.neg_mask[:], in_=self.neg_mask[:], compare_op=ALU.is_ge, fill=NEG,
                                     base=0, pattern=[[1, P]], channel_multiplier=-1))
                for l in range(LEVELS):
                    b = 1 << l
                    m = self.lvl_mask[:, l, :].rearrange("p (m r) -> p m r", r=2 * b)
                    link(g.memset(self.lvl_mask[:, l, :], 1.0))
                    link(g.affine_select(out=m, in_=m, compare_op=ALU.is_ge, fill=0.0, base=0,
                                         pattern=[[-2 * b, P // (2 * b)], [0, 2 * b]], channel_multiplier=1))
                    link(g.affine_select(out=m, in_=m, compare_op=ALU.is_ge, fill=0.0, base=b - 1,
                                         pattern=[[2 * b, P // (2 * b)], [0, 2 * b]], channel_multiplier=-1))
                    link(g.affine_select(out=m, in_=m, compare_op=ALU.is_ge, fill=0.0, base=-b,
                                         pattern=[[0, P // (2 * b)], [1, 2 * b]], channel_multiplier=0))

            @block.tensor
            def _(pe):
                pe.wait_ge(c_ready, 4)
                for i in range(NT):
                    pe.wait_ge(x_in[i], 16)
                    if i >= 4:
                        pe.wait_ge(lo_done, i - 3)
                    for k in range(KT):
                        last = nc.tensor.transpose(tp[:, 2 * (i % 4) + k // 4, k % 4, :],
                                                   xtok[:, i, k * P:(k + 1) * P], self.ident[:])
                    last.then_inc(xt_done, 1)
                pe.wait_ge(par_in, 80)
                pe.wait_ge(lo_done, NT - 3)
                for k in range(KT):
                    last = nc.tensor.transpose(tp[:, k // 4, k % 4, 0:N_PAR], rows[:, k * P:(k + 1) * P],
                                               self.ident[0:N_PAR, 0:N_PAR])
                last.then_inc(par_done, 1)
                pe.wait_ge(ab_lo, 1)
                pe.wait_ge(lo_done, NT)
                for hf in range(2):
                    out = tp[:, 2 + hf, :, :].rearrange("p a b -> p (a b)")
                    for k in range(KT):
                        last = split3(nc, out, wab_hi[:, k, :], wab_lo[:, k, :],
                                      self.x_hi[:, k, hf * HALF:(hf + 1) * HALF],
                                      self.x_lo[:, k, hf * HALF:(hf + 1) * HALF], k == 0, k == KT - 1)
                last.then_inc(ab_done, 1)
                pe.wait_ge(dv, 7)
                pe.wait_ge(beta_moved, 16)
                for t in range(NT):
                    nc.tensor.transpose(tp[:, 4, 0, t * H:(t + 1) * H], gc[:, t * P:(t + 1) * P],
                                        self.ident[0:H, 0:H])
                    last = nc.tensor.transpose(tp[:, 5, 0, t * H:(t + 1) * H], brow[:, t * P:(t + 1) * P],
                                               self.ident[0:H, 0:H])
                last.then_inc(cols_done, 1)
                pe.wait_ge(gcol_done, 1)
                pe.wait_ge(c_ready, 7)
                nc.tensor.matmul(tp[:, 6, 0, 0:NT * H], self.last_row[:],
                                 self.gcol_neg[:].rearrange("p t h -> p (t h)"), start=True, stop=True
                                 ).then_inc(gl_done, 1)

            @block.scalar
            def _(act):
                for i in range(NT):
                    act.wait_ge(xt_done, i + 1)
                    nc.scalar.activation(self.x_hi[:, :, i * P:(i + 1) * P].rearrange("p (b k) t -> p b k t", b=2),
                                         tp[:, 2 * (i % 4):2 * (i % 4) + 2, :, :], ACT.Copy).then_inc(hi_done, 1)
                act.wait_ge(wab_in, 16)
                nc.scalar.activation(wab_hi[:], wab[:], ACT.Copy).then_inc(ab_hi, 1)
                act.wait_ge(ab_done, 1)
                ab_ps = tp[0:2 * H, 2:4, :, :].rearrange("p a b c -> p (a b c)")
                nc.scalar.activation(b_sig[:], ab_ps, ACT.Sigmoid).then_inc(av, 1)
                act.wait_ge(dv, 2)
                nc.scalar.activation(t1[:], t1[:], ACT.Exp, scale=-1.0).then_inc(av, 1)
                nc.scalar.activation(nexpa[:], alog[:], ACT.Exp).then_inc(av, 1)
                act.wait_ge(av, 3)
                nc.scalar.activation(t1[:], t1[:], ACT.Ln, bias=1.0).then_inc(av, 1)
                act.wait_ge(gcol_done, 1)
                nc.scalar.activation(ecol[:], self.gcol_neg[:].rearrange("p t h -> p (t h)"), ACT.Exp,
                                     scale=-1.0).then_inc(av, 1)
                act.wait_ge(dv, 9)
                nc.scalar.activation(self.kdcol[:].rearrange("p t h -> p (t h)"), gb[:], ACT.Exp).then_inc(av, 1)

            @block.vector
            def _(dve):
                v = nc.vector
                for i in range(NT):
                    dve.wait_ge(hi_done, i + 1)
                    sl = self.x_lo[:, :, i * P:(i + 1) * P].rearrange("p (b k) t -> p b k t", b=2)
                    hi = self.x_hi[:, :, i * P:(i + 1) * P].rearrange("p (b k) t -> p b k t", b=2).bitcast(F32)
                    for b in range(2):
                        last = v.tensor_tensor(sl[:, b], tp[:, 2 * (i % 4) + b, :, :], hi[:, b], ALU.subtract)
                    last.then_inc(lo_done, 1)
                dve.wait_ge(ab_hi, 1)
                v.tensor_tensor(wab_lo[:], wab[:], wab_hi[:].bitcast(F32), ALU.subtract).then_inc(ab_lo, 1)
                dve.wait_ge(par_done, 1)
                for b in range(2):
                    last = v.tensor_copy(self.par[:, 4 * b:4 * b + 4, :], tp[:, b, :, 0:N_PAR])
                last.then_inc(par_used, 1)
                v.memset(gate[:], 1.0).then_inc(par_used, 1)
                dve.wait_ge(par_used, 2)
                v.memset(gate[:].rearrange("p (t c) -> p t c", c=P)[:, :, 0:1], 0.0).then_inc(par_used, 1)
                dve.wait_ge(av, 1)
                dve.wait_ge(small_in, 48)
                a_ps = tp[0:H, 2:4, :, :].rearrange("p a b c -> p (a b c)")
                v.tensor_scalar(t0[:], a_ps, dtb[:], None, ALU.add).then_inc(dv, 1)
                dve.wait_ge(dv, 1)
                v.scalar_tensor_tensor(out=t1[:], in0=t0[:], scalar=-1.0, in1=t0[:], op0=ALU.mult, op1=ALU.max).then_inc(dv, 1)
                v.tensor_scalar(t2[:], t0[:], 0.0, None, ALU.max).then_inc(dv, 1)
                dve.wait_ge(av, 4)
                dve.wait_ge(dv, 3)
                v.tensor_tensor(t0[:], t1[:], t2[:], ALU.add).then_inc(dv, 1)
                v.tensor_scalar(nexpa[:], nexpa[:], -1.0, None, ALU.mult).then_inc(dv, 1)
                dve.wait_ge(dv, 5)
                v.tensor_scalar(t2[:], t0[:], nexpa[:], None, ALU.mult).then_inc(dv, 1)
                dve.wait_ge(dv, 6)
                dve.wait_ge(par_used, 3)
                v.tensor_tensor_scan(gc[:], gate[:], t2[:], 0.0, ALU.mult, ALU.add).then_inc(dv, 1)
                dve.wait_ge(cols_done, 1)
                v.tensor_copy(self.bcol[:].rearrange("p t h -> p (t h)"), tp[:, 5, 0, 0:NT * H]).then_inc(dv, 1)
                v.tensor_scalar(self.gcol_neg[:].rearrange("p t h -> p (t h)"), tp[:, 4, 0, 0:NT * H], -1.0, None,
                                ALU.mult).then_inc(gcol_done, 1)
                dve.wait_ge(gl_done, 1)
                dve.wait_ge(gcol_done, 1)
                v.tensor_tensor(gb[:], self.gcol_neg[:].rearrange("p t h -> p (t h)"), tp[:, 6, 0, 0:NT * H],
                                ALU.subtract).then_inc(dv, 1)
                dve.wait_ge(av, 5)
                dve.wait_ge(dv, 8)
                v.scalar_tensor_tensor(out=self.nbecol[:].rearrange("p t h -> p (t h)"), in0=ecol[:], scalar=-1.0,
                                       in1=self.bcol[:].rearrange("p t h -> p (t h)"), op0=ALU.mult,
                                       op1=ALU.mult)


    def project(self, r, out, j, x_hi, x_lo, steps=range(KT), halves=(0, 1)):
        for k in steps:
            for hf in halves:
                last = split3(self.nc, out[:, hf, :], r["hi"][j][:, k, :], r["lo"][j][:, k, :],
                              x_hi[:, k, hf * HALF:(hf + 1) * HALF], x_lo[:, k, hf * HALF:(hf + 1) * HALF],
                              k == 0, k == KT - 1)
        return last

    def w_in_tile(self, col):
        return self.a["w_in"][0, :, bass.ds(col, P)].rearrange("(k p) n -> p k n", p=P)

    def conformer_conv(self, uc):
        nc = self.nc
        PAD = TAPS_L - 1
        with ExitStack() as ctx:
            r = self.ring(ctx, "glu")
            u = [self.sb(ctx, f"u{b}", [P, PAD + S]) for b in range(2)]
            sg = self.sb(ctx, "glu_sig", [P, S])
            pj = [ctx.enter_context(nc.psum_tensor(f"glu_ps{j}", [P, 2, HALF], F32)) for j in range(2)]
            pj_done, pj_free, a_moved, b_sig, sg_free, u_free, taps = self.sems(
                ctx, "glu_pj_done", "glu_pj_free", "glu_a_moved", "glu_b_sig", "glu_sg_free", "glu_u_free",
                "conv_taps")
            block = ctx.enter_context(nc.Block())
            PER_TILE = 1 + 2 * TAPS_L

            @block.sync
            def _(sp):
                sp.sem_inc(r["raw_free"], 2)
                with sp.Fori(0, KT) as c:
                    for j in range(2):
                        self.ring_load(sp, r, c, j, self.w_in_tile(c * P + COL_GLU + j * D))

            @block.tensor
            def _(pe):
                pe.sem_inc(r["w_free"], 2)
                pe.sem_inc(pj_free, 2)
                with pe.Fori(0, KT) as c:
                    for j in range(2):
                        pe.wait_ge(r["w_ready"], c * 2 + j + 1)
                        pe.wait_ge(pj_free, c * 2 + j + 1)
                        self.project(r, pj[j], j, self.x_hi, self.x_lo).then_inc(pj_done, 1)
                        pe.wait_ge(pj_done, c * 2 + j + 1)
                        pe.sem_inc(r["w_free"], 1)

            @block.scalar
            def _(act):
                for b in range(2):
                    nc.scalar.activation(u[b][:, 0:PAD], self.ones[:, 0:PAD], ACT.Copy, scale=0.0)
                act.sem_inc(pj_free, 0) if False else None

                def tile_pair(c2, b, more):
                    c = c2 * 2 + b
                    act.wait_ge(pj_done, c * 2 + 1)
                    act.wait_ge(u_free, c + 1)
                    nc.scalar.activation(u[b][:, PAD:PAD + S], pj[0][:].rearrange("p a b -> p (a b)"),
                                         ACT.Copy).then_inc(a_moved, 1)
                    act.wait_ge(a_moved, c + 1)
                    act.sem_inc(pj_free, 1)
                    if more:
                        self.ring_hi(act, r, c + 1, 0)
                    act.wait_ge(pj_done, c * 2 + 2)
                    act.wait_ge(sg_free, c + 1)
                    nc.scalar.activation(sg[:], pj[1][:].rearrange("p a b -> p (a b)"),
                                         ACT.Sigmoid).then_inc(b_sig, 1)
                    act.wait_ge(b_sig, c + 1)
                    act.sem_inc(pj_free, 1)
                    if more:
                        self.ring_hi(act, r, c + 1, 1)

                for j in range(2):
                    self.ring_hi(act, r, 0, j)
                with act.Fori(0, KT // 2 - 1) as c2:
                    for b in range(2):
                        tile_pair(c2, b, True)
                tile_pair(KT // 2 - 1, 0, True)
                tile_pair(KT // 2 - 1, 1, False)

            @block.vector
            def _(dve):
                v = nc.vector
                dve.sem_inc(u_free, 2)
                dve.sem_inc(sg_free, 1)

                def tile_pair(c2, b, more):
                    c = c2 * 2 + b
                    base = c * PER_TILE
                    if more:
                        self.ring_lo(dve, r, c + 1, 0)
                    dve.wait_ge(a_moved, c + 1)
                    dve.wait_ge(b_sig, c + 1)
                    v.tensor_tensor(u[b][:, PAD:PAD + S], u[b][:, PAD:PAD + S], sg[:], ALU.mult).then_inc(taps, 1)
                    dve.wait_ge(taps, base + 1)
                    dve.sem_inc(sg_free, 1)
                    if more:
                        self.ring_lo(dve, r, c + 1, 1)
                    for t in range(TAPS_L):
                        w = self.par[:, bass.ds(c, 1), R_DW + t]
                        for hf in range(2):
                            acc = uc[:, bass.ds(c, 1), hf * HALF:(hf + 1) * HALF].rearrange("p a t -> p (a t)")
                            src = u[b][:, hf * HALF + t:hf * HALF + t + HALF]
                            if t == 0:
                                ins = v.tensor_scalar(acc, src, w, self.par[:, bass.ds(c, 1), R_DWB],
                                                      ALU.mult, ALU.add)
                            else:
                                dve.wait_ge(taps, base + 2 * t + hf)
                                ins = v.scalar_tensor_tensor(out=acc, in0=src, scalar=w, in1=acc,
                                                             op0=ALU.mult, op1=ALU.add)
                            ins.then_inc(taps, 1)
                    dve.wait_ge(taps, base + PER_TILE)
                    dve.sem_inc(u_free, 1)

                for j in range(2):
                    self.ring_lo(dve, r, 0, j)
                with dve.Fori(0, KT // 2 - 1) as c2:
                    for b in range(2):
                        tile_pair(c2, b, True)
                tile_pair(KT // 2 - 1, 0, True)
                tile_pair(KT // 2 - 1, 1, False)


    def delta_net(self):
        nc, sb, a = self.nc, self.sb, self.a
        PAD = TAPS_S - 1
        with ExitStack() as ctx:
            r = self.ring(ctx, "dn")
            rp = [sb(ctx, f"pre_conv{j}", [P, PAD + S]) for j in range(2)]
            sq = [sb(ctx, f"norm_sq{j}", [P, S]) for j in range(2)]
            zt = sq
            rn = sb(ctx, "norm_r", [P, HALF])
            nxt = sb(ctx, "qkv_next", [P, 3, GH, S])
            cur = sb(ctx, "qkv_cur", [P, 3, GH, S])
            gcb = sb(ctx, "gc_bc", [P, GH, 2 * P])
            beb = sb(ctx, "beta_bc", [P, GH, 2 * P])
            zs = sb(ctx, "z_pair", [P, GH, 2 * P])
            egc, qd, kb = (sb(ctx, n, [P, GH, 2 * P]) for n in ("exp_gc", "q_decayed", "k_beta"))
            ld, at, qk = (sb(ctx, n, [P, 4, P]) for n in ("decay", "a_t", "qk_t"))
            dt = ld
            NA = 4
            atl = [sb(ctx, f"a_lvl{l}", [P, 4, P]) for l in range(NA)]
            xt, xx, yy = (sb(ctx, n, [P, 4, P]) for n in ("inv_t", "inv", "y_sb"))
            kbe, kd, vb = (sb(ctx, n, [P, 4, P]) for n in ("k_beta_e", "k_dec", "v_beta"))
            wt = xx
            vn = sb(ctx, "v_new", [P, GH, P])
            st = sb(ctx, "state", [P, GH, P])
            ob, osq = (sb(ctx, n, [P, 4 * P]) for n in ("o_pair", "o_sq"))
            orn = osq
            z_d = nc.dram_tensor("z_rows", (D, S), F32, kind="Internal").ap()
            pj = [ctx.enter_context(nc.psum_tensor(f"dn_pj{j}", [P, 2, HALF], F32)) for j in range(2)]
            ga, gb, gc, gd = (ctx.enter_context(nc.psum_tensor(f"dn_{n}", [P, 4, P], F32)) for n in "abcd")
            pj_done, pj_moved, conv_sem, silu_done, sq_done, ns_done, rn_done, n_scaled, z_ready, z_stored, cur_ready = \
                self.sems(ctx, "dn_pj_done", "dn_pj_moved", "dn_conv", "dn_silu", "dn_sq", "dn_ns_done", "dn_rn",
                          "dn_scaled", "dn_z_ready", "dn_z_stored", "dn_cur_ready")
            (slices_in, z_in, egc_done, kb_ready, qk_done, ld_ready, dt_done, at_ready, masked, kvt_done, kv_read,
             xt_t, xt_evac, x_upd, y_done, y_evac, z_done, w_done, w_evac, vn_done, vn_evac, o_done, o_read,
             ds_done, s_upd, osq_done, ss_done, orn_done, o_fin, o_stored, ld_sub, act_ln, zero_s) = self.sems(
                ctx, "slices_in", "zs_in", "egc_done", "kb_ready", "qk_done", "ld_ready", "dt_done", "at_ready",
                "masked", "kvt_done", "kv_read", "xt_t", "xt_evac", "x_upd", "y_done", "y_evac", "z_done",
                "w_done", "w_evac", "vn_done", "vn_evac", "o_done", "o_read", "ds_done", "s_upd", "osq_done",
                "ss_done", "orn_done", "o_fin", "o_stored", "ld_sub", "act_ln", "zero_s")
            self.rn_exp, self.qk_sem, self.o_self = self.sems(ctx, "rn_exp", "qk_ready", "o_self")
            block = ctx.enter_context(nc.Block())
            Q, K, V = range(3)
            KIND = (3, 0, 1, 2)
            CONV_TILE = 1 + 2 * TAPS_S
            FLAT = "p a b -> p (a b)"

            def after(eng, sem, value):
                if not isinstance(value, int) or value > 0:
                    eng.wait_ge(sem, value)

            def tok(p, cc):
                return slice((2 * p + cc) * P, (2 * p + cc + 1) * P)

            def conv_no(G, p, j):
                return G * 6 + 2 * (p - 1) + j

            @block.sync
            def _(sp):
                def tile(G, p, j):
                    after(sp, r["w_ready"], G * 8 + 2 * p + j - 1)
                    sp.dma_start(r["raw"][j][:], self.w_in_tile(KIND[p] * D + G * GH * P + j * P)
                                 ).then_inc(r["loaded"][j], 16)

                def slices(g, p):
                    q = g * 4 + p
                    sp.wait_ge(kb_ready, 1 + q)
                    sp.wait_ge(ld_ready, 1 + q)
                    for dst, src in ((gcb, self.gc_d), (beb, self.be_d)):
                        sp.dma_start(dst[:], src[bass.ds(g * GH, GH), 2 * p * P:2 * (p + 1) * P]
                                     .partition_broadcast(P)).then_inc(slices_in, 16)

                def z_slice(g, p):
                    q = g * 4 + p
                    sp.wait_ge(o_fin, 1 + q)
                    sp.wait_ge(z_stored, g * 32 + 32)
                    sp.dma_start(zs[:], z_d[bass.ds(g * GH * P, GH * P), 2 * p * P:2 * (p + 1) * P]
                                 .rearrange("(h p) t -> p h t", p=P)).then_inc(z_in, 16)

                def solve(g, more):
                    for p in range(NPAIR):
                        slices(g, p)
                        if more:
                            for j in range(2):
                                if p < NPAIR - 1:
                                    tile(g + 1, p + 1, j)
                                else:
                                    tile(g + 2, 0, j)
                        z_slice(g, p)

                for sem in (kb_ready, ld_ready, o_fin, act_ln, o_read, s_upd, kvt_done, o_done, masked, self.qk_sem):
                    sp.sem_inc(sem, 1)
                for p in range(NPAIR):
                    for j in range(2):
                        tile(0, p, j)
                for j in range(2):
                    tile(1, 0, j)
                with sp.Fori(0, NG - 1) as g:
                    solve(g, True)
                solve(NG - 1, False)

            @block.tensor
            def _(pe):
                mm, tr = nc.tensor.matmul, nc.tensor.transpose

                def fill(G, p, s):
                    j, k = s // KT, s % KT
                    n = G * 8 + 2 * p + j
                    if k == 0:
                        pe.wait_ge(r["w_ready"], n + 1)
                        after(pe, pj_moved, n - 1)
                    last = self.project(r, pj[j], j, self.x_hi, self.x_lo, steps=(k,))
                    if k == KT - 1:
                        last.then_inc(pj_done, 1)

                def norm_sum(G, p, m, prev_read):
                    pe.wait_ge(sq_done, G * 4 + 2 * (p - 1) + m // 2 + 1)
                    after(pe, rn_done, G * 8 + 4 * (p - 1) + m)
                    mm(gd[:].rearrange(FLAT), self.ones[:],
                       sq[m // 2][:, (m % 2) * HALF:(m % 2 + 1) * HALF], start=True, stop=True
                       ).then_inc(ns_done, 1)

                def solve(g, p, more):
                    q = g * 4 + p
                    G = g + 1

                    def f(s):
                        if more:
                            fill(G, p, s)

                    units = [(hh, cc) for hh in range(GH) for cc in range(2)]
                    if p == 0:
                        pe.wait_ge(cur_ready, g * 3 + 3)
                    pe.wait_ge(kb_ready, 1 + q + 1)
                    pe.wait_ge(act_ln, 1 + q)
                    for u, (hh, cc) in enumerate(units):
                        mm(ga[:, u, :], cur[:, K, hh, tok(p, cc)], kb[:, hh, cc * P:(cc + 1) * P], start=True, stop=True)
                    for u, (hh, cc) in enumerate(units):
                        last = mm(gb[:, u, :], cur[:, K, hh, tok(p, cc)], cur[:, Q, hh, tok(p, cc)], start=True, stop=True)
                    last.then_inc(qk_done, 1)
                    f(0)
                    pe.wait_ge(o_read, 1 + q)
                    pe.wait_ge(s_upd, 1 + 2 * q)
                    for u, (hh, cc) in enumerate(units):
                        tr(gc[:, u, :], cur[:, K, hh, tok(p, cc)], self.ident[:])
                    for u, (hh, cc) in enumerate(units):
                        last = tr(gd[:, u, :], cur[:, V, hh, tok(p, cc)], self.ident[:])
                    last.then_inc(kvt_done, 1)
                    f(1)
                    pe.wait_ge(kv_read, q + 1)
                    pe.wait_ge(x_upd, q * 7 + 1)
                    for u in range(4):
                        last = tr(gc[:, u, :], xt[:, u, :], self.ident[:])
                    last.then_inc(xt_t, 1)
                    f(2)
                    for l in range(1, LEVELS):
                        if l == 1:
                            pe.wait_ge(xt_evac, q * 6 + 1)
                            pe.wait_ge(masked, 1 + q * 7 + 2)
                        else:
                            pe.wait_ge(x_upd, q * 7 + l)
                            pe.wait_ge(masked, 1 + q * 7 + l + 1)
                            for u in range(4):
                                last = tr(gc[:, u, :], xx[:, u, :], self.ident[:])
                            last.then_inc(xt_t, 1)
                        for u in range(4):
                            last = mm(ga[:, u, :], atl[l % NA][:, u, :], xx[:, u, :], start=True, stop=True)
                        last.then_inc(y_done, 1)
                        f(1 + 2 * l)
                        if more and p in (2, 3) and l <= 4:
                            norm_sum(G, p - 1, l - 1, None)
                        pe.wait_ge(y_evac, q * 6 + l)
                        pe.wait_ge(xt_evac, q * 6 + l)
                        for u in range(4):
                            if l < LEVELS - 1:
                                last = mm(gb[:, u, :], xt[:, u, :], yy[:, u, :], start=True, stop=True)
                            else:
                                last = mm(gb[:, u, :], yy[:, u, :], xt[:, u, :], start=True, stop=True)
                        last.then_inc(z_done, 1)
                        f(2 + 2 * l)
                    pe.wait_ge(x_upd, q * 7 + 7)
                    for u in range(4):
                        last = mm(ga[:, u, :], kbe[:, u, :], xt[:, u, :], start=True, stop=True)
                    last.then_inc(w_done, 1)
                    f(15)
                    pe.wait_ge(w_evac, q + 1)
                    for cc in range(2):
                        s = q * 2 + cc
                        pe.wait_ge(s_upd, 1 + s)
                        if p == 0 and cc == 0:
                            pe.wait_ge(zero_s, g + 1)
                        for hh in range(GH):
                            u = 2 * hh + cc
                            mm(gb[:, u, :], xt[:, u, :], vb[:, u, :], start=True, stop=False)
                            last = mm(gb[:, u, :], wt[:, u, :], st[:, hh, :], start=False, stop=True)
                        last.then_inc(vn_done, 1)
                        pe.wait_ge(vn_evac, s + 1)
                        for hh in range(GH):
                            u = 2 * hh + cc
                            last = mm(gd[:, u, :], kd[:, u, :], vn[:, hh, :], start=True, stop=True)
                        for hh in range(GH):
                            u = 2 * hh + cc
                            mm(gc[:, u, :], st[:, hh, :], qd[:, hh, cc * P:(cc + 1) * P], start=True, stop=False)
                            last = mm(gc[:, u, :], vn[:, hh, :], qk[:, u, :], start=False, stop=True)
                        last.then_inc(o_done, 1)
                    pe.wait_ge(osq_done, q + 1)
                    mm(ga[:].rearrange(FLAT), self.ones[:], osq[:], start=True, stop=True).then_inc(ss_done, 1)

                for p in range(NPAIR):
                    for s in range(2 * KT):
                        fill(0, p, s)
                    if p >= 2:
                        for m in range(4):
                            norm_sum(0, p - 1, m, None)
                with pe.Fori(0, NG - 1) as g:
                    for p in range(NPAIR):
                        solve(g, p, True)
                for p in range(NPAIR):
                    solve(NG - 1, p, False)

            @block.scalar
            def _(act):
                A = nc.scalar.activation

                def hi(n2, j, wait_used=None):
                    act.wait_ge(r["loaded"][j], n2 * 16 + 16)
                    if wait_used is not None:
                        act.wait_ge(pj_done, wait_used)
                    A(r["hi"][j][:], r["raw"][j][:], ACT.Copy).then_inc(r["hi_ready"], 1)

                def tile_move(G, p, j):
                    n = G * 8 + 2 * p + j
                    act.wait_ge(pj_done, n + 1)
                    ps = pj[j][:].rearrange(FLAT)
                    if p == 0:
                        after(act, ns_done, G * 8)
                        A(zt[j][:], ps, ACT.Silu).then_inc(pj_moved, 1)
                    else:
                        after(act, conv_sem, conv_no(G, p, j) * (2 * TAPS_S) - 2 * TAPS_S)
                        A(rp[j][:, PAD:PAD + S], ps, ACT.Copy).then_inc(pj_moved, 1)
                    hi(G * 4 + p + 1, j, n + 1)

                def tile_silu(G, p, j):
                    if p == 0:
                        return
                    c = conv_no(G, p, j)
                    act.wait_ge(conv_sem, (c + 1) * 2 * TAPS_S)
                    A(nxt[:, KIND[p], j, :], nxt[:, KIND[p], j, :], ACT.Silu).then_inc(silu_done, 1)
                    if p < 3:
                        act.wait_ge(silu_done, c + 1)
                        if p == 1:
                            act.wait_ge(z_stored, G * 32 + 32)
                        else:
                            act.wait_ge(ns_done, G * 8 + 4 * (p - 1) - 4 + 2 * j + 2)
                        A(sq[j][:], nxt[:, KIND[p], j, :], ACT.Square).then_inc(sq_done, 1)

                def norm(G, p, m):
                    i = G * 8 + 4 * (p - 1) + m
                    act.wait_ge(ns_done, i + 1)
                    after(act, n_scaled, i)
                    A(rn[:], gd[:].rearrange(FLAT), ACT.Ln, bias=self.eps[:]).then_inc(rn_done, 1)
                    act.wait_ge(rn_done, i + 1)
                    A(rn[:], rn[:], ACT.Exp, scale=-0.5).then_inc(self_rn, 1)

                def cur_k(g):
                    act.wait_ge(n_scaled, g * 8 + 8)
                    act.wait_ge(kvt_done, 1 + g * 4)
                    A(cur[:, K], nxt[:, K], ACT.Copy).then_inc(cur_ready, 1)

                def solve(g, p, more):
                    q = g * 4 + p
                    G = g + 1
                    if p == 0:
                        cur_k(g)
                    act.wait_ge(slices_in, q * 32 + 32)
                    act.wait_ge(o_done, 1 + 2 * q)
                    act.wait_ge(s_upd, 1 + 2 * q)
                    A(egc[:].rearrange(FLAT), gcb[:].rearrange(FLAT), ACT.Exp).then_inc(egc_done, 1)
                    act.wait_ge(ld_ready, 1 + q + 1)
                    A(dt[:].rearrange(FLAT), ld[:].rearrange(FLAT), ACT.Exp).then_inc(dt_done, 1)
                    act.wait_ge(xt_t, q * 6 + 1)
                    A(xx[:].rearrange(FLAT), gc[:].rearrange(FLAT), ACT.Copy).then_inc(xt_evac, 1)
                    for l in range(1, LEVELS):
                        act.wait_ge(y_done, q * 6 + l)
                        A(yy[:].rearrange(FLAT), ga[:].rearrange(FLAT), ACT.Copy).then_inc(y_evac, 1)
                        if l > 1:
                            A(xt[:].rearrange(FLAT), gc[:].rearrange(FLAT), ACT.Copy).then_inc(xt_evac, 1)
                        if more and p in (2, 3) and l <= 4:
                            norm(G, p - 1, l - 1)
                        if more and l == 5:
                            tile_move(G, p, 0)
                    act.wait_ge(w_done, q + 1)
                    A(wt[:].rearrange(FLAT), ga[:].rearrange(FLAT), ACT.Copy).then_inc(w_evac, 1)
                    for cc in range(2):
                        act.wait_ge(vn_done, q * 2 + cc + 1)
                        A(vn[:], gb[:].rearrange("p (h c) t -> p h c t", c=2)[:, :, cc, :], ACT.Copy).then_inc(vn_evac, 1)
                    if more:
                        tile_silu(G, p, 0)
                    act.wait_ge(o_read, 1 + q + 1)
                    act.wait_ge(o_fin, 1 + q)
                    A(osq[:], ob[:], ACT.Square).then_inc(osq_done, 1)
                    if more:
                        tile_move(G, p, 1)
                    act.wait_ge(ss_done, q + 1)
                    act.wait_ge(o_fin, 1 + q)
                    A(orn[:], ga[:].rearrange(FLAT), ACT.Ln, scale=1.0 / P, bias=self.eps[:]).then_inc(act_ln, 1)
                    act.wait_ge(act_ln, 1 + q + 1)
                    A(orn[:], orn[:], ACT.Exp, scale=-0.5).then_inc(orn_done, 1)
                    if more:
                        tile_silu(G, p, 1)

                self_rn = self.rn_exp
                for j in range(2):
                    A(rp[j][:, 0:PAD], self.ones[:, 0:PAD], ACT.Copy, scale=0.0)
                    hi(0, j)
                for p in range(NPAIR):
                    for j in range(2):
                        tile_move(0, p, j)
                    if p >= 2:
                        for m in range(4):
                            norm(0, p - 1, m)
                    for j in range(2):
                        tile_silu(0, p, j)
                with act.Fori(0, NG - 1) as g:
                    for p in range(NPAIR):
                        solve(g, p, True)
                for p in range(NPAIR):
                    solve(NG - 1, p, False)

            @block.vector
            def _(dve):
                v = nc.vector
                tt, stt = v.tensor_tensor, v.scalar_tensor_tensor

                def lo(n, j):
                    dve.wait_ge(r["hi_ready"], n + 1)
                    tt(r["lo"][j][:], r["raw"][j][:], r["hi"][j][:].bitcast(F32), ALU.subtract).then_inc(r["w_ready"], 1)

                def conv(G, p, j):
                    n = G * 8 + 2 * p + j
                    lo(n + 2, j)
                    if p == 0:
                        return
                    base = conv_no(G, p, j) * 2 * TAPS_S
                    dve.wait_ge(pj_moved, n + 1)
                    if p == 1 and j == 0:
                        after(dve, cur_ready, G * 3)
                    for t in range(TAPS_S):
                        w = self.par[:, bass.ds(G * GH + j, 1), R_SC + t * 3 + KIND[p]]
                        for hf in range(2):
                            acc = nxt[:, KIND[p], j, hf * HALF:(hf + 1) * HALF]
                            src = rp[j][:, hf * HALF + t:hf * HALF + t + HALF]
                            if t == 0:
                                ins = v.tensor_scalar(acc, src, w, None, ALU.mult)
                            else:
                                dve.wait_ge(conv_sem, base + 2 * t + hf - 1)
                                ins = stt(out=acc, in0=src, scalar=w, in1=acc, op0=ALU.mult, op1=ALU.add)
                            ins.then_inc(conv_sem, 1)

                def scale(G, p, m):
                    dve.wait_ge(self.rn_exp, G * 8 + 4 * (p - 1) + m + 1)
                    sl = nxt[:, KIND[p], m // 2, (m % 2) * HALF:(m % 2 + 1) * HALF]
                    tt(sl, sl, rn[:], ALU.mult).then_inc(n_scaled, 1)

                def solve(g, p, more):
                    q = g * 4 + p
                    G = g + 1
                    if p == 0:
                        dve.wait_ge(n_scaled, g * 8 + 8)
                        dve.wait_ge(o_done, 1 + g * 8)
                        v.tensor_scalar(cur[:, Q], nxt[:, Q], float(P) ** -0.5, None, ALU.mult).then_inc(cur_ready, 1)
                        v.memset(st[:], 0.0).then_inc(zero_s, 1)
                        dve.wait_ge(cur_ready, g * 3 + 3)
                    dve.wait_ge(egc_done, q + 1)
                    dve.wait_ge(slices_in, q * 32 + 32)
                    tsl = slice(2 * p * P, 2 * (p + 1) * P)
                    tt(qd[:], cur[:, Q, :, tsl], egc[:], ALU.mult)
                    tt(kb[:], cur[:, K, :, tsl], beb[:], ALU.mult).then_inc(kb_ready, 1)
                    dve.wait_ge(kvt_done, 1 + q + 1)
                    def col(x):
                        return x[:, 2 * p:2 * p + 2, bass.ds(g * GH, GH)].rearrange("p c h -> p h c")\
                            .unsqueeze(3).to_broadcast([P, GH, 2, P])
                    v4 = lambda x: x[:].rearrange("p (h c) t -> p h c t", c=2)
                    dve.wait_ge(o_done, 1 + 2 * q)
                    tt(v4(kbe), v4(gc), col(self.nbecol), ALU.mult)
                    tt(v4(kd), v4(gc), col(self.kdcol), ALU.mult)
                    tt(v4(vb), v4(gd), col(self.bcol), ALU.mult).then_inc(kv_read, 1)
                    dve.wait_ge(dt_done, q + 1)
                    dve.wait_ge(qk_done, q + 1)
                    dve.wait_ge(masked, 1 + q * 7)
                    tt(at[:], ga[:], dt[:], ALU.mult).then_inc(at_ready, 1)
                    tt(qk[:], gb[:], dt[:], ALU.mult).then_inc(self.qk_sem, 1)
                    dve.wait_ge(masked, 1 + q * 7 + 1)
                    tt(xt[:], self.ident[:].unsqueeze(1).to_broadcast([P, 4, P]), atl[0][:], ALU.subtract).then_inc(x_upd, 1)
                    for l in range(1, LEVELS):
                        dve.wait_ge(z_done, q * 6 + l)
                        dst = xx if l < LEVELS - 1 else xt
                        if l > 1:
                            dve.wait_ge(x_upd, q * 7 + l)
                        tt(dst[:], dst[:], gb[:], ALU.subtract).then_inc(x_upd, 1)
                        if more and l == 1:
                            if p == 0:
                                pass
                        if more and p in (2, 3) and l <= 4:
                            scale(G, p - 1, l - 1)
                        if more and l == 5:
                            conv(G, p, 0)
                    for cc in range(2):
                        dve.wait_ge(o_done, 1 + q * 2 + cc + 1)
                        for hh in range(GH):
                            ins = stt(out=st[:, hh, :], in0=st[:, hh, :],
                                      scalar=egc[:, hh, (cc + 1) * P - 1:(cc + 1) * P], in1=gd[:, 2 * hh + cc, :],
                                      op0=ALU.mult, op1=ALU.add)
                        ins.then_inc(s_upd, 1)
                        if cc == 0:
                            dve.wait_ge(s_upd, 1 + q * 2 + 1)
                    dve.wait_ge(o_stored, 16 + q * 16)
                    v.tensor_copy(ob[:], gc[:].rearrange(FLAT)).then_inc(o_read, 1)
                    if more:
                        conv(G, p, 1)
                    dve.wait_ge(orn_done, q + 1)
                    dve.wait_ge(z_in, q * 16 + 16)
                    stt(out=ob[:], in0=ob[:], scalar=self.ong[:], in1=orn[:], op0=ALU.mult, op1=ALU.mult).then_inc(self.o_self, 1)
                    dve.wait_ge(self.o_self, q + 1)
                    tt(ob[:], ob[:], zs[:].rearrange(FLAT), ALU.mult).then_inc(o_fin, 1)

                for j in range(2):
                    lo(j, j)
                for p in range(NPAIR):
                    for j in range(2):
                        conv(0, p, j)
                    if p >= 2:
                        for m in range(4):
                            scale(0, p - 1, m)
                with dve.Fori(0, NG - 1) as g:
                    for p in range(NPAIR):
                        solve(g, p, True)
                for p in range(NPAIR):
                    solve(NG - 1, p, False)

            @block.gpsimd
            def _(pool):
                tt = nc.gpsimd.tensor_tensor

                def z_store(G):
                    for j in range(2):
                        pool.wait_ge(pj_moved, G * 8 + j + 1)
                        pool.dma_start(z_d[bass.ds(G * GH * P + j * P, P), :], zt[j][:]).then_inc(z_stored, 16)

                def solve(g, p, more):
                    q = g * 4 + p
                    if p == 0:
                        pool.wait_ge(silu_done, g * 6 + 6)
                        pool.wait_ge(kvt_done, 1 + g * 4)
                        alone(pool, self.passed)
                        nc.gpsimd.tensor_copy(cur[:, V], nxt[:, V]).then_inc(cur_ready, 1)
                    pool.wait_ge(slices_in, q * 32 + 32)
                    pool.wait_ge(self.qk_sem, 1 + q)
                    v4 = lambda x: x[:].rearrange("p (h c) t -> p h c t", c=2)
                    tt(v4(ld), gcb[:].rearrange("p h (c t) -> p h c t", c=2),
                       self.gcol_neg[:, 2 * p:2 * p + 2, bass.ds(g * GH, GH)].rearrange("p c h -> p h c")
                       .unsqueeze(3).to_broadcast([P, GH, 2, P]), ALU.add).then_inc(ld_sub, 1)
                    pool.wait_ge(ld_sub, q + 1)
                    tt(ld[:], ld[:], self.neg_mask[:].unsqueeze(1).to_broadcast([P, 4, P]), ALU.add).then_inc(ld_ready, 1)
                    if more and p == 1:
                        z_store(g + 1)
                    pool.wait_ge(at_ready, q + 1)
                    for l in range(LEVELS):
                        if l == NA:
                            pool.wait_ge(x_upd, q * 7 + 1)
                        elif l > NA:
                            pool.wait_ge(y_done, q * 6 + l - NA)
                        tt(atl[l % NA][:], at[:], self.lvl_mask[:, l, :].unsqueeze(1).to_broadcast([P, 4, P]),
                           ALU.mult).then_inc(masked, 1)
                    pool.wait_ge(o_fin, 1 + q + 1)
                    pool.dma_start(self.o_d[bass.ds(g * GH * P, GH * P), 2 * p * P:2 * (p + 1) * P]
                                   .rearrange("(h p) t -> p h t", p=P),
                                   ob[:].rearrange("p (h t) -> p h t", h=GH)).then_inc(o_stored, 16)

                pool.dma_start(self.credit_d, self.ong[:]).then_inc(o_stored, 16)
                z_store(0)
                with pool.Fori(0, NG - 1) as g:
                    for p in range(NPAIR):
                        solve(g, p, True)
                for p in range(NPAIR):
                    solve(NG - 1, p, False)
                pool.wait_ge(o_stored, 16 + NG * NPAIR * 16)


    def branches(self, uc):
        nc, sb, a = self.nc, self.sb, self.a
        with ExitStack() as ctx:
            r = self.ring(ctx, "br")
            src_hi = [sb(ctx, f"br_src_hi{b}", [P, KT, HALF], F32R) for b in range(2)]
            src_lo = [sb(ctx, f"br_src_lo{b}", [P, KT, HALF], F32R) for b in range(2)]
            oh = [sb(ctx, f"o_in{i}", [P, HALF]) for i in range(2)]
            sg = [sb(ctx, f"br_sig{b}", [P, HALF]) for b in range(2)]
            ht = [sb(ctx, f"br_h{b}", [P, HALF]) for b in range(2)]
            rstd = sb(ctx, "cln_rstd", [P, HALF])
            ps = [ctx.enter_context(nc.psum_tensor(f"br_ps{i}", [P, HALF], F32)) for i in range(4)]
            st_m = ctx.enter_context(nc.psum_tensor("cln_sum", [P, HALF], F32))
            st_v = ctx.enter_context(nc.psum_tensor("cln_var", [P, HALF], F32))
            o_in = [self.sems(ctx, f"o_in_sem{i}") for i in range(2)]
            (o_hi, o_lo, mean_done, centred, sqd, var_done, sqrt_done, rstd_done, normed, activated, u_hi, u_lo,
             mm_done, sig_done, ps_read, h_ready, h_stored) = self.sems(
                ctx, "o_hi", "o_lo", "mean_done", "centred", "cln_sq", "var_done", "cln_sqrt", "rstd_done",
                "normed", "activated", "u_hi", "u_lo", "br_mm", "br_sig_done", "br_read", "h_ready", "h_stored")
            self.cln_sq = sg
            block = ctx.enter_context(nc.Block())
            hs = [slice(t * HALF, (t + 1) * HALF) for t in range(2)]
            TILES = 4 * KT

            @block.sync
            def _(sp):
                def tile(t, c, br, j):
                    w = (a["w_oa"], a["w_ob"])[br][0, :, bass.ds(c * P, P)].rearrange("(k p) n -> p k n", p=P)
                    sp.dma_start(r["raw"][j][:], w if j == 0 else self.w_in_tile(c * P + (COL_GA, COL_GB)[br])
                                 ).then_inc(r["loaded"][j], 16)

                for t in range(2):
                    for k in range(KT):
                        n = t * KT + k
                        if n >= 2:
                            sp.wait_ge(o_lo, n - 1)
                        sp.dma_start(oh[k % 2][:], self.o_d[k * P:(k + 1) * P, hs[t]]).then_inc(o_in[k % 2], 16)
                        if k == 1:
                            for j in range(2):
                                if t:
                                    sp.wait_ge(r["w_ready"], t * TILES + j - 1)
                                tile(t, 0, 0, j)
                    for j in range(2):
                        sp.wait_ge(r["w_ready"], t * TILES + j + 1)
                        tile(t, 0, 1, j)
                    with sp.Fori(1, KT) as c:
                        for br in range(2):
                            for j in range(2):
                                sp.wait_ge(r["w_ready"], c * 4 + t * TILES + 2 * br + j - 1)
                                tile(t, c, br, j)

            @block.tensor
            def _(pe):
                mm = nc.tensor.matmul
                for t in range(2):
                    for k in range(KT):
                        last = mm(st_m[:], self.ones[:], uc[:, k, hs[t]], start=k == 0, stop=k == KT - 1)
                    last.then_inc(mean_done, 1)
                    for k in range(KT):
                        pe.wait_ge(sqd, t * KT + k + 1)
                        last = mm(st_v[:], self.ones[:], self.cln_sq[k % 2][:], start=k == 0, stop=k == KT - 1)
                        last.then_inc(var_done, 1)
                    pe.wait_ge(o_lo, (t + 1) * KT)
                    pe.wait_ge(u_lo, (t + 1) * KT)
                    with pe.Fori(0, KT) as c:
                        for br in range(2):
                            for j in range(2):
                                n = c * 4 + t * TILES + 2 * br + j
                                pe.wait_ge(r["w_ready"], n + 1)
                                pe.wait_ge(ps_read, n - 3 + 4)
                                xh, xl = (src_hi[br], src_lo[br]) if j == 0 else (self.x_hi, self.x_lo)
                                sl = slice(0, HALF) if j == 0 else hs[t]
                                for k in range(KT):
                                    last = split3(nc, ps[2 * br + j][:], r["hi"][j][:, k, :], r["lo"][j][:, k, :],
                                                  xh[:, k, sl], xl[:, k, sl], k == 0, k == KT - 1)
                                last.then_inc(mm_done, 1)

            @block.scalar
            def _(act):
                A = nc.scalar.activation

                def hi(n2, j, used):
                    act.wait_ge(r["loaded"][j], n2 * 16 + 16)
                    if used is not None:
                        act.wait_ge(mm_done, used)
                    A(r["hi"][j][:], r["raw"][j][:], ACT.Copy).then_inc(r["hi_ready"], 1)

                for t in range(2):
                    for j in range(2):
                        hi(16 * t, j, 32 * t + j - 1 if t else None)
                    for k in range(KT):
                        n = t * KT + k
                        act.wait_ge(o_in[k % 2], (n // 2 + 1) * 16)
                        if t and k == 0:
                            act.wait_ge(mm_done, TILES)
                        A(src_hi[0][:, k, :], oh[k % 2][:], ACT.Copy).then_inc(o_hi, 1)
                    for k in range(KT):
                        n = t * KT + k
                        act.wait_ge(centred, n + 1)
                        if t and k == 0:
                            act.wait_ge(ps_read, 4 + TILES)
                        if n >= 2:
                            act.wait_ge(var_done, n - 1)
                        A(self.cln_sq[k % 2][:], uc[:, k, hs[t]], ACT.Square).then_inc(sqd, 1)
                    act.wait_ge(var_done, (t + 1) * KT)
                    if t:
                        act.wait_ge(normed, KT)
                    A(rstd[:], st_v[:], ACT.Sqrt, scale=1.0 / D, bias=self.eps[:]).then_inc(sqrt_done, 1)
                    for k in range(KT):
                        n = t * KT + k
                        act.wait_ge(normed, n + 1)
                        A(uc[:, k, hs[t]], uc[:, k, hs[t]], ACT.Silu, scale=self.par[:, k, R_CG:R_CG + 1],
                          bias=self.par[:, k, R_CB:R_CB + 1]).then_inc(activated, 1)

                    def body(c, last_c):
                        for br in range(2):
                            for j in range(2):
                                n = c * 4 + t * TILES + 2 * br + j
                                act.wait_ge(mm_done, n + 1)
                                if j == 1:
                                    act.wait_ge(ps_read, c * 4 + t * TILES + 2 * br - 2 + 4)
                                    A(sg[br][:], ps[2 * br + 1][:], ACT.Sigmoid).then_inc(sig_done, 1)
                                if not (last_c and br):
                                    hi(c * 2 + 16 * t + br + 1, j, n + 1)

                    with act.Fori(0, KT - 1) as c:
                        body(c, False)
                    body(KT - 1, True)

            @block.vector
            def _(dve):
                v = nc.vector
                tt = v.tensor_tensor
                dve.sem_inc(ps_read, 4)

                def lo(n, j):
                    dve.wait_ge(r["hi_ready"], n + 1)
                    tt(r["lo"][j][:], r["raw"][j][:], r["hi"][j][:].bitcast(F32), ALU.subtract).then_inc(r["w_ready"], 1)

                for t in range(2):
                    for j in range(2):
                        lo(TILES * t + j, j)
                    dve.wait_ge(mean_done, t + 1)
                    for k in range(KT):
                        v.scalar_tensor_tensor(out=uc[:, k, hs[t]], in0=st_m[:], scalar=-1.0 / D,
                                               in1=uc[:, k, hs[t]], op0=ALU.mult, op1=ALU.add).then_inc(centred, 1)
                    for k in range(KT):
                        dve.wait_ge(o_hi, t * KT + k + 1)
                        tt(src_lo[0][:, k, :], oh[k % 2][:], src_hi[0][:, k, :].bitcast(F32), ALU.subtract
                           ).then_inc(o_lo, 1)
                    dve.wait_ge(sqrt_done, t + 1)
                    v.reciprocal(rstd[:], rstd[:]).then_inc(rstd_done, 1)
                    dve.wait_ge(rstd_done, t + 1)
                    dve.wait_ge(centred, (t + 1) * KT)
                    for k in range(KT):
                        tt(uc[:, k, hs[t]], uc[:, k, hs[t]], rstd[:], ALU.mult).then_inc(normed, 1)
                    for k in range(KT):
                        dve.wait_ge(u_hi, t * KT + k + 1)
                        tt(src_lo[1][:, k, :], uc[:, k, hs[t]], src_hi[1][:, k, :].bitcast(F32), ALU.subtract
                           ).then_inc(u_lo, 1)

                    def body(c, last_c):
                        i = c + t * KT
                        for br in range(2):
                            for j in range(2):
                                if not (last_c and br):
                                    lo(c * 4 + t * TILES + 2 * br + j + 2, j)
                            dve.wait_ge(sig_done, i * 2 + br + 1)
                            if br == 0:
                                dve.wait_ge(h_stored, 16 + i * 16)
                            tt(ht[br][:], ps[2 * br][:], sg[br][:], ALU.mult).then_inc(ps_read, 2)
                        dve.wait_ge(ps_read, i * 4 + 8)
                        tt(ht[0][:], ht[0][:], ht[1][:], ALU.add).then_inc(h_ready, 1)

                    with dve.Fori(0, KT - 1) as c:
                        body(c, False)
                    body(KT - 1, True)

            @block.gpsimd
            def _(pool):
                pool.dma_start(self.credit_d, self.ong[:]).then_inc(h_stored, 16)
                for t in range(2):
                    for k in range(KT):
                        n = t * KT + k
                        pool.wait_ge(activated, n + 1)
                        nc.gpsimd.tensor_copy(src_hi[1][:, k, :], uc[:, k, hs[t]]).then_inc(u_hi, 1)
                    with pool.Fori(0, KT) as c:
                        pool.wait_ge(h_ready, c + t * KT + 1)
                        pool.dma_start(self.h_d[bass.ds(c * P, P), hs[t]], ht[0][:]).then_inc(h_stored, 16)
                pool.wait_ge(h_stored, 16 + 2 * KT * 16)


    def norm_stats(self, dve, y, stats, mv, sem, base, met=None):
        v = self.nc.vector
        for hf in range(2):
            v.bn_stats(stats[:, hf, :], y[:, hf * HALF:(hf + 1) * HALF]).then_inc(sem, 1)
        dve.wait_ge(sem, base + 2)
        if met is not None:
            alone(dve, met)
        v.bn_aggr(mv[:], stats[:]).then_inc(sem, 1)

    def mix_norm(self):
        nc, sb, a = self.nc, self.sb, self.a
        with ExitStack() as ctx:
            wraw = [sb(ctx, f"wo_raw{j}", [P, KT, P]) for j in range(2)]
            wh = sb(ctx, "wo_hi", [P, KT, D], F32R)
            wl = sb(ctx, "wo_lo", [P, KT, D], F32R)
            hraw = [sb(ctx, f"h_raw{j}", [P, KT, P]) for j in range(2)]
            hh = [sb(ctx, f"h_hi{j}", [P, KT, P], F32R) for j in range(2)]
            hl = [sb(ctx, f"h_lo{j}", [P, KT, P], F32R) for j in range(2)]
            y = [sb(ctx, f"y1_{j}", [P, D]) for j in range(2)]
            g_b = sb(ctx, "ln1_g_b", [P, D])
            b_b = sb(ctx, "ln1_b_b", [P, D])
            stats = sb(ctx, "ln1_stats", [P, 2, 6])
            mv = sb(ctx, "ln1_mv", [P, 2])
            rs = sb(ctx, "ln1_rs", [P, 1])
            zero = sb(ctx, "zeros", [P, D])
            ps = [ctx.enter_context(nc.psum_tensor(f"mix_ps{j}", [P, 2, HALF], F32)) for j in range(2)]
            tp = [ctx.enter_context(nc.psum_tensor(f"x1t_ps{j}", [P, 2, 4, P], F32)) for j in range(2)]
            w_in = [self.sems(ctx, f"wo_in{j}") for j in range(2)]
            h_in = [self.sems(ctx, f"h_in{j}") for j in range(2)]
            xr_in = [self.sems(ctx, f"xres_in{j}") for j in range(2)]
            x1_out = [self.sems(ctx, f"x1_out{j}") for j in range(2)]
            (w_hi, w_lo, h_hi, h_lo, par_in, mm_done, res, st, sq, rstd, nrm, x1_ready, tr_done, th, tl, z_done, z_out) = \
                self.sems(ctx, "wo_hi_s", "wo_lo_s", "h_hi_s", "h_lo_s", "ln1_par", "mix_mm", "ln1_res", "ln1_st",
                          "ln1_sq", "ln1_rstd", "ln1_nrm", "x1_ready", "x1_tr", "x1_hi_s", "x1_lo_s",
                          "zero_done", "zero_out")
            block = ctx.enter_context(nc.Block())

            @block.sync
            def _(sp):
                sp.dma_start(g_b[:], a["ln1_g"][0, :].partition_broadcast(P)).then_inc(par_in, 16)
                sp.dma_start(b_b[:], a["ln1_b"][0, :].partition_broadcast(P)).then_inc(par_in, 16)

                def h_tile(i, j):
                    sp.dma_start(hraw[j][:], self.h_d[:, bass.ds(i * P, P)].rearrange("(k p) t -> p k t", p=P)
                                 ).then_inc(h_in[j], 16)

                def x_tile(i, j):
                    sp.dma_start(y[j][:], a["x"][0, bass.ds(i * P, P), :]).then_inc(xr_in[j], 16)

                for j in range(2):
                    h_tile(j, j)
                    x_tile(j, j)
                for c in range(KT):
                    if c >= 2:
                        sp.wait_ge(w_lo, c - 1)
                    sp.dma_start(wraw[c % 2][:], a["w_o"][0, :, c * P:(c + 1) * P].rearrange("(k p) n -> p k n", p=P)
                                 ).then_inc(w_in[c % 2], 16)
                with sp.Fori(1, NT // 2) as i2:
                    for j in range(2):
                        sp.wait_ge(h_lo, i2 * 2 + j - 1)
                        h_tile(i2 * 2 + j, j)
                        sp.wait_ge(x1_out[j], i2 * 16)
                        sp.wait_ge(tl, i2 * 2 + j)
                        x_tile(i2 * 2 + j, j)

            @block.gpsimd
            def _(pool):
                nc.gpsimd.memset(zero[:], 0.0).then_inc(z_done, 1)
                pool.wait_ge(z_done, 1)
                pool.dma_start(self.x1_d[S:NROW, :], zero[:]).then_inc(z_out, 16)
                pool.dma_start(self.y_d[S:NROW, :], zero[:]).then_inc(z_out, 16)
                with pool.Fori(0, NT // 2) as i2:
                    for j in range(2):
                        i = i2 * 2 + j
                        pool.wait_ge(nrm, i * 3 + 2)
                        nc.gpsimd.tensor_tensor(y[j][:], y[j][:], b_b[:], ALU.add).then_inc(x1_ready, 1)
                        pool.wait_ge(x1_ready, i + 1)
                        pool.dma_start(self.x1_d[bass.ds(i * P, P), :], y[j][:]).then_inc(x1_out[j], 16)
                for j in range(2):
                    pool.wait_ge(x1_out[j], NT // 2 * 16)
                pool.wait_ge(z_out, 32)

            @block.tensor
            def _(pe):
                def transposes(i, j):
                    pe.wait_ge(x1_ready, i + 1)
                    for k in range(KT):
                        last = nc.tensor.transpose(tp[j][:, k // 4, k % 4, :], y[j][:, k * P:(k + 1) * P], self.ident[:])
                    last.then_inc(tr_done, 1)

                def tile(i, j, prev):
                    pe.wait_ge(h_lo, i + 1)
                    pe.wait_ge(res, i)
                    for hf in range(2):
                        for k in range(KT):
                            last = split3(nc, ps[j][:, hf, :], hh[j][:, k, :], hl[j][:, k, :],
                                          wh[:, k, hf * HALF:(hf + 1) * HALF], wl[:, k, hf * HALF:(hf + 1) * HALF],
                                          k == 0, k == KT - 1)
                    last.then_inc(mm_done, 1)
                    if prev:
                        transposes(i - 1, 1 - j)

                pe.wait_ge(w_lo, KT)
                tile(0, 0, False)
                tile(1, 1, True)
                with pe.Fori(1, NT // 2) as i2:
                    for j in range(2):
                        pe.wait_ge(tl, i2 * 2 + j - 1)
                        tile(i2 * 2 + j, j, True)
                transposes(NT - 1, 1)

            @block.scalar
            def _(act):
                A = nc.scalar.activation

                def h_split(n, i2, j, wait):
                    act.wait_ge(h_in[j], i2 * 16 + 16)
                    if wait:
                        act.wait_ge(mm_done, n - 1)
                    A(hh[j][:], hraw[j][:], ACT.Copy).then_inc(h_hi, 1)

                def tile(i, j, more):
                    act.wait_ge(st, i * 3 + 3)
                    A(rs[:], mv[:, 1:2], ACT.Sqrt, bias=self.eps[:]).then_inc(sq, 1)
                    if more is not None:
                        h_split(more * 2 + j, more, j, True)
                    act.wait_ge(tr_done, i + 1)
                    A(self.x1_hi[:, :, bass.ds(i * P, P)].rearrange("p (b k) t -> p b k t", b=2), tp[j][:],
                      ACT.Copy).then_inc(th, 1)

                for j in range(2):
                    h_split(j, 0, j, False)
                for c in range(KT):
                    act.wait_ge(w_in[c % 2], (c // 2 + 1) * 16)
                    A(wh[:, :, c * P:(c + 1) * P], wraw[c % 2][:], ACT.Copy).then_inc(w_hi, 1)
                with act.Fori(0, NT // 2 - 1) as i2:
                    for j in range(2):
                        tile(i2 * 2 + j, j, i2 + 1)
                for j in range(2):
                    tile(NT - 2 + j, j, None)

            @block.vector
            def _(dve):
                v = nc.vector

                def h_split(n, j):
                    dve.wait_ge(h_hi, n + 1)
                    v.tensor_tensor(hl[j][:], hraw[j][:], hh[j][:].bitcast(F32), ALU.subtract).then_inc(h_lo, 1)

                def finish(i, j):
                    dve.wait_ge(th, i + 1)
                    for b in range(2):
                        last = v.tensor_tensor(self.x1_lo[:, 4 * b:4 * b + 4, bass.ds(i * P, P)], tp[j][:, b],
                                               self.x1_hi[:, 4 * b:4 * b + 4, bass.ds(i * P, P)].bitcast(F32),
                                               ALU.subtract)
                    last.then_inc(tl, 1)

                def tile(i, j, i2, more):
                    dve.wait_ge(mm_done, i + 1)
                    dve.wait_ge(xr_in[j], i2 * 16 + 16)
                    v.scalar_tensor_tensor(out=y[j][:], in0=y[j][:], scalar=ALPHA,
                                           in1=ps[j][:].rearrange("p a b -> p (a b)"), op0=ALU.mult, op1=ALU.add
                                           ).then_inc(res, 1)
                    dve.wait_ge(res, i + 2)
                    self.norm_stats(dve, y[j], stats, mv, st, i * 3, self.passed)
                    dve.wait_ge(sq, i + 1)
                    v.reciprocal(rs[:], rs[:]).then_inc(nrm, 1)
                    dve.wait_ge(nrm, i * 3 + 1)
                    v.tensor_scalar(y[j][:], y[j][:], mv[:, 0:1], rs[:], ALU.subtract, ALU.mult).then_inc(rstd, 1)
                    dve.wait_ge(rstd, i + 1)
                    v.tensor_tensor(y[j][:], y[j][:], g_b[:], ALU.mult).then_inc(nrm, 2)
                    if more:
                        h_split(i + 2, j)
                    finish(i, j)

                dve.sem_inc(res, 1)
                dve.sem_inc(tl, 1)
                for j in range(2):
                    h_split(j, j)
                for c in range(KT):
                    dve.wait_ge(w_hi, c + 1)
                    v.tensor_tensor(wl[:, :, c * P:(c + 1) * P], wraw[c % 2][:],
                                    wh[:, :, c * P:(c + 1) * P].bitcast(F32), ALU.subtract).then_inc(w_lo, 1)
                dve.wait_ge(par_in, 32)
                with dve.Fori(0, NT // 2 - 1) as i2:
                    for j in range(2):
                        tile(i2 * 2 + j, j, i2, True)
                for j in range(2):
                    tile(NT - 2 + j, j, NT // 2 - 1, False)

    def shared_and_route(self):
        nc, sb, a = self.nc, self.sb, self.a
        with ExitStack() as ctx:
            wsr = [sb(ctx, f"sh_raw{j}", [P, KT, P]) for j in range(2)]
            wsh = [sb(ctx, f"sh_hi{j}", [P, KT, P], F32R) for j in range(2)]
            wsl = [sb(ctx, f"sh_lo{j}", [P, KT, P], F32R) for j in range(2)]
            wdr = sb(ctx, "shd_raw", [P, 2, D])
            wdh = sb(ctx, "shd_hi", [P, 2, D], F32R)
            wdl = sb(ctx, "shd_lo", [P, 2, D], F32R)
            hid = sb(ctx, "sh_hid", [P, 2, S])
            hidh = sb(ctx, "sh_hid_hi", [P, 2, S], F32R)
            hidl = sb(ctx, "sh_hid_lo", [P, 2, S], F32R)
            yt = [sb(ctx, f"sh_y{j}", [P, D]) for j in range(2)]
            wrr = sb(ctx, "wr_raw", [P, KT, P])
            wrh = sb(ctx, "wr_hi", [P, KT, P], F32R)
            wrl = sb(ctx, "wr_lo", [P, KT, P], F32R)
            sT = sb(ctx, "score_t", [E, S])
            s_, bi, ma, se, we, va, rep = (sb(ctx, n, [P, NT, E]) for n in (
                "score", "biased", "masked_sc", "selected", "weight", "slot_val", "replaced"))
            bias_b = sb(ctx, "bias_b", [P, E])
            g8 = sb(ctx, "group_top", [P, NT * NGRP, 8])
            gs = sb(ctx, "group_score", [P, NT, NGRP])
            cmp_, cmq = (sb(ctx, n, [P, NT * NGRP, NGRP]) for n in ("cmp_gt", "cmp_eq"))
            lt = sb(ctx, "lower_index", [P, NGRP, NGRP])
            grk = sb(ctx, "group_rank", [P, NT * NGRP])
            t8 = sb(ctx, "top8", [P, NT, 8])
            s8 = sb(ctx, "slot8", [P, NT, 8])
            si8 = sb(ctx, "slot8_i", [P, NT * 8], U32)
            sums = sb(ctx, "w_sum", [P, NT])
            ebase = sb(ctx, "e_base", [P, E])
            pair = sb(ctx, "tok_weight", [P, NT * 8, 2])
            eq8 = sb(ctx, "eq8", [P, 8, E])
            cnt = sb(ctx, "count", [P, E])
            thr = sb(ctx, "thr", [P, NT])
            cge = sb(ctx, "cge", [P, E, NT])
            nb = sb(ctx, "n_blocks", [P, E])
            nbc = sb(ctx, "n_blocks_cum", [P, E])
            one_r = sb(ctx, "ones_row", [P, E])
            tmp2 = sb(ctx, "tmp2", [P, 8])
            s_idx = [sb(ctx, f"s_idx{j}", [P, 1], U32) for j in range(1)]
            ps = [ctx.enter_context(nc.psum_tensor(f"sh_ps{j}", [P, 2, HALF], F32)) for j in range(2)]
            rps = ctx.enter_context(nc.psum_tensor("rt_ps", [P, 2, HALF], F32))
            pos_ps = ctx.enter_context(nc.psum_tensor("pos_ps", [P, NT, E], F32))
            cnt_ps = ctx.enter_context(nc.psum_tensor("cnt_ps", [P, HALF], F32))
            w_in = [self.sems(ctx, f"sh_in{j}") for j in range(2)]
            y_in = [self.sems(ctx, f"shx_in{j}") for j in range(2)]
            (wr_in, b_in, wd_in, wr_hi, wr_lo, wr_z, r_mm, r_sig, r_tr, dv, pos_done, cnt_done, fill_in, w_hi, w_lo, mm_s,
             act_s, hid_s, hh_s, hl_s, wdh_s, wdl_s, mm_d, y_add, y_out, pool_c, scat, sl_ready, cut) = self.sems(
                ctx, "wr_in", "rb_in", "shd_in", "wr_hi_s", "wr_lo_s", "wr_z", "r_mm", "r_sig", "r_tr", "rt_dve",
                "pos_done", "cnt_done", "fill_in", "sh_hi_s", "sh_lo_s", "sh_mm", "sh_act", "sh_hid_s",
                "sh_hh", "sh_hl", "shd_hi_s", "shd_lo_s", "sh_dn", "sh_add", "sh_out", "rt_pool", "scat", "sl_ready",
                "cut")
            self.sel_done = self.sems(ctx, "sel_done")
            block = ctx.enter_context(nc.Block())
            fl = lambda x: x.rearrange("p a b -> p (a b)")
            sel_done = self.sel_done

            @block.sync
            def _(sp):
                sp.wait_ge(wr_z, 1)
                sp.dma_start(wrr[:, :, 0:E], a["w_router"][0].rearrange("(k p) n -> p k n", p=P)).then_inc(wr_in, 16)
                sp.dma_start(bias_b[:], a["router_bias"][0, :].partition_broadcast(P)).then_inc(b_in, 16)
                for m in range(4):
                    if m >= 2:
                        sp.wait_ge(w_lo, m - 1)
                    w = (a["w_sh_gate"], a["w_sh_up"])[m % 2][0, :, (m // 2) * P:(m // 2 + 1) * P]
                    sp.dma_start(wsr[m % 2][:], w.rearrange("(k p) n -> p k n", p=P)).then_inc(w_in[m % 2], 16)
                sp.dma_start(wdr[:], a["w_sh_down"][0].rearrange("(c p) n -> p c n", p=P)).then_inc(wd_in, 16)
                for i in range(NT):
                    if i >= 2:
                        sp.wait_ge(y_out, 16 * (i - 1))
                    sp.dma_start(yt[i % 2][:], self.x1_d[i * P:(i + 1) * P, :]).then_inc(y_in[i % 2], 16)
                    if i >= 1:
                        k = i - 1
                        sp.wait_ge(y_add, k + 1)
                        sp.dma_start(self.y_d[k * P:(k + 1) * P, :], yt[k % 2][:]).then_inc(y_out, 16)
                sp.wait_ge(y_add, NT)
                sp.dma_start(self.y_d[S - P:S, :], yt[1][:]).then_inc(y_out, 16)
                sp.wait_ge(y_out, 16 * NT)

            @block.tensor
            def _(pe):
                mm = nc.tensor.matmul
                pe.wait_ge(wr_lo, 1)
                for hf in range(2):
                    for k in range(KT):
                        last = split3(nc, rps[:, hf, :], wrh[:, k, :], wrl[:, k, :],
                                      self.x1_hi[:, k, hf * HALF:(hf + 1) * HALF],
                                      self.x1_lo[:, k, hf * HALF:(hf + 1) * HALF], k == 0, k == KT - 1)
                last.then_inc(r_mm, 1)
                pe.wait_ge(r_sig, 1)
                for t in range(NT):
                    last = nc.tensor.transpose(pos_ps[:, t, :], sT[:, t * P:(t + 1) * P], self.ident[0:E, 0:E])
                last.then_inc(r_tr, 1)

                def up(m):
                    pe.wait_ge(w_lo, m + 1)
                    if m >= 2:
                        pe.wait_ge(hid_s, m // 2)
                    for hf in range(2):
                        for k in range(KT):
                            last = split3(nc, ps[m % 2][:, hf, :], wsh[m % 2][:, k, :], wsl[m % 2][:, k, :],
                                          self.x1_hi[:, k, hf * HALF:(hf + 1) * HALF],
                                          self.x1_lo[:, k, hf * HALF:(hf + 1) * HALF], k == 0, k == KT - 1)
                    last.then_inc(mm_s, 1)

                up(0)
                up(1)
                pe.wait_ge(self.sel_done, 1)
                for t in range(NT):
                    for t2 in range(t):
                        mm(pos_ps[:, t, :], self.ones[:], se[:, t2, :], start=t2 == 0, stop=False)
                    last = mm(pos_ps[:, t, :], self.tri_excl[:], se[:, t, :], start=t == 0, stop=True)
                last.then_inc(pos_done, 1)
                for t in range(NT):
                    last = mm(cnt_ps[:, 0:E], self.ones[:], se[:, t, :], start=t == 0, stop=t == NT - 1)
                last.then_inc(cnt_done, 1)
                up(2)
                up(3)
                pe.wait_ge(wdl_s, 1)
                pe.wait_ge(hl_s, 2)
                for i in range(NT):
                    if i >= 2:
                        pe.wait_ge(y_add, i - 1)
                    for hf in range(2):
                        for c in range(2):
                            last = split3(nc, ps[i % 2][:, hf, :], hidh[:, c, i * P:(i + 1) * P],
                                          hidl[:, c, i * P:(i + 1) * P], wdh[:, c, hf * HALF:(hf + 1) * HALF],
                                          wdl[:, c, hf * HALF:(hf + 1) * HALF], c == 0, c == 1)
                    last.then_inc(mm_d, 1)

            @block.scalar
            def _(act):
                A = nc.scalar.activation
                act.wait_ge(wr_in, 16)
                A(wrh[:], wrr[:], ACT.Copy).then_inc(wr_hi, 1)

                def hi(m):
                    act.wait_ge(w_in[m % 2], (m // 2 + 1) * 16)
                    if m >= 2:
                        act.wait_ge(mm_s, m - 1)
                    A(wsh[m % 2][:], wsr[m % 2][:], ACT.Copy).then_inc(w_hi, 1)

                hi(0)
                hi(1)
                act.wait_ge(r_mm, 1)
                A(sT[:], fl(rps[0:E]), ACT.Sigmoid).then_inc(r_sig, 1)
                for c in range(2):
                    act.wait_ge(mm_s, 2 * c + 1)
                    A(hid[:, c, :], fl(ps[0][:]), ACT.Silu).then_inc(act_s, 1)
                    if c == 0:
                        hi(2)
                        hi(3)
                    act.wait_ge(hid_s, c + 1)
                    A(hidh[:, c, :], hid[:, c, :], ACT.Copy).then_inc(hh_s, 1)
                act.wait_ge(wd_in, 16)
                A(wdh[:], wdr[:], ACT.Copy).then_inc(wdh_s, 1)

            @block.vector
            def _(dve):
                v = nc.vector
                tt = v.tensor_tensor
                n = [0]

                def step(ins):
                    n[0] += 1
                    ins.then_inc(dv, 1)
                    dve.wait_ge(dv, n[0])

                def lo(m):
                    dve.wait_ge(w_hi, m + 1)
                    tt(wsl[m % 2][:], wsr[m % 2][:], wsh[m % 2][:].bitcast(F32), ALU.subtract).then_inc(w_lo, 1)

                def hidden(c):
                    dve.wait_ge(mm_s, 2 * c + 2)
                    dve.wait_ge(act_s, c + 1)
                    tt(hid[:, c, :], hid[:, c, :], fl(ps[1][:]), ALU.mult).then_inc(hid_s, 1)
                    dve.wait_ge(hh_s, c + 1)
                    tt(hidl[:, c, :], hid[:, c, :], hidh[:, c, :].bitcast(F32), ALU.subtract).then_inc(hl_s, 1)

                v.memset(wrr[:], 0.0).then_inc(wr_z, 1)
                dve.wait_ge(wr_hi, 1)
                tt(wrl[:], wrr[:], wrh[:].bitcast(F32), ALU.subtract).then_inc(wr_lo, 1)
                lo(0)
                lo(1)
                dve.wait_ge(r_tr, 1)
                dve.wait_ge(b_in, 16)
                bb = bias_b[:].unsqueeze(1).to_broadcast([P, NT, E])
                step(v.tensor_copy(s_[:], pos_ps[:]))
                step(tt(bi[:], s_[:], bb, ALU.add))
                groups = fl(bi[:]).rearrange("p (g e) -> p g e", e=E // NGRP)
                for i in range(NT * NGRP):
                    last = v.max(g8[:, i, :], groups[:, i, :])
                step(last)
                step(tt(fl(gs[:]).unsqueeze(2), g8[:, :, 0:1], g8[:, :, 1:2], ALU.add))
                gsf = fl(gs[:])
                other = gs[:].unsqueeze(2).to_broadcast([P, NT, NGRP, NGRP])
                mine = gsf.unsqueeze(2).to_broadcast([P, NT * NGRP, NGRP])
                c4 = lambda x: x[:].rearrange("p (t g) o -> p t g o", t=NT)
                mine4 = gs[:].unsqueeze(3).to_broadcast([P, NT, NGRP, NGRP])
                dve.wait_ge(pool_c, 6)
                for t in range(NT):
                    sl = slice(t * NGRP, (t + 1) * NGRP)
                    tt(cmp_[:, sl, :], other[:, t], mine4[:, t], ALU.is_gt)
                    last = tt(cmq[:, sl, :], other[:, t], mine4[:, t], ALU.is_equal)
                step(last)
                step(tt(c4(cmq), c4(cmq), lt[:].unsqueeze(1).to_broadcast([P, NT, NGRP, NGRP]), ALU.mult))
                step(tt(cmp_[:], cmp_[:], cmq[:], ALU.add))
                step(v.tensor_reduce(grk[:], cmp_[:], AX.X, ALU.add))
                step(v.tensor_scalar(grk[:], grk[:], 4.0, None, ALU.is_lt))
                gmask = grk[:].unsqueeze(2).to_broadcast([P, NT * NGRP, E // NGRP])
                mg = fl(ma[:]).rearrange("p (g e) -> p g e", e=E // NGRP)
                rg = fl(rep[:]).rearrange("p (g e) -> p g e", e=E // NGRP)
                step(tt(mg, groups, gmask, ALU.mult))
                step(v.tensor_scalar(grk[:], grk[:], 1.0, BIG, ALU.subtract, ALU.mult))
                step(tt(mg, mg, gmask, ALU.add))
                for t in range(NT):
                    last = v.max(t8[:, t, :], ma[:, t, :])
                step(last)
                for t in range(NT):
                    last = v.match_replace(rep[:, t, :], t8[:, t, :], ma[:, t, :], -3.4e38)
                step(last)
                tt(se[:], rep[:], ma[:], ALU.not_equal).then_inc(self.sel_done, 1)
                dve.wait_ge(self.sel_done, 1)
                step(tt(we[:], s_[:], se[:], ALU.mult))
                step(v.tensor_reduce(sums[:], we[:], AX.X, ALU.add))
                step(v.reciprocal(sums[:], sums[:]))
                step(v.tensor_scalar(sums[:], sums[:], ROUTED_SCALE, None, ALU.mult))
                step(tt(we[:], we[:], sums[:].unsqueeze(2).to_broadcast([P, NT, E]), ALU.mult))
                lo(2)
                lo(3)
                hidden(0)
                dve.wait_ge(pos_done, 1)
                step(tt(va[:], pos_ps[:], ebase[:].unsqueeze(1).to_broadcast([P, NT, E]), ALU.add))
                step(tt(va[:], va[:], se[:], ALU.mult))
                for t in range(NT):
                    last = v.max(s8[:, t, :], va[:, t, :])
                step(last)
                for t in range(NT):
                    step(tt(eq8[:], va[:, t, :].unsqueeze(1).to_broadcast([P, 8, E]),
                            s8[:, t, :].unsqueeze(2).to_broadcast([P, 8, E]), ALU.is_equal))
                    step(tt(eq8[:], eq8[:], we[:, t, :].unsqueeze(1).to_broadcast([P, 8, E]), ALU.mult))
                    step(v.tensor_reduce(tmp2[:], eq8[:], AX.X, ALU.add))
                    step(v.tensor_copy(pair[:, t * 8:(t + 1) * 8, 1:2], tmp2[:].unsqueeze(2)))
                v.tensor_scalar(si8[:], fl(s8[:]), 1.0, None, ALU.subtract).then_inc(sl_ready, 1)
                dve.wait_ge(sl_ready, 1)
                dve.wait_ge(cnt_done, 1)
                step(v.tensor_copy(cnt[:], cnt_ps[:, 0:E]))
                step(tt(cge[:], cnt[:].unsqueeze(2).to_broadcast([P, E, NT]),
                        thr[:].unsqueeze(1).to_broadcast([P, E, NT]), ALU.is_gt))
                step(v.tensor_reduce(nb[:], cge[:], AX.X, ALU.add))
                step(v.memset(one_r[:], 1.0))
                step(v.tensor_tensor_scan(nbc[:], one_r[:], nb[:], 0.0, ALU.mult, ALU.add))
                step(tt(nbc[:], nbc[:], nb[:], ALU.subtract))
                step(v.tensor_copy(self.plan[:, :, 0:1], nb[0:1, :].unsqueeze(2)))
                step(v.tensor_copy(self.plan[:, :, 1:2], nbc[0:1, :].unsqueeze(2)))
                hidden(1)
                dve.wait_ge(wdh_s, 1)
                tt(wdl[:], wdr[:], wdh[:].bitcast(F32), ALU.subtract).then_inc(wdl_s, 1)
                for i in range(NT):
                    dve.wait_ge(mm_d, i + 1)
                    dve.wait_ge(y_in[i % 2], (i // 2 + 1) * 16)
                    v.scalar_tensor_tensor(out=yt[i % 2][:], in0=yt[i % 2][:], scalar=ALPHA, in1=fl(ps[i % 2][:]),
                                           op0=ALU.mult, op1=ALU.add).then_inc(y_add, 1)

            @block.gpsimd
            def _(pool):
                g = nc.gpsimd
                g.memset(lt[:], 1.0).then_inc(pool_c, 1)
                pool.wait_ge(pool_c, 1)
                g.affine_select(out=lt[:], in_=lt[:], compare_op=ALU.is_gt, fill=0.0, base=0,
                                pattern=[[1, NGRP], [-1, NGRP]], channel_multiplier=0).then_inc(pool_c, 1)
                g.iota(ebase[:], pattern=[[S, E]], base=1, channel_multiplier=0,
                       allow_small_or_imprecise_dtypes=True).then_inc(pool_c, 1)
                g.iota(thr[:], pattern=[[P, NT]], base=0, channel_multiplier=0,
                       allow_small_or_imprecise_dtypes=True).then_inc(pool_c, 1)
                pool.wait_ge(pool_c, 4)
                g.memset(thr[:, 0:1], -1.0).then_inc(pool_c, 1)
                g.iota(pair[:, :, 0:1].rearrange("p (t k) o -> p t (k o)", k=8), pattern=[[P, NT], [0, 8]], base=0,
                       channel_multiplier=1, allow_small_or_imprecise_dtypes=True).then_inc(pool_c, 1)
                pool.wait_ge(sl_ready, 1)
                for i in range(NT * 8):
                    pool.indirect_dma_start(self.slot_d, bass.IndirectOffsetOnAxis(si8[:, i:i + 1], 0),
                                            pair[:, i, :], None).then_inc(scat, 16)
                pool.wait_ge(scat, NT * 8 * 16)

    def block_tables(self):
        nc, sb = self.nc, self.sb
        Q = E * NT // P
        with ExitStack() as ctx:
            rows = sb(ctx, "slot_rows", [P, Q, P, 2])
            ps = ctx.enter_context(nc.psum_tensor("tab_ps", [P, 2, Q, P], F32))
            r_in, tr_done, tab = self.sems(ctx, "rows_in", "tab_tr", "tab_done")
            tok = sb(ctx, "tok_rows", [P, Q, P])
            wts = sb(ctx, "wt_rows", [P, Q, P])
            block = ctx.enter_context(nc.Block())

            @block.sync
            def _(sp):
                sp.dma_start(rows[:].rearrange("p q s c -> p q (s c)"),
                             self.slot_d.rearrange("(q p s) c -> p q (s c)", p=P, s=P)).then_inc(r_in, 16)

            @block.vector
            def _(dve):
                v = nc.vector
                dve.wait_ge(r_in, 16)
                v.tensor_copy(tok[:].unsqueeze(3), rows[:, :, :, 0:1])
                v.tensor_copy(wts[:].unsqueeze(3), rows[:, :, :, 1:2]).then_inc(tab, 1)
                dve.wait_ge(tr_done, 1)
                v.tensor_copy(self.tok_tab[:], ps[:, 0].rearrange("p q s -> p (q s)"))
                v.tensor_copy(self.wt_tab[:], ps[:, 1].rearrange("p q s -> p (q s)")).then_inc(tab, 1)

            @block.tensor
            def _(pe):
                pe.wait_ge(tab, 1)
                for q in range(Q):
                    nc.tensor.transpose(ps[:, 0, q, :], tok[:, q, :], self.ident[:])
                    last = nc.tensor.transpose(ps[:, 1, q, :], wts[:, q, :], self.ident[:])
                last.then_inc(tr_done, 1)

    def experts(self):
        nc, sb, a = self.nc, self.sb, self.a
        with ExitStack() as ctx:
            PIECES = 6
            BUFS = 3
            SLOTS = 6
            raw = [sb(ctx, f"e_raw{q}", [P, 2 * 2 * FF]) for q in range(SLOTS)]
            wh = [sb(ctx, f"e_hi{j}", [P, KT, 2, FF], F32R) for j in range(BUFS)]
            wl = [sb(ctx, f"e_lo{j}", [P, KT, 2, FF], F32R) for j in range(BUFS)]
            dh = [sb(ctx, f"ed_hi{j}", [P, 2, D], F32R) for j in range(BUFS)]
            dl = [sb(ctx, f"ed_lo{j}", [P, 2, D], F32R) for j in range(BUFS)]
            xg = sb(ctx, "x_gather", [P, D])
            xh = sb(ctx, "xg_hi", [P, KT, P], F32R)
            xl = sb(ctx, "xg_lo", [P, KT, P], F32R)
            sg = sb(ctx, "gate_act", [P, 2, P])
            hid = sb(ctx, "hidden", [P, 2, P])
            hh = sb(ctx, "hid_hi", [P, 2, P], F32R)
            hl = sb(ctx, "hid_lo", [P, 2, P], F32R)
            yb = sb(ctx, "y_block", [P, D])
            idx_g, idx_1, idx_2, idx_s = (sb(ctx, n, [P, 1], U32) for n in ("idx_gather", "idx_1", "idx_2", "idx_scatter"))
            gu = [ctx.enter_context(nc.psum_tensor(f"gu_ps{h}", [P, 2, P], F32)) for h in range(2)]
            xt = ctx.enter_context(nc.psum_tensor("xg_ps", [P, 2, 4, P], F32))
            ht = [ctx.enter_context(nc.psum_tensor(f"ht_ps{h}", [P, P], F32)) for h in range(2)]
            yp = ctx.enter_context(nc.psum_tensor("y_ps", [P, 2, HALF], F32))
            w_in = [self.sems(ctx, f"e_in{q}_gate", f"e_in{q}_up") for q in range(SLOTS)]
            d_in = self.sems(ctx, *(f"e_in{q}_down" for q in range(SLOTS)))
            (hi_s, lo_s, xg_in, t_done, xh_s, xl_s, gu_done, sg_s, hid_s, ht_done, hh_s, hl_s, y_done, y_ready,
             idx_c, idx_t, scat, init) = self.sems(
                ctx, "e_hi_s", "e_lo_s", "xg_in", "xg_tr", "xg_hi_s", "xg_lo_s", "gu_done", "sg_s",
                "hid_s", "ht_done", "hh_s", "hl_s", "yb_done", "yb_ready", "idx_moved", "idx_s_s", "y_scat", "e_init")
            block = ctx.enter_context(nc.Block())
            fl = lambda x: x.rearrange("p a b -> p (a b)")

            def piece(j, i):
                q = (j * PIECES + i) % SLOTS
                if i < 4:
                    s = slice(2 * i, 2 * i + 2)
                    return q, raw[q][:].rearrange("p (k w f) -> p k w f", k=2, w=2), wh[j][:, s], wl[j][:, s]
                return q, raw[q][:], dh[j][:, i - 4], dl[j][:, i - 4]

            def plan(eng, e):
                row = self.plan[0:1, bass.ds(e, 1), :]
                nb = eng.value_load(row[:, :, 0:1].rearrange("p a b -> p (a b)"), min_val=1, max_val=NT)
                base = eng.value_load(row[:, :, 1:2].rearrange("p a b -> p (a b)"), min_val=0, max_val=E * NT)
                return nb, base

            def all_experts(eng, expert):
                with eng.Fori(0, E // BUFS - 1) as e3:
                    for j in range(BUFS):
                        expert(e3 * BUFS + j, j, e3, True)
                for e in range(E // BUFS * BUFS - BUFS, E):
                    expert(e, e % BUFS, e // BUFS, e + 2 < E)

            def loads_before(j, i, nth):
                q, down = (j * PIECES + i) % SLOTS, i >= 4
                same = [(jj, ii) for jj in range(BUFS) for ii in range(PIECES)
                        if (jj * PIECES + ii) % SLOTS == q and (ii >= 4) == down]
                return (nth * len(same) + same.index((j, i)) + 1) * 16

            @block.sync
            def _(sp):
                def load(e, j):
                    for i in range(PIECES):
                        q, r, _, _ = piece(j, i)
                        if not isinstance(e, int) or e * PIECES + i >= SLOTS:
                            sp.wait_ge(lo_s, e * PIECES + (i + 1 - SLOTS))
                        if i < 4:
                            for n, w in enumerate((a["w_gate_e"], a["w_up_e"])):
                                sp.dma_start(r[:, :, n, :],
                                             w[0, bass.ds(e, 1)].rearrange("o (p k) f -> p (o k) f", k=KT)
                                             [:, 2 * i:2 * i + 2, :]).then_inc(w_in[q][n], 16)
                        else:
                            sp.dma_start(r, a["w_down_e"][0, bass.ds(e, 1)].rearrange("o (c p) n -> p (o c) n", p=P)
                                         [:, i - 4, :]).then_inc(d_in[q], 16)

                for j in range(BUFS):
                    load(j, j)
                with sp.Fori(1, E // BUFS) as e3:
                    for j in range(BUFS):
                        load(e3 * BUFS + j, j)
                for e in range(E // BUFS * BUFS, E):
                    load(e, e % BUFS)

            @block.gpsimd
            def _(pool):
                g = nc.gpsimd
                g.memset(yb[:], 0.0).then_inc(init, 1)
                g.iota(idx_g[:], pattern=[[0, 1]], base=S, channel_multiplier=1).then_inc(init, 1)
                pool.wait_ge(init, 2)

                def gather():
                    alone(pool, self.passed)
                    pool.indirect_dma_start(xg[:], None, self.x1_d, bass.IndirectOffsetOnAxis(idx_g[:, 0:1], 0)
                                            ).then_inc(xg_in, 16)

                def scatter():
                    alone(pool, self.passed)
                    pool.indirect_dma_start(self.y_d, bass.IndirectOffsetOnAxis(idx_s[:, 0:1], 0), yb[:], None,
                                            compute_op=ALU.add).then_inc(scat, 16)

                def row_numbers(n, column):
                    pool.wait_ge(xg_in, n * 16 + 16)
                    alone(pool, self.passed)
                    g.tensor_copy(idx_2[:], idx_1[:]).then_inc(idx_c, 1)
                    pool.wait_ge(idx_c, n * 3 + 1)
                    alone(pool, self.passed)
                    g.tensor_copy(idx_1[:], idx_g[:]).then_inc(idx_c, 1)
                    if column is not None:
                        pool.wait_ge(idx_c, n * 3 + 2)
                        alone(pool, self.passed)
                        g.tensor_copy(idx_g[:], column).then_inc(idx_c, 1)
                    else:
                        pool.sem_inc(idx_c, 1)
                    pool.wait_ge(idx_c, n * 3 + 3)

                def add(n):
                    pool.wait_ge(scat, n * 16 + 16)
                    alone(pool, self.passed)
                    g.tensor_copy(idx_s[:], idx_2[:]).then_inc(idx_t, 1)
                    pool.wait_ge(idx_t, n + 1)
                    pool.wait_ge(y_ready, n + 1)
                    scatter()

                pool.sem_inc(t_done, 1)
                pool.sem_inc(y_ready, 2)
                for n, dst in enumerate((idx_s, idx_1)):
                    g.tensor_copy(dst[:], idx_g[:]).then_inc(init, 1)
                pool.wait_ge(init, 4)
                gather()
                scatter()
                with pool.Fori(0, E) as e:
                    nb, base = plan(pool, e)
                    with pool.Fori(0, nb) as b:
                        n = base + b
                        row_numbers(n, self.tok_tab[:, bass.ds(e * NT + b, 1)])
                        pool.wait_ge(t_done, n * 2 + 1)
                        gather()
                        add(n)
                total = pool.value_load(self.plan[0:1, E - 1, 1:2], min_val=0, max_val=E * NT) + \
                    pool.value_load(self.plan[0:1, E - 1, 0:1], min_val=1, max_val=NT)
                row_numbers(total, None)
                pool.wait_ge(t_done, total * 2 + 1)
                gather()
                add(total)
                pool.wait_ge(xg_in, total * 16 + 32)
                row_numbers(total + 1, None)
                add(total + 1)
                pool.wait_ge(scat, total * 16 + 48)

            @block.tensor
            def _(pe):
                def transposes(gb, half):
                    if half == 0:
                        pe.wait_ge(xg_in, gb * 16 + 32)
                    xv = xg[:].rearrange("p (c k) -> p k c", k=KT)
                    for k in range(4 * half, 4 * half + 4):
                        last = nc.tensor.transpose(xt[:, k // 4, k % 4, :], xv[:, k, :], self.ident[:])
                    last.then_inc(t_done, 1)

                def gate_up(j, h, ks, last_k):
                    out = gu[h][:]
                    for k in ks:
                        last = split3(nc, out, xh[:, k, :], xl[:, k, :], wh[j][:, k, :, h * P:(h + 1) * P],
                                      wl[j][:, k, :, h * P:(h + 1) * P], k == 0, k == KT - 1)
                    if last_k:
                        last.then_inc(gu_done, 1)

                def hid_t(gb, h):
                    pe.wait_ge(hid_s, gb * 2 + h + 1)
                    nc.tensor.transpose(ht[h][:], hid[:, h, :], self.ident[:]).then_inc(ht_done, 1)

                def down(j, h, hf):
                    return split3(nc, yp[:, hf, :], hh[:, h, :], hl[:, h, :], dh[j][:, h, hf * HALF:(hf + 1) * HALF],
                                  dl[j][:, h, hf * HALF:(hf + 1) * HALF], h == 0, h == 1)

                def blk(e, j, gb, first):
                    def products(h, kh):
                        if h == 0:
                            pe.wait_ge(xl_s, gb * 2 + kh + 1)
                            if first:
                                pe.wait_ge(lo_s, e * PIECES + 2 * kh + 2)
                        gate_up(j, h, range(4 * kh, 4 * kh + 4), kh == 1)

                    products(0, 0)
                    products(0, 1)
                    products(1, 0)
                    transposes(gb + 1, 0)
                    hid_t(gb, 0)
                    products(1, 1)
                    pe.wait_ge(hl_s, gb * 2 + 1)
                    if first:
                        pe.wait_ge(lo_s, e * PIECES + PIECES)
                    pe.wait_ge(y_ready, gb + 2)
                    down(j, 0, 0)
                    down(j, 0, 1)
                    hid_t(gb, 1)
                    transposes(gb + 1, 1)
                    pe.wait_ge(hl_s, gb * 2 + 2)
                    down(j, 1, 0)
                    down(j, 1, 1).then_inc(y_done, 1)

                def expert(e, j, nth, more):
                    nb, base = plan(pe, e)
                    blk(e, j, base, True)
                    with pe.If(nb > 1):
                        with pe.Fori(1, nb) as b:
                            blk(e, j, base + b, False)

                transposes(0, 0)
                transposes(0, 1)
                all_experts(pe, expert)

            @block.scalar
            def _(act):
                A = nc.scalar.activation

                def hi(j, nth, i):
                    q, r, h, _ = piece(j, i)
                    for sem in w_in[q] if i < 4 else (d_in[q],):
                        act.wait_ge(sem, loads_before(j, i, nth))
                    A(h, r, ACT.Copy).then_inc(hi_s, 1)

                def x_hi(b):
                    A(xh[:, 4 * b:4 * b + 4, :], xt[:, b], ACT.Copy).then_inc(xh_s, 1)

                def blk(e, b, gb, split):
                    act.wait_ge(gu_done, gb * 2 + 1)
                    A(sg[:, 0, :], gu[0][:, 0, :], ACT.Silu).then_inc(sg_s, 1)
                    split(0, 1)
                    act.wait_ge(ht_done, gb * 2 + 1)
                    A(hh[:, 0, :], ht[0][:], ACT.Copy).then_inc(hh_s, 1)
                    split(2)
                    act.wait_ge(gu_done, gb * 2 + 2)
                    A(sg[:, 1, :], gu[1][:, 0, :], ACT.Silu).then_inc(sg_s, 1)
                    act.wait_ge(t_done, gb * 2 + 4)
                    x_hi(0)
                    act.wait_ge(ht_done, gb * 2 + 2)
                    A(hh[:, 1, :], ht[1][:], ACT.Copy).then_inc(hh_s, 1)
                    act.wait_ge(t_done, gb * 2 + 5)
                    x_hi(1)
                    split(3)
                    act.wait_ge(y_done, gb + 1)
                    act.wait_ge(scat, gb * 16 + 48)
                    A(yb[:], fl(yp[:]), ACT.Copy, scale=self.wt_tab[:, bass.ds(e * NT + b, 1)]).then_inc(y_ready, 1)
                    split(4, 5)

                def expert(e, j, nth, more):
                    nb, base = plan(act, e)

                    def split(*pieces):
                        for i in pieces if more else ():
                            hi((j + 2) % BUFS, nth + (j + 2) // BUFS, i)

                    blk(e, 0, base, split)
                    with act.If(nb > 1):
                        with act.Fori(1, nb) as b:
                            blk(e, b, base + b, lambda *pieces: None)

                for i in range(PIECES):
                    hi(0, 0, i)
                act.wait_ge(init, 2)
                act.wait_ge(t_done, 3)
                x_hi(0)
                x_hi(1)
                for i in range(PIECES):
                    hi(1, 0, i)
                all_experts(act, expert)

            @block.vector
            def _(dve):
                v = nc.vector
                tt = v.tensor_tensor

                def lo(e, j, i):
                    _, r, h, l = piece(j, i)
                    dve.wait_ge(hi_s, e * PIECES + i + 1)
                    tt(l, r, h.bitcast(F32), ALU.subtract).then_inc(lo_s, 1)

                def x_lo(gb, b):
                    dve.wait_ge(xh_s, gb * 2 + b + 1)
                    s = slice(4 * b, 4 * b + 4)
                    tt(xl[:, s, :], xt[:, b], xh[:, s, :].bitcast(F32), ALU.subtract).then_inc(xl_s, 1)

                def hidden(gb, h):
                    dve.wait_ge(sg_s, gb * 2 + h + 1)
                    tt(hid[:, h, :], sg[:, h, :], gu[h][:, 1, :], ALU.mult).then_inc(hid_s, 1)

                def hidden_lo(gb, h):
                    dve.wait_ge(hh_s, gb * 2 + h + 1)
                    tt(hl[:, h, :], ht[h][:], hh[:, h, :].bitcast(F32), ALU.subtract).then_inc(hl_s, 1)

                def blk(gb, split):
                    hidden(gb, 0)
                    split(0, 1)
                    hidden_lo(gb, 0)
                    hidden(gb, 1)
                    x_lo(gb + 1, 0)
                    hidden_lo(gb, 1)
                    x_lo(gb + 1, 1)
                    split(2, 3, 4, 5)

                def expert(e, j, nth, more):
                    nb, base = plan(dve, e)

                    def split(*pieces):
                        for i in pieces if more else ():
                            lo(e + 2, (j + 2) % BUFS, i)

                    blk(base, split)
                    with dve.If(nb > 1):
                        with dve.Fori(1, nb) as b:
                            blk(base + b, lambda *pieces: None)

                for i in range(PIECES):
                    lo(0, 0, i)
                x_lo(0, 0)
                x_lo(0, 1)
                for i in range(PIECES):
                    lo(1, 1, i)
                all_experts(dve, expert)

    def final_norm(self):
        nc, sb, a = self.nc, self.sb, self.a
        with ExitStack() as ctx:
            y = [sb(ctx, f"y2_{i}", [P, D]) for i in range(NT)]
            g_b = sb(ctx, "ln2_g_b", [P, D])
            b_b = sb(ctx, "ln2_b_b", [P, D])
            stats = [sb(ctx, f"ln2_stats{i}", [P, 2, 6]) for i in range(NT)]
            mv = [sb(ctx, f"ln2_mv{i}", [P, 2]) for i in range(NT)]
            rs = [sb(ctx, f"ln2_rs{i}", [P, 1]) for i in range(NT)]
            y_in = [self.sems(ctx, f"y2_in{i}") for i in range(NT)]
            par_in, st, sq, rc, nrm, fin, out = self.sems(ctx, "ln2_par", "ln2_st", "ln2_sq", "ln2_rc", "ln2_nrm",
                                                          "ln2_fin", "ln2_out")
            block = ctx.enter_context(nc.Block())

            @block.sync
            def _(sp):
                for i in range(NT):
                    sp.dma_start(y[i][:], self.y_d[i * P:(i + 1) * P, :]).then_inc(y_in[i], 16)
                    if i == 0:
                        sp.dma_start(g_b[:], a["ln2_g"][0, :].partition_broadcast(P)).then_inc(par_in, 16)
                        sp.dma_start(b_b[:], a["ln2_b"][0, :].partition_broadcast(P)).then_inc(par_in, 16)
                for i in range(NT):
                    sp.wait_ge(fin, i + 1)
                    sp.dma_start(a["out"][0, i * P:(i + 1) * P, :], y[i][:]).then_inc(out, 16)
                sp.wait_ge(out, NT * 16)

            @block.scalar
            def _(act):
                for i in range(NT):
                    act.wait_ge(st, i * 3 + 3)
                    nc.scalar.activation(rs[i][:], mv[i][:, 1:2], ACT.Sqrt, bias=self.eps[:]).then_inc(sq, 1)

            @block.vector
            def _(dve):
                v = nc.vector
                for i in range(NT + 1):
                    if i < NT:
                        dve.wait_ge(y_in[i], 16)
                        self.norm_stats(dve, y[i], stats[i], mv[i], st, i * 3)
                    if i >= 1:
                        n = i - 1
                        dve.wait_ge(sq, n + 1)
                        v.reciprocal(rs[n][:], rs[n][:]).then_inc(rc, 1)
                        dve.wait_ge(rc, n + 1)
                        dve.wait_ge(st, n * 3 + 3)
                        v.tensor_scalar(y[n][:], y[n][:], mv[n][:, 0:1], rs[n][:], ALU.subtract, ALU.mult).then_inc(nrm, 1)
                        dve.wait_ge(par_in, 32)
                        dve.wait_ge(nrm, 2 * n + 1)
                        v.tensor_tensor(y[n][:], y[n][:], g_b[:], ALU.mult).then_inc(nrm, 1)

            @block.gpsimd
            def _(pool):
                for n in range(NT):
                    pool.wait_ge(nrm, 2 * n + 2)
                    nc.gpsimd.tensor_tensor(y[n][:], y[n][:], b_b[:], ALU.add).then_inc(fin, 1)


_INS = ["x", "w_in", "conv_qkv", "a_log", "dt_bias", "o_norm_g", "w_oa", "dw_w", "dw_b", "cln_g", "cln_b",
        "w_ob", "w_o", "ln1_g", "ln1_b", "w_router", "router_bias", "w_gate_e", "w_up_e", "w_down_e",
        "w_sh_gate", "w_sh_up", "w_sh_down", "ln2_g", "ln2_b"]


def decoder_layer(nc, *aps, upto=99):
    a = dict(zip(_INS + ["out"], aps))
    ctx = ExitStack()
    with ctx:
        k = Kernel(nc, a)
        k.ctx = ctx
        k.constants()
        with ExitStack() as xctx:
            k.x_hi = k.sb(xctx, "x_hi", [P, KT, S], F32R)
            k.x_lo = k.sb(xctx, "x_lo", [P, KT, S], F32R)
            k.load_x()
            k.end_stage()

            if upto >= 3:
                k.delta_net()
                k.end_stage()
            if upto == 2 or upto >= 4:
                with ExitStack() as uctx:
                    k.uc = k.sb(uctx, "uc", [P, KT, S])
                    k.conformer_conv(k.uc)
                    k.end_stage()
                    if upto >= 4:
                        k.branches(k.uc)
                        k.end_stage()
        if upto < 5:
            return
        k.plan = k.sb(ctx, "plan", [1, E, 2], I32)
        with ExitStack() as tctx:
            with ExitStack() as xctx:
                k.x1_hi = k.sb(xctx, "x1_hi", [P, KT, S], F32R)
                k.x1_lo = k.sb(xctx, "x1_lo", [P, KT, S], F32R)
                k.mix_norm()
                k.end_stage()
                if upto < 6:
                    return
                k.shared_and_route()
                k.end_stage()
            if upto < 7:
                return
            k.tok_tab = k.sb(tctx, "tok_tab", [P, E * NT], U32)
            k.wt_tab = k.sb(tctx, "wt_tab", [P, E * NT])
            k.block_tables()
            k.end_stage()
            if upto < 8:
                return
            k.experts()
            k.end_stage()
        k.final_norm()


def kernel(**inputs):
    import numpy as np
    import concourse.bacc as bacc
    from concourse.bass_utils import run_bass_kernel_spmd

    nc = bacc.Bacc("TRN2", target_bir_lowering=False, num_devices=1)
    arrays, args = {}, []
    for name in _INS:
        arr = np.ascontiguousarray(inputs[name])
        arrays[f"in_{name}_dram"] = arr
        args.append(nc.dram_tensor(f"in_{name}_dram", arr.shape, mybir.dt.from_np(arr.dtype),
                                   kind="ExternalInput").ap())
    args.append(nc.dram_tensor("out_0_dram", (1, S, D), F32, kind="ExternalOutput").ap())
    decoder_layer(nc, *args)
    r = run_bass_kernel_spmd(nc, [arrays], core_ids=[0])
    return r.results[0]["out_0_dram"]
```

```python
from contextlib import ExitStack

import concourse.bass as bass
from concourse import mybir

F32 = mybir.dt.float32
F32R = mybir.dt.float32r
I32 = mybir.dt.int32
U32 = mybir.dt.uint32
ALU = mybir.AluOpType
ACT = mybir.ActivationFunctionType
AX = mybir.AxisListType

P = 128
S = 1024
D = 1024
KT = D // P
NT = S // P
HALF = 512
H = 8
GH = 2
NG = H // GH
NPAIR = NT // 2
TAPS_S, TAPS_L = 4, 31
E = 64
FF = 256
NGRP = 8
TOPK = 8
EPS = 1e-6
ALPHA = 2.0 ** 0.25
ROUTED_SCALE = 2.5
NEG = -1.0e30
BIG = 3.0e38
LEVELS = 7
NROW = S + P
COL_QKVZ, COL_AB, COL_GLU, COL_GA = 0, 4 * D, 4 * D + 2 * H, 6 * D + 2 * H
COL_GB = COL_GA + D
R_DW, R_DWB, R_CG, R_CB, R_SC = 0, 31, 32, 33, 34
N_PAR = R_SC + 3 * TAPS_S


def split3(nc, out, w_hi, w_lo, x_hi, x_lo, first, last):
    nc.tensor.matmul(out, w_hi, x_hi, start=first, stop=False)
    nc.tensor.matmul(out, w_hi, x_lo, start=False, stop=False)
    return nc.tensor.matmul(out, w_lo, x_hi, start=False, stop=last)


def alone(eng, passed):
    eng.sem_inc(passed, 1)


class Kernel:
    def __init__(self, nc, a):
        self.nc, self.a = nc, a
        self.stage_sems = []

    def sems(self, ctx, *names):
        out = [self.nc.alloc_semaphore(n) for n in names]
        self.stage_sems += out
        return out[0] if len(out) == 1 else out

    def end_stage(self):
        self.nc.all_engine_barrier()
        self.nc.clear_and_free_semaphores(self.stage_sems)
        self.nc.all_engine_barrier()
        self.stage_sems = []

    def sb(self, ctx, name, shape, dt=F32):
        return ctx.enter_context(self.nc.sbuf_tensor(name, shape, dt))

    def ring(self, ctx, tag):
        r = {}
        r["raw"] = [self.sb(ctx, f"{tag}_raw{j}", [P, KT, P]) for j in range(2)]
        r["hi"] = [self.sb(ctx, f"{tag}_hi{j}", [P, KT, P], F32R) for j in range(2)]
        r["lo"] = [self.sb(ctx, f"{tag}_lo{j}", [P, KT, P], F32R) for j in range(2)]
        r["loaded"] = [self.sems(ctx, f"{tag}_loaded{j}") for j in range(2)]
        r["raw_free"], r["hi_ready"], r["w_ready"], r["w_free"] = self.sems(
            ctx, f"{tag}_raw_free", f"{tag}_hi_ready", f"{tag}_w_ready", f"{tag}_w_free")
        return r

    def ring_load(self, sp, r, n2, j, src):
        sp.wait_ge(r["raw_free"], n2 * 2 + j + 1)
        sp.dma_start(r["raw"][j][:], src).then_inc(r["loaded"][j], 16)

    def ring_hi(self, act, r, n2, j):
        act.wait_ge(r["loaded"][j], n2 * 16 + 16)
        act.wait_ge(r["w_free"], n2 * 2 + j + 1)
        self.nc.scalar.activation(r["hi"][j][:], r["raw"][j][:], ACT.Copy).then_inc(r["hi_ready"], 1)

    def ring_lo(self, dve, r, n2, j):
        dve.wait_ge(r["hi_ready"], n2 * 2 + j + 1)
        self.nc.vector.tensor_tensor(r["lo"][j][:], r["raw"][j][:], r["hi"][j][:].bitcast(F32),
                                     ALU.subtract).then_inc(r["w_ready"], 1)
        dve.wait_ge(r["w_ready"], n2 * 2 + j + 1)
        dve.sem_inc(r["raw_free"], 1)

    def constants(self):
        nc, ctx, a = self.nc, self.ctx, self.a
        self.passed = nc.alloc_semaphore("passed")
        sb = self.sb
        self.ident = sb(ctx, "ident", [P, P])
        self.ones = sb(ctx, "ones", [P, P])
        self.eps = sb(ctx, "eps", [P, 1])
        self.last_row = sb(ctx, "last_row", [P, P])
        self.tri_excl = sb(ctx, "tri_excl", [P, P])
        self.neg_mask = sb(ctx, "neg_mask", [P, P])
        self.lvl_mask = sb(ctx, "lvl_mask", [P, LEVELS, P])
        self.par = sb(ctx, "par", [P, KT, N_PAR])
        self.ong = sb(ctx, "ong", [P, 1])
        self.gcol_neg = sb(ctx, "gcol_neg", [P, NT, H])
        self.bcol = sb(ctx, "bcol", [P, NT, H])
        self.nbecol = sb(ctx, "nbecol", [P, NT, H])
        self.kdcol = sb(ctx, "kdcol", [P, NT, H])
        self.gc_d = nc.dram_tensor("gc_rows", (H, S), F32, kind="Internal").ap()
        self.be_d = nc.dram_tensor("beta_rows", (H, S), F32, kind="Internal").ap()
        self.o_d = nc.dram_tensor("o_rows", (D, S), F32, kind="Internal").ap()
        self.h_d = nc.dram_tensor("h_rows", (D, S), F32, kind="Internal").ap()
        self.x1_d = nc.dram_tensor("x1_table", (NROW, D), F32, kind="Internal").ap()
        self.y_d = nc.dram_tensor("y_acc", (NROW, D), F32, kind="Internal").ap()
        self.credit_d = nc.dram_tensor("credit", (2, P, 1), F32, kind="Internal").ap()
        self.u_d = nc.dram_tensor("glu_rows", (D, TAPS_L - 1 + S), F32, kind="Internal").ap()
        self.uc_d = nc.dram_tensor("conv_rows", (D, S), F32, kind="Internal").ap()
        self.slot_d = nc.dram_tensor("slot_pairs", (E * S, 2), F32, kind="Internal").ap()

    def load_x(self):
        nc, a = self.nc, self.a
        with ExitStack() as ctx:
            sb = self.sb
            xtok = sb(ctx, "xtok", [P, NT, D])
            rows = sb(ctx, "par_rows", [N_PAR, D])
            junk = sb(ctx, "fill", [P, HALF, 2])
            wab = sb(ctx, "wab", [P, KT, P])
            wab_hi = sb(ctx, "wab_hi", [P, KT, P], F32R)
            wab_lo = sb(ctx, "wab_lo", [P, KT, P], F32R)
            dtb = sb(ctx, "dtb", [H, 1])
            alog = sb(ctx, "alog", [H, 1])
            b_sig = sb(ctx, "b_sig", [2 * H, S])
            ab_raw = sb(ctx, "ab_raw", [2 * H, S])
            t0, t1, t2 = (sb(ctx, f"g_tmp{i}", [H, S]) for i in range(3))
            gate = sb(ctx, "scan_gate", [H, S])
            gc = sb(ctx, "gc", [H, S])
            gb = sb(ctx, "glast_b", [P, NT * H])
            ecol = sb(ctx, "ecol", [P, NT * H])
            nexpa = sb(ctx, "nexpa", [H, 1])
            brow = sb(ctx, "beta_rows_sb", [H, S])
            x_in = [self.sems(ctx, f"x_in{i}") for i in range(NT)]
            (par_in, wab_in, small_in, c_ready, xt_done, hi_done, lo_done, par_done, par_used,
             ab_hi, ab_lo, ab_done, fill_ready, out_done, dv, av, cols_done, beta_moved, gcol_done, gl_done) = self.sems(
                ctx, "par_in", "wab_in", "small_in", "const_ready", "xt_done", "x_hi_done", "x_lo_done",
                "par_done", "par_used", "ab_hi", "ab_lo", "ab_done", "fill_ready", "out_done", "dve_self",
                "act_self", "cols_done", "beta_moved", "gcol_done", "gl_done")
            tp = ctx.enter_context(nc.psum_tensor("x_ps", [P, 8, 4, P], F32))
            block = ctx.enter_context(nc.Block())

            @block.sync
            def _(sp):
                for i in range(NT):
                    sp.dma_start(xtok[:, i, :], a["x"][0, i * P:(i + 1) * P, :]).then_inc(x_in[i], 16)
                sp.dma_start(rows[R_DW:R_DWB, :], a["dw_w"][0]).then_inc(par_in, 16)
                sp.dma_start(rows[R_DWB:R_DWB + 1, :], a["dw_b"]).then_inc(par_in, 16)
                sp.dma_start(rows[R_CG:R_CG + 1, :], a["cln_g"]).then_inc(par_in, 16)
                sp.dma_start(rows[R_CB:R_CB + 1, :], a["cln_b"]).then_inc(par_in, 16)
                sp.dma_start(rows[R_SC:N_PAR, :],
                             a["conv_qkv"][0].rearrange("t (k c) -> (t k) c", c=D)).then_inc(par_in, 16)
                sp.dma_start(wab[:], a["w_in"][0, :, COL_AB:COL_AB + P].rearrange("(k p) n -> p k n", p=P)
                             ).then_inc(wab_in, 16)
                sp.dma_start(self.ong[:], a["o_norm_g"].rearrange("a n -> n a")).then_inc(small_in, 16)
                sp.dma_start(dtb[:], a["dt_bias"].rearrange("a n -> n a")).then_inc(small_in, 16)
                sp.dma_start(alog[:], a["a_log"].rearrange("a n -> n a")).then_inc(small_in, 16)
                sp.wait_ge(fill_ready, 2)
                sp.dma_start(self.slot_d.rearrange("(p n) o -> p (n o)", p=P),
                             junk[:].rearrange("p n o -> p (n o)")).then_inc(out_done, 16)
                sp.wait_ge(av, 1)
                sp.dma_start(brow[:], b_sig[H:2 * H, :]).then_inc(beta_moved, 16)
                sp.dma_start(self.be_d, b_sig[H:2 * H, :]).then_inc(out_done, 16)
                sp.wait_ge(dv, 7)
                sp.dma_start(self.gc_d, gc[:]).then_inc(out_done, 16)
                sp.wait_ge(out_done, 48)

            @block.gpsimd
            def _(pool):
                g = nc.gpsimd
                chain = [0]

                def link(ins):
                    chain[0] += 1
                    ins.then_inc(c_ready, 1)
                    pool.wait_ge(c_ready, chain[0])

                link(g.memset(self.ones[:], 1.0))
                link(g.memset(self.eps[:], EPS))
                link(g.memset(self.ident[:], 0.0))
                link(g.affine_select(out=self.ident[:], in_=self.ident[:], compare_op=ALU.not_equal, fill=1.0,
                                     base=0, pattern=[[-1, P]], channel_multiplier=1))
                link(g.memset(junk[:], 0.0))
                g.iota(junk[:, :, 0:1].rearrange("p (n c) o -> p n (c o)", c=P), pattern=[[0, HALF // P], [1, P]],
                       base=S, channel_multiplier=0, allow_small_or_imprecise_dtypes=True).then_inc(fill_ready, 2)
                link(g.memset(self.last_row[:], 1.0))
                link(g.affine_select(out=self.last_row[:], in_=self.last_row[:], compare_op=ALU.is_ge, fill=0.0,
                                     base=-(P - 1), pattern=[[0, P]], channel_multiplier=1))
                link(g.memset(self.tri_excl[:], 1.0))
                link(g.affine_select(out=self.tri_excl[:], in_=self.tri_excl[:], compare_op=ALU.is_gt, fill=0.0,
                                     base=0, pattern=[[1, P]], channel_multiplier=-1))
                link(g.memset(self.neg_mask[:], 0.0))
                link(g.affine_select(out=self.neg_mask[:], in_=self.neg_mask[:], compare_op=ALU.is_ge, fill=NEG,
                                     base=0, pattern=[[1, P]], channel_multiplier=-1))
                for l in range(LEVELS):
                    b = 1 << l
                    m = self.lvl_mask[:, l, :].rearrange("p (m r) -> p m r", r=2 * b)
                    link(g.memset(self.lvl_mask[:, l, :], 1.0))
                    link(g.affine_select(out=m, in_=m, compare_op=ALU.is_ge, fill=0.0, base=0,
                                         pattern=[[-2 * b, P // (2 * b)], [0, 2 * b]], channel_multiplier=1))
                    link(g.affine_select(out=m, in_=m, compare_op=ALU.is_ge, fill=0.0, base=b - 1,
                                         pattern=[[2 * b, P // (2 * b)], [0, 2 * b]], channel_multiplier=-1))
                    link(g.affine_select(out=m, in_=m, compare_op=ALU.is_ge, fill=0.0, base=-b,
                                         pattern=[[0, P // (2 * b)], [1, 2 * b]], channel_multiplier=0))

            @block.tensor
            def _(pe):
                pe.wait_ge(c_ready, 4)
                for i in range(NT):
                    pe.wait_ge(x_in[i], 16)
                    if i >= 4:
                        pe.wait_ge(lo_done, i - 3)
                    for k in range(KT):
                        last = nc.tensor.transpose(tp[:, 2 * (i % 4) + k // 4, k % 4, :],
                                                   xtok[:, i, k * P:(k + 1) * P], self.ident[:])
                    last.then_inc(xt_done, 1)
                pe.wait_ge(par_in, 80)
                pe.wait_ge(lo_done, NT - 3)
                for k in range(KT):
                    last = nc.tensor.transpose(tp[:, k // 4, k % 4, 0:N_PAR], rows[:, k * P:(k + 1) * P],
                                               self.ident[0:N_PAR, 0:N_PAR])
                last.then_inc(par_done, 1)
                pe.wait_ge(ab_lo, 1)
                pe.wait_ge(lo_done, NT)
                for hf in range(2):
                    out = tp[:, 2 + hf, :, :].rearrange("p a b -> p (a b)")
                    for k in range(KT):
                        last = split3(nc, out, wab_hi[:, k, :], wab_lo[:, k, :],
                                      self.x_hi[:, k, hf * HALF:(hf + 1) * HALF],
                                      self.x_lo[:, k, hf * HALF:(hf + 1) * HALF], k == 0, k == KT - 1)
                last.then_inc(ab_done, 1)
                pe.wait_ge(dv, 7)
                pe.wait_ge(beta_moved, 16)
                for t in range(NT):
                    nc.tensor.transpose(tp[:, 4, 0, t * H:(t + 1) * H], gc[:, t * P:(t + 1) * P],
                                        self.ident[0:H, 0:H])
                    last = nc.tensor.transpose(tp[:, 5, 0, t * H:(t + 1) * H], brow[:, t * P:(t + 1) * P],
                                               self.ident[0:H, 0:H])
                last.then_inc(cols_done, 1)
                pe.wait_ge(gcol_done, 1)
                pe.wait_ge(c_ready, 7)
                nc.tensor.matmul(tp[:, 6, 0, 0:NT * H], self.last_row[:],
                                 self.gcol_neg[:].rearrange("p t h -> p (t h)"), start=True, stop=True
                                 ).then_inc(gl_done, 1)

            @block.scalar
            def _(act):
                for i in range(NT):
                    act.wait_ge(xt_done, i + 1)
                    nc.scalar.activation(self.x_hi[:, :, i * P:(i + 1) * P].rearrange("p (b k) t -> p b k t", b=2),
                                         tp[:, 2 * (i % 4):2 * (i % 4) + 2, :, :], ACT.Copy).then_inc(hi_done, 1)
                act.wait_ge(wab_in, 16)
                nc.scalar.activation(wab_hi[:], wab[:], ACT.Copy).then_inc(ab_hi, 1)
                act.wait_ge(ab_done, 1)
                ab_ps = tp[0:2 * H, 2:4, :, :].rearrange("p a b c -> p (a b c)")
                nc.scalar.activation(b_sig[:], ab_ps, ACT.Sigmoid).then_inc(av, 1)
                act.wait_ge(dv, 2)
                nc.scalar.activation(t1[:], t1[:], ACT.Exp, scale=-1.0).then_inc(av, 1)
                nc.scalar.activation(nexpa[:], alog[:], ACT.Exp).then_inc(av, 1)
                act.wait_ge(av, 3)
                nc.scalar.activation(t1[:], t1[:], ACT.Ln, bias=1.0).then_inc(av, 1)
                act.wait_ge(gcol_done, 1)
                nc.scalar.activation(ecol[:], self.gcol_neg[:].rearrange("p t h -> p (t h)"), ACT.Exp,
                                     scale=-1.0).then_inc(av, 1)
                act.wait_ge(dv, 9)
                nc.scalar.activation(self.kdcol[:].rearrange("p t h -> p (t h)"), gb[:], ACT.Exp).then_inc(av, 1)

            @block.vector
            def _(dve):
                v = nc.vector
                for i in range(NT):
                    dve.wait_ge(hi_done, i + 1)
                    sl = self.x_lo[:, :, i * P:(i + 1) * P].rearrange("p (b k) t -> p b k t", b=2)
                    hi = self.x_hi[:, :, i * P:(i + 1) * P].rearrange("p (b k) t -> p b k t", b=2).bitcast(F32)
                    for b in range(2):
                        last = v.tensor_tensor(sl[:, b], tp[:, 2 * (i % 4) + b, :, :], hi[:, b], ALU.subtract)
                    last.then_inc(lo_done, 1)
                dve.wait_ge(ab_hi, 1)
                v.tensor_tensor(wab_lo[:], wab[:], wab_hi[:].bitcast(F32), ALU.subtract).then_inc(ab_lo, 1)
                dve.wait_ge(par_done, 1)
                for b in range(2):
                    last = v.tensor_copy(self.par[:, 4 * b:4 * b + 4, :], tp[:, b, :, 0:N_PAR])
                last.then_inc(par_used, 1)
                v.memset(gate[:], 1.0).then_inc(par_used, 1)
                dve.wait_ge(par_used, 2)
                v.memset(gate[:].rearrange("p (t c) -> p t c", c=P)[:, :, 0:1], 0.0).then_inc(par_used, 1)
                dve.wait_ge(av, 1)
                dve.wait_ge(small_in, 48)
                a_ps = tp[0:H, 2:4, :, :].rearrange("p a b c -> p (a b c)")
                v.tensor_scalar(t0[:], a_ps, dtb[:], None, ALU.add).then_inc(dv, 1)
                dve.wait_ge(dv, 1)
                v.scalar_tensor_tensor(out=t1[:], in0=t0[:], scalar=-1.0, in1=t0[:], op0=ALU.mult, op1=ALU.max).then_inc(dv, 1)
                v.tensor_scalar(t2[:], t0[:], 0.0, None, ALU.max).then_inc(dv, 1)
                dve.wait_ge(av, 4)
                dve.wait_ge(dv, 3)
                v.tensor_tensor(t0[:], t1[:], t2[:], ALU.add).then_inc(dv, 1)
                v.tensor_scalar(nexpa[:], nexpa[:], -1.0, None, ALU.mult).then_inc(dv, 1)
                dve.wait_ge(dv, 5)
                v.tensor_scalar(t2[:], t0[:], nexpa[:], None, ALU.mult).then_inc(dv, 1)
                dve.wait_ge(dv, 6)
                dve.wait_ge(par_used, 3)
                v.tensor_tensor_scan(gc[:], gate[:], t2[:], 0.0, ALU.mult, ALU.add).then_inc(dv, 1)
                dve.wait_ge(cols_done, 1)
                v.tensor_copy(self.bcol[:].rearrange("p t h -> p (t h)"), tp[:, 5, 0, 0:NT * H]).then_inc(dv, 1)
                v.tensor_scalar(self.gcol_neg[:].rearrange("p t h -> p (t h)"), tp[:, 4, 0, 0:NT * H], -1.0, None,
                                ALU.mult).then_inc(gcol_done, 1)
                dve.wait_ge(gl_done, 1)
                dve.wait_ge(gcol_done, 1)
                v.tensor_tensor(gb[:], self.gcol_neg[:].rearrange("p t h -> p (t h)"), tp[:, 6, 0, 0:NT * H],
                                ALU.subtract).then_inc(dv, 1)
                dve.wait_ge(av, 5)
                dve.wait_ge(dv, 8)
                v.scalar_tensor_tensor(out=self.nbecol[:].rearrange("p t h -> p (t h)"), in0=ecol[:], scalar=-1.0,
                                       in1=self.bcol[:].rearrange("p t h -> p (t h)"), op0=ALU.mult,
                                       op1=ALU.mult)


    def project(self, r, out, j, x_hi, x_lo, steps=range(KT), halves=(0, 1)):
        for k in steps:
            for hf in halves:
                last = split3(self.nc, out[:, hf, :], r["hi"][j][:, k, :], r["lo"][j][:, k, :],
                              x_hi[:, k, hf * HALF:(hf + 1) * HALF], x_lo[:, k, hf * HALF:(hf + 1) * HALF],
                              k == 0, k == KT - 1)
        return last

    def w_in_tile(self, col):
        return self.a["w_in"][0, :, bass.ds(col, P)].rearrange("(k p) n -> p k n", p=P)

    def glu(self):
        nc = self.nc
        PAD = TAPS_L - 1
        with ExitStack() as ctx:
            r = self.ring(ctx, "glu")
            u = [self.sb(ctx, f"u{b}", [P, PAD + S]) for b in range(2)]
            sg = self.sb(ctx, "glu_sig", [P, S])
            pj = [ctx.enter_context(nc.psum_tensor(f"glu_ps{j}", [P, 2, HALF], F32)) for j in range(2)]
            pj_done, pj_free, a_moved, b_sig, u_done, u_free, stored = self.sems(
                ctx, "glu_pj_done", "glu_pj_free", "glu_a_moved", "glu_b_sig", "glu_u_done", "glu_u_free", "glu_stored")
            block = ctx.enter_context(nc.Block())

            @block.sync
            def _(sp):
                sp.sem_inc(r["raw_free"], 2)
                with sp.Fori(0, KT) as c:
                    for j in range(2):
                        self.ring_load(sp, r, c, j, self.w_in_tile(c * P + COL_GLU + j * D))

            @block.tensor
            def _(pe):
                pe.sem_inc(r["w_free"], 2)
                pe.sem_inc(pj_free, 2)
                with pe.Fori(0, KT) as c:
                    for j in range(2):
                        pe.wait_ge(r["w_ready"], c * 2 + j + 1)
                        pe.wait_ge(pj_free, c * 2 + j + 1)
                        self.project(r, pj[j], j, self.x_hi, self.x_lo).then_inc(pj_done, 1)
                        pe.wait_ge(pj_done, c * 2 + j + 1)
                        pe.sem_inc(r["w_free"], 1)

            @block.scalar
            def _(act):
                for b in range(2):
                    nc.scalar.activation(u[b][:, 0:PAD], self.ones[:, 0:PAD], ACT.Copy, scale=0.0)

                def tile_pair(c2, b, more):
                    c = c2 * 2 + b
                    act.wait_ge(pj_done, c * 2 + 1)
                    act.wait_ge(u_free, c + 1)
                    nc.scalar.activation(u[b][:, PAD:PAD + S], pj[0][:].rearrange("p a b -> p (a b)"),
                                         ACT.Copy).then_inc(a_moved, 1)
                    act.wait_ge(a_moved, c + 1)
                    act.sem_inc(pj_free, 1)
                    if more:
                        self.ring_hi(act, r, c + 1, 0)
                    act.wait_ge(pj_done, c * 2 + 2)
                    act.wait_ge(u_done, c + 1)
                    nc.scalar.activation(sg[:], pj[1][:].rearrange("p a b -> p (a b)"),
                                         ACT.Sigmoid).then_inc(b_sig, 1)
                    act.wait_ge(b_sig, c + 1)
                    act.sem_inc(pj_free, 1)
                    if more:
                        self.ring_hi(act, r, c + 1, 1)

                for j in range(2):
                    self.ring_hi(act, r, 0, j)
                with act.Fori(0, KT // 2 - 1) as c2:
                    for b in range(2):
                        tile_pair(c2, b, True)
                tile_pair(KT // 2 - 1, 0, True)
                tile_pair(KT // 2 - 1, 1, False)

            @block.vector
            def _(dve):
                v = nc.vector
                dve.sem_inc(u_done, 1)

                def tile_pair(c2, b, more):
                    c = c2 * 2 + b
                    if more:
                        self.ring_lo(dve, r, c + 1, 0)
                    dve.wait_ge(a_moved, c + 1)
                    dve.wait_ge(b_sig, c + 1)
                    v.tensor_tensor(u[b][:, PAD:PAD + S], u[b][:, PAD:PAD + S], sg[:], ALU.mult).then_inc(u_done, 1)
                    if more:
                        self.ring_lo(dve, r, c + 1, 1)

                for j in range(2):
                    self.ring_lo(dve, r, 0, j)
                with dve.Fori(0, KT // 2 - 1) as c2:
                    for b in range(2):
                        tile_pair(c2, b, True)
                tile_pair(KT // 2 - 1, 0, True)
                tile_pair(KT // 2 - 1, 1, False)

            @block.gpsimd
            def _(pool):
                pool.sem_inc(u_free, 2)
                with pool.Fori(0, KT // 2) as c2:
                    for b in range(2):
                        c = c2 * 2 + b
                        pool.wait_ge(u_done, c + 2)
                        alone(pool, self.passed)
                        pool.dma_start(self.u_d[bass.ds(c * P, P), :], u[b][:]).then_inc(stored, 16)
                        pool.wait_ge(stored, c * 16 + 16)
                        pool.sem_inc(u_free, 1)

    def delta_net(self):
        nc, sb, a = self.nc, self.sb, self.a
        PAD = TAPS_S - 1
        with ExitStack() as ctx:
            u_in = sb(ctx, "u_in", [P, TAPS_L - 1 + HALF])
            uc = sb(ctx, "uc_half", [P, HALF])
            r = self.ring(ctx, "dn")
            rp = [sb(ctx, f"pre_conv{j}", [P, PAD + S]) for j in range(2)]
            sq = [sb(ctx, f"norm_sq{j}", [P, S]) for j in range(2)]
            zt = sq
            nxt = sb(ctx, "qkv_next", [P, 3, GH, S])
            cur = sb(ctx, "qkv_cur", [P, 3, GH, S])
            gcb = sb(ctx, "gc_bc", [P, GH, 2 * P])
            beb = sb(ctx, "beta_bc", [P, GH, 2 * P])
            zs = sb(ctx, "z_pair", [P, GH, 2 * P])
            egc, qd, kb = (sb(ctx, n, [P, GH, 2 * P]) for n in ("exp_gc", "q_decayed", "k_beta"))
            ld, at, qk = (sb(ctx, n, [P, 4, P]) for n in ("decay", "a_t", "qk_t"))
            dt = ld
            NA = 3
            atl = [sb(ctx, f"a_lvl{l}", [P, 4, P]) for l in range(NA)]
            xt, xx, yy = (sb(ctx, n, [P, 4, P]) for n in ("inv_t", "inv", "y_sb"))
            kbe, kd, vb = (sb(ctx, n, [P, 4, P]) for n in ("k_beta_e", "k_dec", "v_beta"))
            wt = xx
            st = sb(ctx, "state", [P, GH, P])
            ob, osq = (sb(ctx, n, [P, 4 * P]) for n in ("o_pair", "o_sq"))
            orn = osq
            vn = osq[:, 0:GH * P].rearrange("p (h t) -> p h t", h=GH)
            z_d = nc.dram_tensor("z_rows", (D, S), F32, kind="Internal").ap()
            pj = [ctx.enter_context(nc.psum_tensor(f"dn_pj{j}", [P, 2, HALF], F32)) for j in range(2)]
            ga, gb, gc, gd = (ctx.enter_context(nc.psum_tensor(f"dn_{n}", [P, 4, P], F32)) for n in "abcd")
            pj_done, pj_moved, conv_sem, silu_done, sq_done, ns_done, rn_done, n_scaled, z_ready, z_stored, cur_ready = \
                self.sems(ctx, "dn_pj_done", "dn_pj_moved", "dn_conv", "dn_silu", "dn_sq", "dn_ns_done", "dn_rn",
                          "dn_scaled", "dn_z_ready", "dn_z_stored", "dn_cur_ready")
            (slices_in, z_in, egc_done, kb_ready, qk_done, ld_ready, dt_done, at_ready, masked, kvt_done, kv_read,
             xt_t, xt_evac, x_upd, y_done, y_evac, z_done, w_done, w_evac, vn_done, vn_evac, o_done, o_read,
             ds_done, s_upd, osq_done, ss_done, orn_done, o_fin, o_stored, ld_sub, act_ln, zero_s) = self.sems(
                ctx, "slices_in", "zs_in", "egc_done", "kb_ready", "qk_done", "ld_ready", "dt_done", "at_ready",
                "masked", "kvt_done", "kv_read", "xt_t", "xt_evac", "x_upd", "y_done", "y_evac", "z_done",
                "w_done", "w_evac", "vn_done", "vn_evac", "o_done", "o_read", "ds_done", "s_upd", "osq_done",
                "ss_done", "orn_done", "o_fin", "o_stored", "ld_sub", "act_ln", "zero_s")
            u_loaded, taps_done, uc_stored = self.sems(ctx, "u_loaded", "taps_done", "uc_stored")
            rn_exp, self.qk_sem, self.o_self = self.sems(ctx, "rn_exp", "qk_ready", "o_self")
            block = ctx.enter_context(nc.Block())
            Q, K, V = range(3)
            KIND = (3, 0, 1, 2)
            CONV_TILE = 1 + 2 * TAPS_S
            FLAT = "p a b -> p (a b)"

            def after(eng, sem, value):
                if not isinstance(value, int) or value > 0:
                    eng.wait_ge(sem, value)

            def all_pairs(eng, solve):
                for p in range(NPAIR):
                    solve(0, p, True, p > 0)
                with eng.Fori(1, NG - 1) as g:
                    for p in range(NPAIR):
                        solve(g, p, True, True)
                for p in range(NPAIR):
                    solve(NG - 1, p, False, True)

            def tok(p, cc):
                return slice((2 * p + cc) * P, (2 * p + cc + 1) * P)

            def conv_no(G, p, j):
                return G * 6 + 2 * (p - 1) + j

            @block.sync
            def _(sp):
                def tile(G, p, j):
                    after(sp, r["w_ready"], G * 8 + 2 * p + j - 1)
                    sp.dma_start(r["raw"][j][:], self.w_in_tile(KIND[p] * D + G * GH * P + j * P)
                                 ).then_inc(r["loaded"][j], 16)

                def slices(g, p):
                    q = g * 4 + p
                    sp.wait_ge(kb_ready, 1 + q)
                    sp.wait_ge(egc_done, 1 + q)
                    sp.wait_ge(ld_ready, 1 + q)
                    for dst, src in ((gcb, self.gc_d), (beb, self.be_d)):
                        sp.dma_start(dst[:], src[bass.ds(g * GH, GH), 2 * p * P:2 * (p + 1) * P]
                                     .partition_broadcast(P)).then_inc(slices_in, 16)

                def z_slice(g, p):
                    q = g * 4 + p
                    sp.wait_ge(o_fin, 1 + q)
                    sp.wait_ge(z_stored, g * 32 + 32)
                    sp.dma_start(zs[:], z_d[bass.ds(g * GH * P, GH * P), 2 * p * P:2 * (p + 1) * P]
                                 .rearrange("(h p) t -> p h t", p=P)).then_inc(z_in, 16)

                def u_half(g, p):
                    sp.wait_ge(taps_done, 1 + (g * 4 + p) * TAPS_L)
                    sp.dma_start(u_in[:], self.u_d[bass.ds(g * 2 * P + p // 2 * P, P),
                                                   p % 2 * HALF:p % 2 * HALF + TAPS_L - 1 + HALF]).then_inc(u_loaded, 16)

                def solve(g, p, more, prev):
                    slices(g, p)
                    u_half(g, p)
                    if more:
                        for j in range(2):
                            if p < NPAIR - 1:
                                tile(g + 1, p + 1, j)
                            else:
                                tile(g + 2, 0, j)
                    z_slice(g, p)

                for sem in (kb_ready, taps_done, egc_done, ld_ready, o_fin, act_ln, o_read, s_upd, kvt_done, o_done, masked, self.qk_sem):
                    sp.sem_inc(sem, 1)
                for p in range(NPAIR):
                    for j in range(2):
                        tile(0, p, j)
                for j in range(2):
                    tile(1, 0, j)
                all_pairs(sp, solve)

            @block.tensor
            def _(pe):
                mm, tr = nc.tensor.matmul, nc.tensor.transpose

                def fill(G, p, s):
                    j, k = s // KT, s % KT
                    n = G * 8 + 2 * p + j
                    if k == 0:
                        pe.wait_ge(r["w_ready"], n + 1)
                        after(pe, pj_moved, n - 1)
                    last = self.project(r, pj[j], j, self.x_hi, self.x_lo, steps=(k,))
                    if k == KT - 1:
                        last.then_inc(pj_done, 1)

                def norm_sum(G, p, m):
                    pe.wait_ge(sq_done, G * 4 + 2 * (p - 1) + m // 2 + 1)
                    after(pe, rn_done, G * 8 + 4 * (p - 1) + m)
                    mm(gd[:].rearrange(FLAT), self.ones[:],
                       sq[m // 2][:, (m % 2) * HALF:(m % 2 + 1) * HALF], start=True, stop=True
                       ).then_inc(ns_done, 1)

                def solve(g, p, more, prev):
                    q = g * 4 + p
                    G = g + 1

                    steps = iter(range(2 * KT))

                    def f(n=1):
                        for _ in range(n if more else 0):
                            fill(G, p, next(steps))

                    def square_sum(q, bank):
                        pe.wait_ge(osq_done, q + 1)
                        mm(bank[:].rearrange(FLAT), self.ones[:], osq[:], start=True, stop=True).then_inc(ss_done, 1)

                    units = [(hh, cc) for hh in range(GH) for cc in range(2)]
                    if p == 0:
                        pe.wait_ge(cur_ready, g * 2 + 2)
                    pe.wait_ge(kb_ready, 1 + q + 1)
                    for u, (hh, cc) in enumerate(units):
                        mm(ga[:, u, :], cur[:, K, hh, tok(p, cc)], kb[:, hh, cc * P:(cc + 1) * P], start=True, stop=True)
                    for u, (hh, cc) in enumerate(units):
                        last = mm(gb[:, u, :], cur[:, K, hh, tok(p, cc)], cur[:, Q, hh, tok(p, cc)], start=True, stop=True)
                    last.then_inc(qk_done, 1)
                    f()
                    pe.wait_ge(o_read, 1 + q)
                    pe.wait_ge(s_upd, 1 + 2 * q)
                    for u, (hh, cc) in enumerate(units):
                        tr(gc[:, u, :], cur[:, K, hh, tok(p, cc)], self.ident[:])
                    if p == 0:
                        pe.wait_ge(silu_done, g * 6 + 6)
                    for u, (hh, cc) in enumerate(units):
                        last = tr(gd[:, u, :], cur[:, V, hh, tok(p, cc)], self.ident[:])
                    last.then_inc(kvt_done, 1)
                    f(2)
                    pe.wait_ge(kv_read, q + 1)
                    if prev:
                        square_sum(q - 1, gd)
                    pe.wait_ge(x_upd, q * 7 + 1)
                    for u in range(4):
                        last = tr(gc[:, u, :], xt[:, u, :], self.ident[:])
                    last.then_inc(xt_t, 1)
                    f()
                    for l in range(1, LEVELS):
                        if l == 1:
                            pe.wait_ge(xt_evac, q * 6 + 1)
                            pe.wait_ge(masked, 1 + q * 7 + 2)
                        else:
                            pe.wait_ge(x_upd, q * 7 + l)
                            pe.wait_ge(masked, 1 + q * 7 + l + 1)
                            for u in range(4):
                                last = tr(gc[:, u, :], xx[:, u, :], self.ident[:])
                            last.then_inc(xt_t, 1)
                        for u in range(4):
                            last = mm(ga[:, u, :], atl[l % NA][:, u, :], xx[:, u, :], start=True, stop=True)
                        last.then_inc(y_done, 1)
                        f()
                        if more and p in (2, 3) and l <= 4:
                            if l == 1:
                                pe.wait_ge(act_ln, 1 + q)
                            norm_sum(G, p - 1, l - 1)
                        pe.wait_ge(y_evac, q * 6 + l)
                        pe.wait_ge(xt_evac, q * 6 + l)
                        for u in range(4):
                            if l < LEVELS - 1:
                                last = mm(gb[:, u, :], xt[:, u, :], yy[:, u, :], start=True, stop=True)
                            else:
                                last = mm(gb[:, u, :], yy[:, u, :], xt[:, u, :], start=True, stop=True)
                        last.then_inc(z_done, 1)
                        if l <= 5:
                            f()
                    pe.wait_ge(x_upd, q * 7 + 7)
                    for u in range(4):
                        last = mm(ga[:, u, :], kbe[:, u, :], xt[:, u, :], start=True, stop=True)
                    last.then_inc(w_done, 1)
                    f()
                    pe.wait_ge(w_evac, q + 1)
                    if prev:
                        pe.wait_ge(act_ln, 1 + q)
                    for cc in range(2):
                        s = q * 2 + cc
                        pe.wait_ge(s_upd, 1 + s)
                        if p == 0 and cc == 0:
                            pe.wait_ge(zero_s, g + 1)
                        for hh in range(GH):
                            u = 2 * hh + cc
                            mm(gb[:, u, :], xt[:, u, :], vb[:, u, :], start=True, stop=False)
                            last = mm(gb[:, u, :], wt[:, u, :], st[:, hh, :], start=False, stop=True)
                        last.then_inc(vn_done, 1)
                        pe.wait_ge(vn_evac, s + 1)
                        for hh in range(GH):
                            u = 2 * hh + cc
                            last = mm(gd[:, u, :], kd[:, u, :], vn[:, hh, :], start=True, stop=True)
                        for hh in range(GH):
                            u = 2 * hh + cc
                            mm(gc[:, u, :], st[:, hh, :], qd[:, hh, cc * P:(cc + 1) * P], start=True, stop=False)
                            last = mm(gc[:, u, :], vn[:, hh, :], qk[:, u, :], start=False, stop=True)
                        last.then_inc(o_done, 1)
                    if p == NPAIR - 1 and not more:
                        square_sum(q, ga)

                for p in range(NPAIR):
                    for s in range(2 * KT):
                        fill(0, p, s)
                    if p >= 2:
                        for m in range(4):
                            norm_sum(0, p - 1, m)
                all_pairs(pe, solve)

            @block.scalar
            def _(act):
                A = nc.scalar.activation

                def hi(n2, j, wait_used=None):
                    act.wait_ge(r["loaded"][j], n2 * 16 + 16)
                    if wait_used is not None:
                        act.wait_ge(pj_done, wait_used)
                    A(r["hi"][j][:], r["raw"][j][:], ACT.Copy).then_inc(r["hi_ready"], 1)

                def tile_move(G, p, j):
                    n = G * 8 + 2 * p + j
                    act.wait_ge(pj_done, n + 1)
                    ps = pj[j][:].rearrange(FLAT)
                    if p == 0:
                        after(act, n_scaled, G * 8)
                        A(zt[j][:], ps, ACT.Silu).then_inc(pj_moved, 1)
                    else:
                        after(act, conv_sem, conv_no(G, p, j) * (2 * TAPS_S) - 2 * TAPS_S)
                        A(rp[j][:, PAD:PAD + S], ps, ACT.Copy).then_inc(pj_moved, 1)
                    hi(G * 4 + p + 1, j, n + 1)

                def tile_silu(G, p, j):
                    if p == 0:
                        return
                    c = conv_no(G, p, j)
                    act.wait_ge(conv_sem, (c + 1) * 2 * TAPS_S)
                    if p == 3:
                        act.wait_ge(kvt_done, 1 + G * 4)
                    dst = cur if p == 3 else nxt
                    A(dst[:, KIND[p], j, :], nxt[:, KIND[p], j, :], ACT.Silu).then_inc(silu_done, 1)
                    if p < 3:
                        act.wait_ge(silu_done, c + 1)
                        if p == 1:
                            act.wait_ge(z_stored, G * 32 + 32)
                        else:
                            act.wait_ge(n_scaled, G * 8 + 2 * j + 2)
                        A(sq[j][:], nxt[:, KIND[p], j, :], ACT.Square).then_inc(sq_done, 1)

                def norm(G, p, m):
                    i = G * 8 + 4 * (p - 1) + m
                    act.wait_ge(ns_done, i + 1)
                    A(sq[m // 2][:, m % 2 * HALF:(m % 2 + 1) * HALF], gd[:].rearrange(FLAT), ACT.Ln, bias=self.eps[:]
                      ).then_inc(rn_done, 1)

                def norm_exp(G, p):
                    act.wait_ge(rn_done, G * 8 + 4 * p)
                    for j in range(2):
                        A(sq[j][:], sq[j][:], ACT.Exp, scale=-0.5).then_inc(rn_exp, 1)

                def squares(q):
                    act.wait_ge(o_read, 1 + q + 1)
                    act.wait_ge(o_fin, 1 + q)
                    A(osq[:], ob[:], ACT.Square).then_inc(osq_done, 1)

                def inverse_root(q, bank):
                    act.wait_ge(ss_done, q + 1)
                    A(orn[:], bank[:].rearrange(FLAT), ACT.Ln, scale=1.0 / P, bias=self.eps[:]).then_inc(act_ln, 1)
                    act.wait_ge(act_ln, 1 + q + 1)
                    A(orn[:], orn[:], ACT.Exp, scale=-0.5).then_inc(orn_done, 1)

                def cur_k(g):
                    act.wait_ge(n_scaled, g * 8 + 8)
                    act.wait_ge(kvt_done, 1 + g * 4)
                    A(cur[:, K], nxt[:, K], ACT.Copy).then_inc(cur_ready, 1)

                def solve(g, p, more, prev):
                    q = g * 4 + p
                    G = g + 1
                    act.wait_ge(slices_in, q * 32 + 32)
                    act.wait_ge(o_done, 1 + 2 * q)
                    act.wait_ge(s_upd, 1 + 2 * q)
                    A(egc[:].rearrange(FLAT), gcb[:].rearrange(FLAT), ACT.Exp).then_inc(egc_done, 1)
                    act.wait_ge(ld_ready, 1 + q + 1)
                    A(dt[:].rearrange(FLAT), ld[:].rearrange(FLAT), ACT.Exp).then_inc(dt_done, 1)
                    if prev:
                        if p == 0:
                            tile_silu(g, 3, 1)
                        squares(q - 1)
                        if more and p > 0:
                            tile_silu(G, p - 1, 0)
                            tile_move(G, p - 1, 1)
                    act.wait_ge(xt_t, q * 6 + 1)
                    A(xx[:].rearrange(FLAT), gc[:].rearrange(FLAT), ACT.Copy).then_inc(xt_evac, 1)
                    if prev:
                        inverse_root(q - 1, gd)
                    for l in range(1, LEVELS):
                        act.wait_ge(y_done, q * 6 + l)
                        A(yy[:].rearrange(FLAT), ga[:].rearrange(FLAT), ACT.Copy).then_inc(y_evac, 1)
                        if l > 1:
                            A(xt[:].rearrange(FLAT), gc[:].rearrange(FLAT), ACT.Copy).then_inc(xt_evac, 1)
                        if more and l == 2 and p > 0:
                            tile_silu(G, p - 1, 1)
                        if more and p in (2, 3) and l <= 4:
                            norm(G, p - 1, l - 1)
                            if l == 4:
                                norm_exp(G, p - 1)
                        if more and l == 4:
                            tile_move(G, p, 0)
                        if more and l == 6 and p == 3:
                            cur_k(G)
                    act.wait_ge(w_done, q + 1)
                    A(wt[:].rearrange(FLAT), ga[:].rearrange(FLAT), ACT.Copy).then_inc(w_evac, 1)
                    if more and p == 3:
                        tile_move(G, p, 1)
                    for cc in range(2):
                        act.wait_ge(vn_done, q * 2 + cc + 1)
                        A(vn, gb[:].rearrange("p (h c) t -> p h c t", c=2)[:, :, cc, :], ACT.Copy).then_inc(vn_evac, 1)
                        if more and p == 3 and cc == 0:
                            tile_silu(G, p, 0)
                    if p == NPAIR - 1 and not more:
                        squares(q)
                        inverse_root(q, ga)

                for j in range(2):
                    A(rp[j][:, 0:PAD], self.ones[:, 0:PAD], ACT.Copy, scale=0.0)
                    hi(0, j)
                for p in range(NPAIR):
                    for j in range(2):
                        tile_move(0, p, j)
                    if p >= 2:
                        for m in range(4):
                            norm(0, p - 1, m)
                        norm_exp(0, p - 1)
                    for j in range(2):
                        tile_silu(0, p, j)
                cur_k(0)
                all_pairs(act, solve)

            @block.vector
            def _(dve):
                v = nc.vector
                tt, stt = v.tensor_tensor, v.scalar_tensor_tensor

                def lo(n, j):
                    dve.wait_ge(r["hi_ready"], n + 1)
                    tt(r["lo"][j][:], r["raw"][j][:], r["hi"][j][:].bitcast(F32), ALU.subtract).then_inc(r["w_ready"], 1)

                def conv(G, p, j, part=range(-1, TAPS_S)):
                    n = G * 8 + 2 * p + j
                    if -1 in part:
                        lo(n + 2, j)
                    if p == 0:
                        return
                    base = conv_no(G, p, j) * 2 * TAPS_S
                    if 0 in part:
                        dve.wait_ge(pj_moved, n + 1)
                        if p == 1 and j == 0:
                            after(dve, cur_ready, G * 2)
                        if p == 3:
                            after(dve, silu_done, G * 6)
                    for t in part:
                        if t < 0:
                            continue
                        w = self.par[:, bass.ds(G * GH + j, 1), R_SC + t * 3 + KIND[p]]
                        for hf in range(2):
                            acc = nxt[:, KIND[p], j, hf * HALF:(hf + 1) * HALF]
                            src = rp[j][:, hf * HALF + t:hf * HALF + t + HALF]
                            if t == 0:
                                ins = v.tensor_scalar(acc, src, w, None, ALU.mult)
                            else:
                                dve.wait_ge(conv_sem, base + 2 * t + hf - 1)
                                ins = stt(out=acc, in0=src, scalar=w, in1=acc, op0=ALU.mult, op1=ALU.add)
                            ins.then_inc(conv_sem, 1)

                def scale(G, p, m):
                    dve.wait_ge(rn_exp, G * 4 + 2 * (p - 1) + m // 2 + 1)
                    half = slice(m % 2 * HALF, (m % 2 + 1) * HALF)
                    sl = nxt[:, KIND[p], m // 2, half]
                    tt(sl, sl, sq[m // 2][:, half], ALU.mult).then_inc(n_scaled, 1)

                def k_beta(q, g, p):
                    dve.wait_ge(slices_in, q * 32 + 32)
                    if p == 0:
                        dve.wait_ge(cur_ready, g * 2 + 2)
                    after(dve, qk_done, q)
                    tt(kb[:], cur[:, K, :, 2 * p * P:2 * (p + 1) * P], beb[:], ALU.mult).then_inc(kb_ready, 1)

                def cur_q(g):
                    dve.wait_ge(n_scaled, g * 8 + 8)
                    dve.wait_ge(kvt_done, 1 + g * 4)
                    v.tensor_scalar(cur[:, Q], nxt[:, Q], float(P) ** -0.5, None, ALU.mult).then_inc(cur_ready, 1)

                def finish(q):
                    dve.wait_ge(orn_done, q + 1)
                    dve.wait_ge(z_in, q * 16 + 16)
                    stt(out=ob[:], in0=ob[:], scalar=self.ong[:], in1=orn[:], op0=ALU.mult, op1=ALU.mult).then_inc(self.o_self, 1)
                    dve.wait_ge(self.o_self, q + 1)
                    tt(ob[:], ob[:], zs[:].rearrange(FLAT), ALU.mult).then_inc(o_fin, 1)

                def solve(g, p, more, prev):
                    q = g * 4 + p
                    G = g + 1
                    tap_numbers = iter(range(TAPS_L))
                    if more:
                        tap_plan = ((7, 3, 6, 2, 1, 7), (7, 3, 6, 2, 1, 7), (8, 4, 7, 1, 0, 6), (8, 4, 7, 1, 0, 9))[p]
                    else:
                        tap_plan = (5, 4, 5, 5, 5, 2)

                    def taps(n):
                        for t in (next(tap_numbers) for _ in range(n)):
                            w = self.par[:, bass.ds(g * 2 + p // 2, 1), R_DW + t]
                            if t == 0:
                                dve.wait_ge(u_loaded, q * 16 + 16)
                                dve.wait_ge(uc_stored, q * 16 + 16)
                                ins = v.tensor_scalar(uc[:], u_in[:, 0:HALF], w,
                                                      self.par[:, bass.ds(g * 2 + p // 2, 1), R_DWB],
                                                      ALU.mult, ALU.add)
                            else:
                                dve.wait_ge(taps_done, 1 + q * TAPS_L + t)
                                ins = stt(out=uc[:], in0=u_in[:, t:t + HALF], scalar=w, in1=uc[:],
                                          op0=ALU.mult, op1=ALU.add)
                            ins.then_inc(taps_done, 1)

                    if p == 0:
                        dve.wait_ge(o_done, 1 + g * 8)
                        v.memset(st[:], 0.0).then_inc(zero_s, 1)
                    if not prev:
                        k_beta(q, g, p)
                    dve.wait_ge(egc_done, 1 + q + 1)
                    tt(qd[:], cur[:, Q, :, 2 * p * P:2 * (p + 1) * P], egc[:], ALU.mult)
                    taps(2)
                    dve.wait_ge(kvt_done, 1 + q + 1)
                    def col(x):
                        return x[:, 2 * p:2 * p + 2, bass.ds(g * GH, GH)].rearrange("p c h -> p h c")\
                            .unsqueeze(3).to_broadcast([P, GH, 2, P])
                    v4 = lambda x: x[:].rearrange("p (h c) t -> p h c t", c=2)
                    dve.wait_ge(o_done, 1 + 2 * q)
                    tt(v4(kbe), v4(gc), col(self.nbecol), ALU.mult)
                    tt(v4(kd), v4(gc), col(self.kdcol), ALU.mult)
                    tt(v4(vb), v4(gd), col(self.bcol), ALU.mult).then_inc(kv_read, 1)
                    dve.wait_ge(dt_done, q + 1)
                    dve.wait_ge(qk_done, q + 1)
                    dve.wait_ge(masked, 1 + q * 7)
                    tt(at[:], ga[:], dt[:], ALU.mult).then_inc(at_ready, 1)
                    tt(qk[:], gb[:], dt[:], ALU.mult).then_inc(self.qk_sem, 1)
                    dve.wait_ge(masked, 1 + q * 7 + 1)
                    tt(xt[:], self.ident[:].unsqueeze(1).to_broadcast([P, 4, P]), atl[0][:], ALU.subtract).then_inc(x_upd, 1)
                    if more and p > 0:
                        conv(G, p - 1, 1)
                    for l in range(1, LEVELS):
                        dve.wait_ge(z_done, q * 6 + l)
                        dst = xx if l < LEVELS - 1 else xt
                        if l > 1:
                            dve.wait_ge(x_upd, q * 7 + l)
                        tt(dst[:], dst[:], gb[:], ALU.subtract).then_inc(x_upd, 1)
                        if l == 2 and prev:
                            finish(q - 1)
                        if more and p in (2, 3) and l == 5:
                            for m in range(4):
                                scale(G, p - 1, m)
                        taps(tap_plan[l - 1])
                        if more and l == 4:
                            conv(G, p, 0, range(-1, 2))
                        if more and l == 5:
                            conv(G, p, 0, range(2, TAPS_S))
                        if l == 5 and p < NPAIR - 1:
                            k_beta(q + 1, g, p + 1)
                        if l == 6 and p == NPAIR - 1 and more:
                            cur_q(G)
                            k_beta(q + 1, G, 0)
                    for cc in range(2):
                        dve.wait_ge(o_done, 1 + q * 2 + cc + 1)
                        for hh in range(GH):
                            ins = stt(out=st[:, hh, :], in0=st[:, hh, :],
                                      scalar=egc[:, hh, (cc + 1) * P - 1:(cc + 1) * P], in1=gd[:, 2 * hh + cc, :],
                                      op0=ALU.mult, op1=ALU.add)
                        ins.then_inc(s_upd, 1)
                        if cc == 0 and more and p == 3:
                            conv(G, p, 1, range(-1, 2))
                        elif cc == 0:
                            taps(3)
                            dve.wait_ge(s_upd, 1 + q * 2 + 1)
                    dve.wait_ge(o_stored, 16 + q * 16)
                    v.tensor_copy(ob[:], gc[:].rearrange(FLAT)).then_inc(o_read, 1)
                    if more and p == 3:
                        conv(G, p, 1, range(2, TAPS_S))
                    if p == NPAIR - 1 and not more:
                        finish(q)

                for j in range(2):
                    lo(j, j)
                for p in range(NPAIR):
                    for j in range(2):
                        conv(0, p, j)
                    if p >= 2:
                        for m in range(4):
                            scale(0, p - 1, m)
                cur_q(0)
                all_pairs(dve, solve)

            @block.gpsimd
            def _(pool):
                tt = nc.gpsimd.tensor_tensor

                def z_store(G):
                    for j in range(2):
                        pool.wait_ge(pj_moved, G * 8 + j + 1)
                        alone(pool, self.passed)
                        pool.dma_start(z_d[bass.ds(G * GH * P + j * P, P), :], zt[j][:]).then_inc(z_stored, 16)

                def o_store(g, p):
                    pool.wait_ge(o_fin, 1 + g * 4 + p + 1)
                    alone(pool, self.passed)
                    pool.dma_start(self.o_d[bass.ds(g * GH * P, GH * P), 2 * p * P:2 * (p + 1) * P]
                                   .rearrange("(h p) t -> p h t", p=P),
                                   ob[:].rearrange("p (h t) -> p h t", h=GH)).then_inc(o_stored, 16)

                def solve(g, p, more, prev):
                    q = g * 4 + p
                    pool.wait_ge(slices_in, q * 32 + 32)
                    pool.wait_ge(self.qk_sem, 1 + q)
                    v4 = lambda x: x[:].rearrange("p (h c) t -> p h c t", c=2)
                    tt(v4(ld), gcb[:].rearrange("p h (c t) -> p h c t", c=2),
                       self.gcol_neg[:, 2 * p:2 * p + 2, bass.ds(g * GH, GH)].rearrange("p c h -> p h c")
                       .unsqueeze(3).to_broadcast([P, GH, 2, P]), ALU.add).then_inc(ld_sub, 1)
                    pool.wait_ge(ld_sub, q + 1)
                    tt(ld[:], ld[:], self.neg_mask[:].unsqueeze(1).to_broadcast([P, 4, P]), ALU.add).then_inc(ld_ready, 1)
                    if more and p == 1:
                        z_store(g + 1)
                    pool.wait_ge(at_ready, q + 1)
                    for l in range(LEVELS):
                        if l == NA:
                            pool.wait_ge(x_upd, q * 7 + 1)
                        elif l > NA:
                            pool.wait_ge(y_done, q * 6 + l - NA)
                        tt(atl[l % NA][:], at[:], self.lvl_mask[:, l, :].unsqueeze(1).to_broadcast([P, 4, P]),
                           ALU.mult).then_inc(masked, 1)
                    if prev:
                        o_store(*((g, p - 1) if p else (g - 1, NPAIR - 1)))
                    pool.wait_ge(taps_done, 1 + q * TAPS_L + TAPS_L)
                    alone(pool, self.passed)
                    pool.dma_start(self.uc_d[bass.ds(g * 2 * P + p // 2 * P, P), p % 2 * HALF:(p % 2 + 1) * HALF],
                                   uc[:]).then_inc(uc_stored, 16)
                    if p == NPAIR - 1 and not more:
                        o_store(g, p)

                pool.dma_start(self.credit_d[0], self.ong[:]).then_inc(o_stored, 16)
                pool.dma_start(self.credit_d[1], self.ong[:]).then_inc(uc_stored, 16)
                z_store(0)
                all_pairs(pool, solve)
                pool.wait_ge(o_stored, 16 + NG * NPAIR * 16)
                pool.wait_ge(uc_stored, 16 + NG * NPAIR * 16)


    def branches(self):
        nc, sb, a = self.nc, self.sb, self.a
        with ExitStack() as ctx:
            r = self.ring(ctx, "br")
            src_hi = [sb(ctx, f"br_src_hi{b}", [P, KT, HALF], F32R) for b in range(2)]
            src_lo = [sb(ctx, f"br_src_lo{b}", [P, KT, HALF], F32R) for b in range(2)]
            oh = [sb(ctx, f"o_in{i}", [P, HALF]) for i in range(2)]
            sg = [sb(ctx, f"br_sig{b}", [P, HALF]) for b in range(2)]
            ht = [sb(ctx, f"br_h{b}", [P, HALF]) for b in range(2)]
            rstd = sb(ctx, "cln_rstd", [P, HALF])
            ps = [ctx.enter_context(nc.psum_tensor(f"br_ps{i}", [P, HALF], F32)) for i in range(4)]
            st_m = [ctx.enter_context(nc.psum_tensor(f"cln_sum{t}", [P, HALF], F32)) for t in range(2)]
            st_v = [ctx.enter_context(nc.psum_tensor(f"cln_var{t}", [P, HALF], F32)) for t in range(2)]
            o_in = [self.sems(ctx, f"o_in_sem{i}") for i in range(2)]
            uc_in = [self.sems(ctx, f"uc_in{t}") for t in range(2)]
            uc = sb(ctx, "uc", [P, KT, S])
            (o_hi, o_lo, mean_done, centred, sqd, var_done, sqrt_done, rstd_done, normed, activated, u_hi, u_lo,
             mm_done, sig_done, ps_read, h_ready, h_stored) = self.sems(
                ctx, "o_hi", "o_lo", "mean_done", "centred", "cln_sq", "var_done", "cln_sqrt", "rstd_done",
                "normed", "activated", "u_hi", "u_lo", "br_mm", "br_sig_done", "br_read", "h_ready", "h_stored")
            self.cln_sq = sg
            block = ctx.enter_context(nc.Block())
            hs = [slice(t * HALF, (t + 1) * HALF) for t in range(2)]
            TILES = 4 * KT

            @block.sync
            def _(sp):
                def tile(t, c, br, j):
                    w = (a["w_oa"], a["w_ob"])[br][0, :, bass.ds(c * P, P)].rearrange("(k p) n -> p k n", p=P)
                    sp.dma_start(r["raw"][j][:], w if j == 0 else self.w_in_tile(c * P + (COL_GA, COL_GB)[br])
                                 ).then_inc(r["loaded"][j], 16)

                for t in range(2):
                    sp.dma_start(uc[:, :, hs[t]], self.uc_d[:, hs[t]].rearrange("(k p) t -> p k t", p=P)
                                 ).then_inc(uc_in[t], 16)
                for t in range(2):
                    for k in range(KT):
                        n = t * KT + k
                        if n >= 2:
                            sp.wait_ge(o_lo, n - 1)
                        sp.dma_start(oh[k % 2][:], self.o_d[k * P:(k + 1) * P, hs[t]]).then_inc(o_in[k % 2], 16)
                        if k == 1:
                            for j in range(2):
                                if t:
                                    sp.wait_ge(r["w_ready"], t * TILES + j - 1)
                                tile(t, 0, 0, j)
                    for j in range(2):
                        sp.wait_ge(r["w_ready"], t * TILES + j + 1)
                        tile(t, 0, 1, j)
                    with sp.Fori(1, KT) as c:
                        for br in range(2):
                            for j in range(2):
                                sp.wait_ge(r["w_ready"], c * 4 + t * TILES + 2 * br + j - 1)
                                tile(t, c, br, j)

            @block.tensor
            def _(pe):
                mm = nc.tensor.matmul
                for t in range(2):
                    pe.wait_ge(uc_in[t], 16)
                    for k in range(KT):
                        last = mm(st_m[t][:], self.ones[:], uc[:, k, hs[t]], start=k == 0, stop=k == KT - 1)
                    last.then_inc(mean_done, 1)
                for t in range(2):
                    for k in range(KT):
                        pe.wait_ge(sqd, t * KT + k + 1)
                        mm(st_v[t][:], self.ones[:], self.cln_sq[k % 2][:], start=k == 0, stop=k == KT - 1
                           ).then_inc(var_done, 1)
                for t in range(2):
                    pe.wait_ge(o_lo, (t + 1) * KT)
                    with pe.Fori(0, KT) as c:
                        for br in range(2):
                            for j in range(2):
                                n = c * 4 + t * TILES + 2 * br + j
                                pe.wait_ge(r["w_ready"], n + 1)
                                pe.wait_ge(ps_read, n - 3 + 4)
                                if br == 1 and j == 0:
                                    pe.wait_ge(u_lo, (t + 1) * KT)
                                xh, xl = (src_hi[br], src_lo[br]) if j == 0 else (self.x_hi, self.x_lo)
                                sl = slice(0, HALF) if j == 0 else hs[t]
                                for k in range(KT):
                                    last = split3(nc, ps[2 * br + j][:], r["hi"][j][:, k, :], r["lo"][j][:, k, :],
                                                  xh[:, k, sl], xl[:, k, sl], k == 0, k == KT - 1)
                                last.then_inc(mm_done, 1)

            @block.scalar
            def _(act):
                A = nc.scalar.activation

                def hi(n2, j, used):
                    act.wait_ge(r["loaded"][j], n2 * 16 + 16)
                    if used is not None:
                        act.wait_ge(mm_done, used)
                    A(r["hi"][j][:], r["raw"][j][:], ACT.Copy).then_inc(r["hi_ready"], 1)

                def o_split(t):
                    for k in range(KT):
                        n = t * KT + k
                        act.wait_ge(o_in[k % 2], (n // 2 + 1) * 16)
                        if t and k == 0:
                            act.wait_ge(mm_done, TILES)
                        A(src_hi[0][:, k, :], oh[k % 2][:], ACT.Copy).then_inc(o_hi, 1)

                def u_split(t):
                    for k in range(KT):
                        act.wait_ge(activated, t * KT + k + 1)
                        A(src_hi[1][:, k, :], uc[:, k, hs[t]], ACT.Copy).then_inc(u_hi, 1)

                def squares(t):
                    for k in range(KT):
                        n = t * KT + k
                        act.wait_ge(centred, n + 1)
                        if n >= 2:
                            act.wait_ge(var_done, n - 1)
                        A(self.cln_sq[k % 2][:], uc[:, k, hs[t]], ACT.Square).then_inc(sqd, 1)

                def activate(t):
                    act.wait_ge(var_done, (t + 1) * KT)
                    if t:
                        act.wait_ge(normed, KT)
                    A(rstd[:], st_v[t][:], ACT.Sqrt, scale=1.0 / D, bias=self.eps[:]).then_inc(sqrt_done, 1)
                    for k in range(KT):
                        act.wait_ge(normed, t * KT + k + 1)
                        A(uc[:, k, hs[t]], uc[:, k, hs[t]], ACT.Silu, scale=self.par[:, k, R_CG:R_CG + 1],
                          bias=self.par[:, k, R_CB:R_CB + 1]).then_inc(activated, 1)

                for t in range(2):
                    for j in range(2):
                        hi(16 * t, j, 32 * t + j - 1 if t else None)
                    if t == 0:
                        squares(0)
                        squares(1)
                        o_split(0)
                        activate(0)
                        u_split(0)
                        activate(1)
                    else:
                        o_split(1)
                        u_split(1)

                    def body(c, last_c):
                        for br in range(2):
                            for j in range(2):
                                n = c * 4 + t * TILES + 2 * br + j
                                act.wait_ge(mm_done, n + 1)
                                if j == 1:
                                    act.wait_ge(ps_read, c * 4 + t * TILES + 2 * br - 2 + 4)
                                    A(sg[br][:], ps[2 * br + 1][:], ACT.Sigmoid).then_inc(sig_done, 1)
                                if not (last_c and br):
                                    hi(c * 2 + 16 * t + br + 1, j, n + 1)

                    with act.Fori(0, KT - 1) as c:
                        body(c, False)
                    body(KT - 1, True)

            @block.vector
            def _(dve):
                v = nc.vector
                tt = v.tensor_tensor
                dve.sem_inc(ps_read, 4)

                def lo(n, j):
                    dve.wait_ge(r["hi_ready"], n + 1)
                    tt(r["lo"][j][:], r["raw"][j][:], r["hi"][j][:].bitcast(F32), ALU.subtract).then_inc(r["w_ready"], 1)

                def centre(t):
                    dve.wait_ge(mean_done, t + 1)
                    for k in range(KT):
                        v.scalar_tensor_tensor(out=uc[:, k, hs[t]], in0=st_m[t][:], scalar=-1.0 / D,
                                               in1=uc[:, k, hs[t]], op0=ALU.mult, op1=ALU.add).then_inc(centred, 1)

                def o_split(t):
                    for k in range(KT):
                        dve.wait_ge(o_hi, t * KT + k + 1)
                        tt(src_lo[0][:, k, :], oh[k % 2][:], src_hi[0][:, k, :].bitcast(F32), ALU.subtract
                           ).then_inc(o_lo, 1)

                def u_split(t):
                    for k in range(KT):
                        dve.wait_ge(u_hi, t * KT + k + 1)
                        tt(src_lo[1][:, k, :], uc[:, k, hs[t]], src_hi[1][:, k, :].bitcast(F32), ALU.subtract
                           ).then_inc(u_lo, 1)

                def normalize(t):
                    dve.wait_ge(sqrt_done, t + 1)
                    v.reciprocal(rstd[:], rstd[:]).then_inc(rstd_done, 1)
                    dve.wait_ge(rstd_done, t + 1)
                    dve.wait_ge(centred, (t + 1) * KT)
                    for k in range(KT):
                        tt(uc[:, k, hs[t]], uc[:, k, hs[t]], rstd[:], ALU.mult).then_inc(normed, 1)

                for t in range(2):
                    for j in range(2):
                        lo(TILES * t + j, j)
                    if t == 0:
                        centre(0)
                        centre(1)
                        o_split(0)
                        normalize(0)
                        u_split(0)
                        normalize(1)
                    else:
                        o_split(1)
                        u_split(1)

                    def body(c, last_c):
                        i = c + t * KT
                        for br in range(2):
                            for j in range(2):
                                if not (last_c and br):
                                    lo(c * 4 + t * TILES + 2 * br + j + 2, j)
                            dve.wait_ge(sig_done, i * 2 + br + 1)
                            if br == 0:
                                dve.wait_ge(h_stored, 16 + i * 16)
                            tt(ht[br][:], ps[2 * br][:], sg[br][:], ALU.mult).then_inc(ps_read, 2)
                        dve.wait_ge(ps_read, i * 4 + 8)
                        tt(ht[0][:], ht[0][:], ht[1][:], ALU.add).then_inc(h_ready, 1)

                    with dve.Fori(0, KT - 1) as c:
                        body(c, False)
                    body(KT - 1, True)

            @block.gpsimd
            def _(pool):
                pool.dma_start(self.credit_d[0], self.ong[:]).then_inc(h_stored, 16)
                for t in range(2):
                    with pool.Fori(0, KT) as c:
                        pool.wait_ge(h_ready, c + t * KT + 1)
                        pool.dma_start(self.h_d[bass.ds(c * P, P), hs[t]], ht[0][:]).then_inc(h_stored, 16)
                pool.wait_ge(h_stored, 16 + 2 * KT * 16)


    def norm_stats(self, dve, y, stats, mv, sem, base, met=None):
        v = self.nc.vector
        for hf in range(2):
            v.bn_stats(stats[:, hf, :], y[:, hf * HALF:(hf + 1) * HALF]).then_inc(sem, 1)
        dve.wait_ge(sem, base + 2)
        if met is not None:
            alone(dve, met)
        v.bn_aggr(mv[:], stats[:]).then_inc(sem, 1)

    def mix_norm(self):
        nc, sb, a = self.nc, self.sb, self.a
        with ExitStack() as ctx:
            wraw = [sb(ctx, f"wo_raw{j}", [P, 2, D]) for j in range(3)]
            wh = sb(ctx, "wo_hi", [P, KT, D], F32R)
            wl = sb(ctx, "wo_lo", [P, KT, D], F32R)
            hraw = [sb(ctx, f"h_raw{j}", [P, KT, P]) for j in range(2)]
            hh = [sb(ctx, f"h_hi{j}", [P, KT, P], F32R) for j in range(2)]
            hl = [sb(ctx, f"h_lo{j}", [P, KT, P], F32R) for j in range(2)]
            y = [sb(ctx, f"y1_{j}", [P, D]) for j in range(2)]
            g_b = sb(ctx, "ln1_g_b", [P, D])
            b_b = sb(ctx, "ln1_b_b", [P, D])
            stats = sb(ctx, "ln1_stats", [P, 2, 6])
            mv = sb(ctx, "ln1_mv", [P, 2])
            rs = sb(ctx, "ln1_rs", [P, 1])
            zero = sb(ctx, "zeros", [P, D])
            ps = [ctx.enter_context(nc.psum_tensor(f"mix_ps{j}", [P, 2, HALF], F32)) for j in range(2)]
            tp = [ctx.enter_context(nc.psum_tensor(f"x1t_ps{j}", [P, 2, 4, P], F32)) for j in range(2)]
            PARTS = KT // 2
            parts = [slice(i * KT // PARTS, (i + 1) * KT // PARTS) for i in range(PARTS)]
            w_in = [self.sems(ctx, f"wo_in{i}") for i in range(PARTS)]
            h_in = [self.sems(ctx, f"h_in{j}") for j in range(2)]
            xr_in = [self.sems(ctx, f"xres_in{j}") for j in range(2)]
            x1_out = [self.sems(ctx, f"x1_out{j}") for j in range(2)]
            (w_hi, w_lo, h_hi, h_lo, par_in, mm_done, res, st, sq, rstd, nrm, x1_ready, tr_done, th, tl, z_done, z_out) = \
                self.sems(ctx, "wo_hi_s", "wo_lo_s", "h_hi_s", "h_lo_s", "ln1_par", "mix_mm", "ln1_res", "ln1_st",
                          "ln1_sq", "ln1_rstd", "ln1_nrm", "x1_ready", "x1_tr", "x1_hi_s", "x1_lo_s",
                          "zero_done", "zero_out")
            block = ctx.enter_context(nc.Block())

            @block.sync
            def _(sp):
                def h_tile(i, j):
                    sp.dma_start(hraw[j][:], self.h_d[:, bass.ds(i * P, P)].rearrange("(k p) t -> p k t", p=P)
                                 ).then_inc(h_in[j], 16)

                def x_tile(i, j):
                    sp.dma_start(y[j][:], a["x"][0, bass.ds(i * P, P), :]).then_inc(xr_in[j], 16)

                w_o = a["w_o"][0].rearrange("(k p) n -> p k n", p=P)
                h_tile(0, 0)
                for i, ks in enumerate(parts):
                    if i == 3:
                        h_tile(1, 1)
                        for j in range(2):
                            x_tile(j, j)
                        sp.wait_ge(w_lo, 1)
                    sp.dma_start(wraw[i % 3][:], w_o[:, ks, :]).then_inc(w_in[i], 16)
                sp.dma_start(g_b[:], a["ln1_g"][0, :].partition_broadcast(P)).then_inc(par_in, 16)
                sp.dma_start(b_b[:], a["ln1_b"][0, :].partition_broadcast(P)).then_inc(par_in, 16)
                with sp.Fori(1, NT // 2) as i2:
                    for j in range(2):
                        sp.wait_ge(h_lo, i2 * 2 + j - 1)
                        h_tile(i2 * 2 + j, j)
                        sp.wait_ge(x1_out[j], i2 * 16)
                        sp.wait_ge(tl, i2 * 2 + j)
                        x_tile(i2 * 2 + j, j)

            @block.gpsimd
            def _(pool):
                nc.gpsimd.memset(zero[:], 0.0).then_inc(z_done, 1)
                pool.wait_ge(z_done, 1)
                pool.dma_start(self.x1_d[S:NROW, :], zero[:]).then_inc(z_out, 16)
                pool.dma_start(self.y_d[S:NROW, :], zero[:]).then_inc(z_out, 16)
                with pool.Fori(0, NT // 2) as i2:
                    for j in range(2):
                        i = i2 * 2 + j
                        pool.wait_ge(nrm, i * 3 + 2)
                        nc.gpsimd.tensor_tensor(y[j][:], y[j][:], b_b[:], ALU.add).then_inc(x1_ready, 1)
                        pool.wait_ge(x1_ready, i + 1)
                        pool.dma_start(self.x1_d[bass.ds(i * P, P), :], y[j][:]).then_inc(x1_out[j], 16)
                for j in range(2):
                    pool.wait_ge(x1_out[j], NT // 2 * 16)
                pool.wait_ge(z_out, 32)

            @block.tensor
            def _(pe):
                def transposes(i, j):
                    pe.wait_ge(x1_ready, i + 1)
                    for k in range(KT):
                        last = nc.tensor.transpose(tp[j][:, k // 4, k % 4, :], y[j][:, k * P:(k + 1) * P], self.ident[:])
                    last.then_inc(tr_done, 1)

                def tile(i, j, prev):
                    pe.wait_ge(h_lo, i + 1)
                    pe.wait_ge(res, i)
                    for hf in range(2):
                        for k in range(KT):
                            if not prev and hf == 0 and k % (KT // PARTS) == 0:
                                pe.wait_ge(w_lo, k // (KT // PARTS) + 1)
                            last = split3(nc, ps[j][:, hf, :], hh[j][:, k, :], hl[j][:, k, :],
                                          wh[:, k, hf * HALF:(hf + 1) * HALF], wl[:, k, hf * HALF:(hf + 1) * HALF],
                                          k == 0, k == KT - 1)
                    last.then_inc(mm_done, 1)
                    if prev:
                        transposes(i - 1, 1 - j)

                tile(0, 0, False)
                tile(1, 1, True)
                with pe.Fori(1, NT // 2) as i2:
                    for j in range(2):
                        pe.wait_ge(tl, i2 * 2 + j - 1)
                        tile(i2 * 2 + j, j, True)
                transposes(NT - 1, 1)

            @block.scalar
            def _(act):
                A = nc.scalar.activation

                def h_split(n, i2, j, wait):
                    act.wait_ge(h_in[j], i2 * 16 + 16)
                    if wait:
                        act.wait_ge(mm_done, n - 1)
                    A(hh[j][:], hraw[j][:], ACT.Copy).then_inc(h_hi, 1)

                def tile(i, j, more):
                    act.wait_ge(st, i * 3 + 3)
                    A(rs[:], mv[:, 1:2], ACT.Sqrt, bias=self.eps[:]).then_inc(sq, 1)
                    if more is not None:
                        h_split(more * 2 + j, more, j, True)
                    act.wait_ge(tr_done, i + 1)
                    A(self.x1_hi[:, :, bass.ds(i * P, P)].rearrange("p (b k) t -> p b k t", b=2), tp[j][:],
                      ACT.Copy).then_inc(th, 1)

                h_split(0, 0, 0, False)
                for i, ks in enumerate(parts):
                    act.wait_ge(w_in[i], 16)
                    A(wh[:, ks, :], wraw[i % 3][:], ACT.Copy).then_inc(w_hi, 1)
                h_split(1, 0, 1, False)
                with act.Fori(0, NT // 2 - 1) as i2:
                    for j in range(2):
                        tile(i2 * 2 + j, j, i2 + 1)
                for j in range(2):
                    tile(NT - 2 + j, j, None)

            @block.vector
            def _(dve):
                v = nc.vector

                def h_split(n, j):
                    dve.wait_ge(h_hi, n + 1)
                    v.tensor_tensor(hl[j][:], hraw[j][:], hh[j][:].bitcast(F32), ALU.subtract).then_inc(h_lo, 1)

                def finish(i, j):
                    dve.wait_ge(th, i + 1)
                    for b in range(2):
                        last = v.tensor_tensor(self.x1_lo[:, 4 * b:4 * b + 4, bass.ds(i * P, P)], tp[j][:, b],
                                               self.x1_hi[:, 4 * b:4 * b + 4, bass.ds(i * P, P)].bitcast(F32),
                                               ALU.subtract)
                    last.then_inc(tl, 1)

                def tile(i, j, i2, more):
                    dve.wait_ge(mm_done, i + 1)
                    dve.wait_ge(xr_in[j], i2 * 16 + 16)
                    v.scalar_tensor_tensor(out=y[j][:], in0=y[j][:], scalar=ALPHA,
                                           in1=ps[j][:].rearrange("p a b -> p (a b)"), op0=ALU.mult, op1=ALU.add
                                           ).then_inc(res, 1)
                    dve.wait_ge(res, i + 2)
                    self.norm_stats(dve, y[j], stats, mv, st, i * 3, self.passed)
                    dve.wait_ge(sq, i + 1)
                    v.reciprocal(rs[:], rs[:]).then_inc(nrm, 1)
                    dve.wait_ge(nrm, i * 3 + 1)
                    v.tensor_scalar(y[j][:], y[j][:], mv[:, 0:1], rs[:], ALU.subtract, ALU.mult).then_inc(rstd, 1)
                    dve.wait_ge(rstd, i + 1)
                    v.tensor_tensor(y[j][:], y[j][:], g_b[:], ALU.mult).then_inc(nrm, 2)
                    if more:
                        h_split(i + 2, j)
                    finish(i, j)

                dve.sem_inc(res, 1)
                dve.sem_inc(tl, 1)
                h_split(0, 0)
                for i, ks in enumerate(parts):
                    dve.wait_ge(w_hi, i + 1)
                    v.tensor_tensor(wl[:, ks, :], wraw[i % 3][:], wh[:, ks, :].bitcast(F32), ALU.subtract
                                    ).then_inc(w_lo, 1)
                h_split(1, 1)
                dve.wait_ge(par_in, 32)
                with dve.Fori(0, NT // 2 - 1) as i2:
                    for j in range(2):
                        tile(i2 * 2 + j, j, i2, True)
                for j in range(2):
                    tile(NT - 2 + j, j, NT // 2 - 1, False)

    def shared_and_route(self):
        nc, sb, a = self.nc, self.sb, self.a
        with ExitStack() as ctx:
            wsr = [sb(ctx, f"sh_raw{j}", [P, KT, P]) for j in range(2)]
            wsh = [sb(ctx, f"sh_hi{j}", [P, KT, P], F32R) for j in range(2)]
            wsl = [sb(ctx, f"sh_lo{j}", [P, KT, P], F32R) for j in range(2)]
            wdr = sb(ctx, "shd_raw", [P, 2, D])
            wdh = sb(ctx, "shd_hi", [P, 2, D], F32R)
            wdl = sb(ctx, "shd_lo", [P, 2, D], F32R)
            hid = sb(ctx, "sh_hid", [P, 2, S])
            hidh = sb(ctx, "sh_hid_hi", [P, 2, S], F32R)
            hidl = sb(ctx, "sh_hid_lo", [P, 2, S], F32R)
            yt = [sb(ctx, f"sh_y{j}", [P, D]) for j in range(2)]
            wrr = sb(ctx, "wr_raw", [P, KT, P])
            wrh = sb(ctx, "wr_hi", [P, KT, P], F32R)
            wrl = sb(ctx, "wr_lo", [P, KT, P], F32R)
            sT = sb(ctx, "score_t", [E, S])
            s_, bi, ma, se, we, va, rep = (sb(ctx, n, [P, NT, E]) for n in (
                "score", "biased", "masked_sc", "selected", "weight", "slot_val", "replaced"))
            bias_b = sb(ctx, "bias_b", [P, E])
            g8 = sb(ctx, "group_top", [P, NT * NGRP, 8])
            gs = sb(ctx, "group_score", [P, NT, NGRP])
            cmp_, cmq = (sb(ctx, n, [P, NT * NGRP, NGRP]) for n in ("cmp_gt", "cmp_eq"))
            lt = sb(ctx, "lower_index", [P, NGRP, NGRP])
            grk = sb(ctx, "group_rank", [P, NT * NGRP])
            t8 = sb(ctx, "top8", [P, NT, 8])
            s8 = sb(ctx, "slot8", [P, NT, 8])
            si8 = sb(ctx, "slot8_i", [P, NT * 8], U32)
            sums = sb(ctx, "w_sum", [P, NT])
            ebase = sb(ctx, "e_base", [P, E])
            pair = sb(ctx, "tok_weight", [P, NT * 8, 2])
            eq8 = sb(ctx, "eq8", [P, 8, E])
            cnt = sb(ctx, "count", [P, E])
            thr = sb(ctx, "thr", [P, NT])
            cge = sb(ctx, "cge", [P, E, NT])
            nb = sb(ctx, "n_blocks", [P, E])
            nbc = sb(ctx, "n_blocks_cum", [P, E])
            one_r = sb(ctx, "ones_row", [P, E])
            tmp2 = sb(ctx, "tmp2", [P, 8])
            s_idx = [sb(ctx, f"s_idx{j}", [P, 1], U32) for j in range(1)]
            ps = [ctx.enter_context(nc.psum_tensor(f"sh_ps{j}", [P, 2, HALF], F32)) for j in range(2)]
            rps = ctx.enter_context(nc.psum_tensor("rt_ps", [P, 2, HALF], F32))
            pos_ps = ctx.enter_context(nc.psum_tensor("pos_ps", [P, NT, E], F32))
            cnt_ps = ctx.enter_context(nc.psum_tensor("cnt_ps", [P, HALF], F32))
            w_in = [self.sems(ctx, f"sh_in{j}") for j in range(2)]
            y_in = [self.sems(ctx, f"shx_in{j}") for j in range(2)]
            (wr_in, b_in, wd_in, wr_hi, wr_lo, wr_z, r_mm, r_sig, r_tr, dv, pos_done, cnt_done, fill_in, w_hi, w_lo, mm_s,
             act_s, hid_s, hh_s, hl_s, wdh_s, wdl_s, mm_d, y_add, y_out, pool_c, scat, sl_ready, cut) = self.sems(
                ctx, "wr_in", "rb_in", "shd_in", "wr_hi_s", "wr_lo_s", "wr_z", "r_mm", "r_sig", "r_tr", "rt_dve",
                "pos_done", "cnt_done", "fill_in", "sh_hi_s", "sh_lo_s", "sh_mm", "sh_act", "sh_hid_s",
                "sh_hh", "sh_hl", "shd_hi_s", "shd_lo_s", "sh_dn", "sh_add", "sh_out", "rt_pool", "scat", "sl_ready",
                "cut")
            self.sel_done = self.sems(ctx, "sel_done")
            block = ctx.enter_context(nc.Block())
            fl = lambda x: x.rearrange("p a b -> p (a b)")
            sel_done = self.sel_done

            @block.sync
            def _(sp):
                sp.wait_ge(wr_z, 1)
                sp.dma_start(wrr[:, :, 0:E], a["w_router"][0].rearrange("(k p) n -> p k n", p=P)).then_inc(wr_in, 16)
                sp.dma_start(bias_b[:], a["router_bias"][0, :].partition_broadcast(P)).then_inc(b_in, 16)
                for m in range(4):
                    if m >= 2:
                        sp.wait_ge(w_lo, m - 1)
                    w = (a["w_sh_gate"], a["w_sh_up"])[m % 2][0, :, (m // 2) * P:(m // 2 + 1) * P]
                    sp.dma_start(wsr[m % 2][:], w.rearrange("(k p) n -> p k n", p=P)).then_inc(w_in[m % 2], 16)
                sp.dma_start(wdr[:], a["w_sh_down"][0].rearrange("(c p) n -> p c n", p=P)).then_inc(wd_in, 16)
                for i in range(NT):
                    if i >= 2:
                        sp.wait_ge(y_out, 16 * (i - 1))
                    sp.dma_start(yt[i % 2][:], self.x1_d[i * P:(i + 1) * P, :]).then_inc(y_in[i % 2], 16)
                    if i >= 1:
                        k = i - 1
                        sp.wait_ge(y_add, k + 1)
                        sp.dma_start(self.y_d[k * P:(k + 1) * P, :], yt[k % 2][:]).then_inc(y_out, 16)
                sp.wait_ge(y_add, NT)
                sp.dma_start(self.y_d[S - P:S, :], yt[1][:]).then_inc(y_out, 16)
                sp.wait_ge(y_out, 16 * NT)

            @block.tensor
            def _(pe):
                mm = nc.tensor.matmul
                pe.wait_ge(wr_lo, 1)
                for hf in range(2):
                    for k in range(KT):
                        last = split3(nc, rps[:, hf, :], wrh[:, k, :], wrl[:, k, :],
                                      self.x1_hi[:, k, hf * HALF:(hf + 1) * HALF],
                                      self.x1_lo[:, k, hf * HALF:(hf + 1) * HALF], k == 0, k == KT - 1)
                last.then_inc(r_mm, 1)
                pe.wait_ge(r_sig, 1)
                for t in range(NT):
                    last = nc.tensor.transpose(pos_ps[:, t, :], sT[:, t * P:(t + 1) * P], self.ident[0:E, 0:E])
                last.then_inc(r_tr, 1)

                def up(m):
                    pe.wait_ge(w_lo, m + 1)
                    if m >= 2:
                        pe.wait_ge(hid_s, m // 2)
                    for hf in range(2):
                        for k in range(KT):
                            last = split3(nc, ps[m % 2][:, hf, :], wsh[m % 2][:, k, :], wsl[m % 2][:, k, :],
                                          self.x1_hi[:, k, hf * HALF:(hf + 1) * HALF],
                                          self.x1_lo[:, k, hf * HALF:(hf + 1) * HALF], k == 0, k == KT - 1)
                    last.then_inc(mm_s, 1)

                up(0)
                up(1)
                pe.wait_ge(self.sel_done, 1)
                for t in range(NT):
                    for t2 in range(t):
                        mm(pos_ps[:, t, :], self.ones[:], se[:, t2, :], start=t2 == 0, stop=False)
                    last = mm(pos_ps[:, t, :], self.tri_excl[:], se[:, t, :], start=t == 0, stop=True)
                last.then_inc(pos_done, 1)
                for t in range(NT):
                    last = mm(cnt_ps[:, 0:E], self.ones[:], se[:, t, :], start=t == 0, stop=t == NT - 1)
                last.then_inc(cnt_done, 1)
                up(2)
                up(3)
                pe.wait_ge(wdl_s, 1)
                pe.wait_ge(hl_s, 2)
                for i in range(NT):
                    if i >= 2:
                        pe.wait_ge(y_add, i - 1)
                    for hf in range(2):
                        for c in range(2):
                            last = split3(nc, ps[i % 2][:, hf, :], hidh[:, c, i * P:(i + 1) * P],
                                          hidl[:, c, i * P:(i + 1) * P], wdh[:, c, hf * HALF:(hf + 1) * HALF],
                                          wdl[:, c, hf * HALF:(hf + 1) * HALF], c == 0, c == 1)
                    last.then_inc(mm_d, 1)

            @block.scalar
            def _(act):
                A = nc.scalar.activation
                act.wait_ge(wr_in, 16)
                A(wrh[:], wrr[:], ACT.Copy).then_inc(wr_hi, 1)

                def hi(m):
                    act.wait_ge(w_in[m % 2], (m // 2 + 1) * 16)
                    if m >= 2:
                        act.wait_ge(mm_s, m - 1)
                    A(wsh[m % 2][:], wsr[m % 2][:], ACT.Copy).then_inc(w_hi, 1)

                hi(0)
                hi(1)
                act.wait_ge(r_mm, 1)
                A(sT[:], fl(rps[0:E]), ACT.Sigmoid).then_inc(r_sig, 1)
                for c in range(2):
                    act.wait_ge(mm_s, 2 * c + 1)
                    A(hid[:, c, :], fl(ps[0][:]), ACT.Silu).then_inc(act_s, 1)
                    if c == 0:
                        hi(2)
                        hi(3)
                    act.wait_ge(hid_s, c + 1)
                    A(hidh[:, c, :], hid[:, c, :], ACT.Copy).then_inc(hh_s, 1)
                act.wait_ge(wd_in, 16)
                A(wdh[:], wdr[:], ACT.Copy).then_inc(wdh_s, 1)

            @block.vector
            def _(dve):
                v = nc.vector
                tt = v.tensor_tensor
                n = [0]

                def step(ins):
                    n[0] += 1
                    ins.then_inc(dv, 1)
                    dve.wait_ge(dv, n[0])

                def lo(m):
                    dve.wait_ge(w_hi, m + 1)
                    tt(wsl[m % 2][:], wsr[m % 2][:], wsh[m % 2][:].bitcast(F32), ALU.subtract).then_inc(w_lo, 1)

                def hidden(c):
                    dve.wait_ge(mm_s, 2 * c + 2)
                    dve.wait_ge(act_s, c + 1)
                    tt(hid[:, c, :], hid[:, c, :], fl(ps[1][:]), ALU.mult).then_inc(hid_s, 1)
                    dve.wait_ge(hh_s, c + 1)
                    tt(hidl[:, c, :], hid[:, c, :], hidh[:, c, :].bitcast(F32), ALU.subtract).then_inc(hl_s, 1)

                v.memset(wrr[:], 0.0).then_inc(wr_z, 1)
                dve.wait_ge(wr_hi, 1)
                tt(wrl[:], wrr[:], wrh[:].bitcast(F32), ALU.subtract).then_inc(wr_lo, 1)
                lo(0)
                lo(1)
                dve.wait_ge(r_tr, 1)
                dve.wait_ge(b_in, 16)
                bb = bias_b[:].unsqueeze(1).to_broadcast([P, NT, E])
                step(v.tensor_copy(s_[:], pos_ps[:]))
                step(tt(bi[:], s_[:], bb, ALU.add))
                groups = fl(bi[:]).rearrange("p (g e) -> p g e", e=E // NGRP)
                for i in range(NT * NGRP):
                    last = v.max(g8[:, i, :], groups[:, i, :])
                step(last)
                step(tt(fl(gs[:]).unsqueeze(2), g8[:, :, 0:1], g8[:, :, 1:2], ALU.add))
                gsf = fl(gs[:])
                other = gs[:].unsqueeze(2).to_broadcast([P, NT, NGRP, NGRP])
                mine = gsf.unsqueeze(2).to_broadcast([P, NT * NGRP, NGRP])
                c4 = lambda x: x[:].rearrange("p (t g) o -> p t g o", t=NT)
                mine4 = gs[:].unsqueeze(3).to_broadcast([P, NT, NGRP, NGRP])
                dve.wait_ge(pool_c, 6)
                for t in range(NT):
                    sl = slice(t * NGRP, (t + 1) * NGRP)
                    tt(cmp_[:, sl, :], other[:, t], mine4[:, t], ALU.is_gt)
                    last = tt(cmq[:, sl, :], other[:, t], mine4[:, t], ALU.is_equal)
                step(last)
                step(tt(c4(cmq), c4(cmq), lt[:].unsqueeze(1).to_broadcast([P, NT, NGRP, NGRP]), ALU.mult))
                step(tt(cmp_[:], cmp_[:], cmq[:], ALU.add))
                step(v.tensor_reduce(grk[:], cmp_[:], AX.X, ALU.add))
                step(v.tensor_scalar(grk[:], grk[:], 4.0, None, ALU.is_lt))
                gmask = grk[:].unsqueeze(2).to_broadcast([P, NT * NGRP, E // NGRP])
                mg = fl(ma[:]).rearrange("p (g e) -> p g e", e=E // NGRP)
                rg = fl(rep[:]).rearrange("p (g e) -> p g e", e=E // NGRP)
                step(tt(mg, groups, gmask, ALU.mult))
                step(v.tensor_scalar(grk[:], grk[:], 1.0, BIG, ALU.subtract, ALU.mult))
                step(tt(mg, mg, gmask, ALU.add))
                for t in range(NT):
                    last = v.max(t8[:, t, :], ma[:, t, :])
                step(last)
                for t in range(NT):
                    last = v.match_replace(rep[:, t, :], t8[:, t, :], ma[:, t, :], -3.4e38)
                step(last)
                tt(se[:], rep[:], ma[:], ALU.not_equal).then_inc(self.sel_done, 1)
                dve.wait_ge(self.sel_done, 1)
                step(tt(we[:], s_[:], se[:], ALU.mult))
                step(v.tensor_reduce(sums[:], we[:], AX.X, ALU.add))
                step(v.reciprocal(sums[:], sums[:]))
                step(v.tensor_scalar(sums[:], sums[:], ROUTED_SCALE, None, ALU.mult))
                step(tt(we[:], we[:], sums[:].unsqueeze(2).to_broadcast([P, NT, E]), ALU.mult))
                lo(2)
                lo(3)
                hidden(0)
                dve.wait_ge(pos_done, 1)
                step(tt(va[:], pos_ps[:], ebase[:].unsqueeze(1).to_broadcast([P, NT, E]), ALU.add))
                step(tt(va[:], va[:], se[:], ALU.mult))
                for t in range(NT):
                    last = v.max(s8[:, t, :], va[:, t, :])
                step(last)
                for t in range(NT):
                    step(tt(eq8[:], va[:, t, :].unsqueeze(1).to_broadcast([P, 8, E]),
                            s8[:, t, :].unsqueeze(2).to_broadcast([P, 8, E]), ALU.is_equal))
                    step(tt(eq8[:], eq8[:], we[:, t, :].unsqueeze(1).to_broadcast([P, 8, E]), ALU.mult))
                    step(v.tensor_reduce(tmp2[:], eq8[:], AX.X, ALU.add))
                    step(v.tensor_copy(pair[:, t * 8:(t + 1) * 8, 1:2], tmp2[:].unsqueeze(2)))
                v.tensor_scalar(si8[:], fl(s8[:]), 1.0, None, ALU.subtract).then_inc(sl_ready, 1)
                dve.wait_ge(sl_ready, 1)
                dve.wait_ge(cnt_done, 1)
                step(v.tensor_copy(cnt[:], cnt_ps[:, 0:E]))
                step(tt(cge[:], cnt[:].unsqueeze(2).to_broadcast([P, E, NT]),
                        thr[:].unsqueeze(1).to_broadcast([P, E, NT]), ALU.is_gt))
                step(v.tensor_reduce(nb[:], cge[:], AX.X, ALU.add))
                step(v.memset(one_r[:], 1.0))
                step(v.tensor_tensor_scan(nbc[:], one_r[:], nb[:], 0.0, ALU.mult, ALU.add))
                step(tt(nbc[:], nbc[:], nb[:], ALU.subtract))
                step(v.tensor_copy(self.plan[:, :, 0:1], nb[0:1, :].unsqueeze(2)))
                step(v.tensor_copy(self.plan[:, :, 1:2], nbc[0:1, :].unsqueeze(2)))
                hidden(1)
                dve.wait_ge(wdh_s, 1)
                tt(wdl[:], wdr[:], wdh[:].bitcast(F32), ALU.subtract).then_inc(wdl_s, 1)
                for i in range(NT):
                    dve.wait_ge(mm_d, i + 1)
                    dve.wait_ge(y_in[i % 2], (i // 2 + 1) * 16)
                    v.scalar_tensor_tensor(out=yt[i % 2][:], in0=yt[i % 2][:], scalar=ALPHA, in1=fl(ps[i % 2][:]),
                                           op0=ALU.mult, op1=ALU.add).then_inc(y_add, 1)

            @block.gpsimd
            def _(pool):
                g = nc.gpsimd
                g.memset(lt[:], 1.0).then_inc(pool_c, 1)
                pool.wait_ge(pool_c, 1)
                g.affine_select(out=lt[:], in_=lt[:], compare_op=ALU.is_gt, fill=0.0, base=0,
                                pattern=[[1, NGRP], [-1, NGRP]], channel_multiplier=0).then_inc(pool_c, 1)
                g.iota(ebase[:], pattern=[[S, E]], base=1, channel_multiplier=0,
                       allow_small_or_imprecise_dtypes=True).then_inc(pool_c, 1)
                g.iota(thr[:], pattern=[[P, NT]], base=0, channel_multiplier=0,
                       allow_small_or_imprecise_dtypes=True).then_inc(pool_c, 1)
                pool.wait_ge(pool_c, 4)
                g.memset(thr[:, 0:1], -1.0).then_inc(pool_c, 1)
                g.iota(pair[:, :, 0:1].rearrange("p (t k) o -> p t (k o)", k=8), pattern=[[P, NT], [0, 8]], base=0,
                       channel_multiplier=1, allow_small_or_imprecise_dtypes=True).then_inc(pool_c, 1)
                pool.wait_ge(sl_ready, 1)
                for i in range(NT * 8):
                    pool.indirect_dma_start(self.slot_d, bass.IndirectOffsetOnAxis(si8[:, i:i + 1], 0),
                                            pair[:, i, :], None).then_inc(scat, 16)
                pool.wait_ge(scat, NT * 8 * 16)

    def block_tables(self):
        nc, sb = self.nc, self.sb
        Q = E * NT // P
        with ExitStack() as ctx:
            rows = sb(ctx, "slot_rows", [P, Q, P, 2])
            ps = ctx.enter_context(nc.psum_tensor("tab_ps", [P, 2, Q, P], F32))
            r_in, tr_done, tab = self.sems(ctx, "rows_in", "tab_tr", "tab_done")
            tok = sb(ctx, "tok_rows", [P, Q, P])
            wts = sb(ctx, "wt_rows", [P, Q, P])
            block = ctx.enter_context(nc.Block())

            @block.sync
            def _(sp):
                sp.dma_start(rows[:].rearrange("p q s c -> p q (s c)"),
                             self.slot_d.rearrange("(q p s) c -> p q (s c)", p=P, s=P)).then_inc(r_in, 16)

            @block.vector
            def _(dve):
                v = nc.vector
                dve.wait_ge(r_in, 16)
                v.tensor_copy(tok[:].unsqueeze(3), rows[:, :, :, 0:1])
                v.tensor_copy(wts[:].unsqueeze(3), rows[:, :, :, 1:2]).then_inc(tab, 1)
                dve.wait_ge(tr_done, 1)
                v.tensor_copy(self.tok_tab[:], ps[:, 0].rearrange("p q s -> p (q s)"))
                v.tensor_copy(self.wt_tab[:], ps[:, 1].rearrange("p q s -> p (q s)")).then_inc(tab, 1)

            @block.tensor
            def _(pe):
                pe.wait_ge(tab, 1)
                for q in range(Q):
                    nc.tensor.transpose(ps[:, 0, q, :], tok[:, q, :], self.ident[:])
                    last = nc.tensor.transpose(ps[:, 1, q, :], wts[:, q, :], self.ident[:])
                last.then_inc(tr_done, 1)

    def experts(self):
        nc, sb, a = self.nc, self.sb, self.a
        with ExitStack() as ctx:
            PIECES = 6
            BUFS = 3
            SLOTS = 6
            raw = [sb(ctx, f"e_raw{q}", [P, 2 * 2 * FF]) for q in range(SLOTS)]
            wh = [sb(ctx, f"e_hi{j}", [P, KT, 2, FF], F32R) for j in range(BUFS)]
            wl = [sb(ctx, f"e_lo{j}", [P, KT, 2, FF], F32R) for j in range(BUFS)]
            dh = [sb(ctx, f"ed_hi{j}", [P, 2, D], F32R) for j in range(BUFS)]
            dl = [sb(ctx, f"ed_lo{j}", [P, 2, D], F32R) for j in range(BUFS)]
            xg = sb(ctx, "x_gather", [P, D])
            xh = sb(ctx, "xg_hi", [P, KT, P], F32R)
            xl = sb(ctx, "xg_lo", [P, KT, P], F32R)
            sg = sb(ctx, "gate_act", [P, 2, P])
            hid = sb(ctx, "hidden", [P, 2, P])
            hh = sb(ctx, "hid_hi", [P, 2, P], F32R)
            hl = sb(ctx, "hid_lo", [P, 2, P], F32R)
            yb = sb(ctx, "y_block", [P, D])
            idx_g, idx_1, idx_2, idx_s = (sb(ctx, n, [P, 1], U32) for n in ("idx_gather", "idx_1", "idx_2", "idx_scatter"))
            gu = [ctx.enter_context(nc.psum_tensor(f"gu_ps{h}", [P, 2, P], F32)) for h in range(2)]
            xt = ctx.enter_context(nc.psum_tensor("xg_ps", [P, 2, 4, P], F32))
            ht = [ctx.enter_context(nc.psum_tensor(f"ht_ps{h}", [P, P], F32)) for h in range(2)]
            yp = ctx.enter_context(nc.psum_tensor("y_ps", [P, 2, HALF], F32))
            w_in = [self.sems(ctx, f"e_in{q}_gate", f"e_in{q}_up") for q in range(SLOTS)]
            d_in = self.sems(ctx, *(f"e_in{q}_down" for q in range(SLOTS)))
            (hi_s, lo_s, xg_in, t_done, xh_s, xl_s, gu_done, sg_s, hid_s, ht_done, hh_s, hl_s, y_done, y_ready,
             idx_c, idx_t, scat, init) = self.sems(
                ctx, "e_hi_s", "e_lo_s", "xg_in", "xg_tr", "xg_hi_s", "xg_lo_s", "gu_done", "sg_s",
                "hid_s", "ht_done", "hh_s", "hl_s", "yb_done", "yb_ready", "idx_moved", "idx_s_s", "y_scat", "e_init")
            block = ctx.enter_context(nc.Block())
            fl = lambda x: x.rearrange("p a b -> p (a b)")

            def piece(j, i):
                q = (j * PIECES + i) % SLOTS
                if i < 4:
                    s = slice(2 * i, 2 * i + 2)
                    return q, raw[q][:].rearrange("p (k w f) -> p k w f", k=2, w=2), wh[j][:, s], wl[j][:, s]
                return q, raw[q][:], dh[j][:, i - 4], dl[j][:, i - 4]

            def plan(eng, e):
                row = self.plan[0:1, bass.ds(e, 1), :]
                nb = eng.value_load(row[:, :, 0:1].rearrange("p a b -> p (a b)"), min_val=1, max_val=NT)
                base = eng.value_load(row[:, :, 1:2].rearrange("p a b -> p (a b)"), min_val=0, max_val=E * NT)
                return nb, base

            def all_experts(eng, expert):
                with eng.Fori(0, E // BUFS - 1) as e3:
                    for j in range(BUFS):
                        expert(e3 * BUFS + j, j, e3, True)
                for e in range(E // BUFS * BUFS - BUFS, E):
                    expert(e, e % BUFS, e // BUFS, e + 2 < E)

            def loads_before(j, i, nth):
                q, down = (j * PIECES + i) % SLOTS, i >= 4
                same = [(jj, ii) for jj in range(BUFS) for ii in range(PIECES)
                        if (jj * PIECES + ii) % SLOTS == q and (ii >= 4) == down]
                return (nth * len(same) + same.index((j, i)) + 1) * 16

            @block.sync
            def _(sp):
                def load(e, j):
                    for i in range(PIECES):
                        q, r, _, _ = piece(j, i)
                        if not isinstance(e, int) or e * PIECES + i >= SLOTS:
                            sp.wait_ge(lo_s, e * PIECES + (i + 1 - SLOTS))
                        if i < 4:
                            for n, w in enumerate((a["w_gate_e"], a["w_up_e"])):
                                sp.dma_start(r[:, :, n, :],
                                             w[0, bass.ds(e, 1)].rearrange("o (p k) f -> p (o k) f", k=KT)
                                             [:, 2 * i:2 * i + 2, :]).then_inc(w_in[q][n], 16)
                        else:
                            sp.dma_start(r, a["w_down_e"][0, bass.ds(e, 1)].rearrange("o (c p) n -> p (o c) n", p=P)
                                         [:, i - 4, :]).then_inc(d_in[q], 16)

                for j in range(BUFS):
                    load(j, j)
                with sp.Fori(1, E // BUFS) as e3:
                    for j in range(BUFS):
                        load(e3 * BUFS + j, j)
                for e in range(E // BUFS * BUFS, E):
                    load(e, e % BUFS)

            @block.gpsimd
            def _(pool):
                g = nc.gpsimd
                g.memset(yb[:], 0.0).then_inc(init, 1)
                g.iota(idx_g[:], pattern=[[0, 1]], base=S, channel_multiplier=1).then_inc(init, 1)
                pool.wait_ge(init, 2)

                def gather():
                    alone(pool, self.passed)
                    pool.indirect_dma_start(xg[:], None, self.x1_d, bass.IndirectOffsetOnAxis(idx_g[:, 0:1], 0)
                                            ).then_inc(xg_in, 16)

                def scatter():
                    alone(pool, self.passed)
                    pool.indirect_dma_start(self.y_d, bass.IndirectOffsetOnAxis(idx_s[:, 0:1], 0), yb[:], None,
                                            compute_op=ALU.add).then_inc(scat, 16)

                def row_numbers(n, column):
                    pool.wait_ge(xg_in, n * 16 + 16)
                    alone(pool, self.passed)
                    g.tensor_copy(idx_2[:], idx_1[:]).then_inc(idx_c, 1)
                    pool.wait_ge(idx_c, n * 3 + 1)
                    alone(pool, self.passed)
                    g.tensor_copy(idx_1[:], idx_g[:]).then_inc(idx_c, 1)
                    if column is not None:
                        pool.wait_ge(idx_c, n * 3 + 2)
                        alone(pool, self.passed)
                        g.tensor_copy(idx_g[:], column).then_inc(idx_c, 1)
                    else:
                        pool.sem_inc(idx_c, 1)
                    pool.wait_ge(idx_c, n * 3 + 3)

                def add(n):
                    pool.wait_ge(scat, n * 16 + 16)
                    alone(pool, self.passed)
                    g.tensor_copy(idx_s[:], idx_2[:]).then_inc(idx_t, 1)
                    pool.wait_ge(idx_t, n + 1)
                    pool.wait_ge(y_ready, n + 1)
                    scatter()

                pool.sem_inc(t_done, 1)
                pool.sem_inc(y_ready, 2)
                for n, dst in enumerate((idx_s, idx_1)):
                    g.tensor_copy(dst[:], idx_g[:]).then_inc(init, 1)
                pool.wait_ge(init, 4)
                gather()
                scatter()
                with pool.Fori(0, E) as e:
                    nb, base = plan(pool, e)
                    with pool.Fori(0, nb) as b:
                        n = base + b
                        row_numbers(n, self.tok_tab[:, bass.ds(e * NT + b, 1)])
                        pool.wait_ge(t_done, n * 2 + 1)
                        gather()
                        add(n)
                total = pool.value_load(self.plan[0:1, E - 1, 1:2], min_val=0, max_val=E * NT) + \
                    pool.value_load(self.plan[0:1, E - 1, 0:1], min_val=1, max_val=NT)
                row_numbers(total, None)
                pool.wait_ge(t_done, total * 2 + 1)
                gather()
                add(total)
                pool.wait_ge(xg_in, total * 16 + 32)
                row_numbers(total + 1, None)
                add(total + 1)
                pool.wait_ge(scat, total * 16 + 48)

            @block.tensor
            def _(pe):
                def transposes(gb, half):
                    if half == 0:
                        pe.wait_ge(xg_in, gb * 16 + 32)
                    xv = xg[:].rearrange("p (c k) -> p k c", k=KT)
                    for k in range(4 * half, 4 * half + 4):
                        last = nc.tensor.transpose(xt[:, k // 4, k % 4, :], xv[:, k, :], self.ident[:])
                    last.then_inc(t_done, 1)

                def gate_up(j, h, ks, last_k):
                    out = gu[h][:]
                    for k in ks:
                        last = split3(nc, out, xh[:, k, :], xl[:, k, :], wh[j][:, k, :, h * P:(h + 1) * P],
                                      wl[j][:, k, :, h * P:(h + 1) * P], k == 0, k == KT - 1)
                    if last_k:
                        last.then_inc(gu_done, 1)

                def hid_t(gb, h):
                    pe.wait_ge(hid_s, gb * 2 + h + 1)
                    nc.tensor.transpose(ht[h][:], hid[:, h, :], self.ident[:]).then_inc(ht_done, 1)

                def down(j, h, hf):
                    return split3(nc, yp[:, hf, :], hh[:, h, :], hl[:, h, :], dh[j][:, h, hf * HALF:(hf + 1) * HALF],
                                  dl[j][:, h, hf * HALF:(hf + 1) * HALF], h == 0, h == 1)

                def blk(e, j, gb, first):
                    def products(h, kh):
                        if h == 0:
                            pe.wait_ge(xl_s, gb * 2 + kh + 1)
                            if first:
                                pe.wait_ge(lo_s, e * PIECES + 2 * kh + 2)
                        gate_up(j, h, range(4 * kh, 4 * kh + 4), kh == 1)

                    products(0, 0)
                    products(0, 1)
                    products(1, 0)
                    transposes(gb + 1, 0)
                    hid_t(gb, 0)
                    products(1, 1)
                    transposes(gb + 1, 1)
                    pe.wait_ge(hl_s, gb * 2 + 1)
                    if first:
                        pe.wait_ge(lo_s, e * PIECES + PIECES)
                    pe.wait_ge(y_ready, gb + 2)
                    down(j, 0, 0)
                    hid_t(gb, 1)
                    down(j, 0, 1)
                    pe.wait_ge(hl_s, gb * 2 + 2)
                    down(j, 1, 0)
                    down(j, 1, 1).then_inc(y_done, 1)

                def expert(e, j, nth, more):
                    nb, base = plan(pe, e)
                    blk(e, j, base, True)
                    with pe.If(nb > 1):
                        with pe.Fori(1, nb) as b:
                            blk(e, j, base + b, False)

                transposes(0, 0)
                transposes(0, 1)
                all_experts(pe, expert)

            @block.scalar
            def _(act):
                A = nc.scalar.activation

                def hi(j, nth, i):
                    q, r, h, _ = piece(j, i)
                    for sem in w_in[q] if i < 4 else (d_in[q],):
                        act.wait_ge(sem, loads_before(j, i, nth))
                    A(h, r, ACT.Copy).then_inc(hi_s, 1)

                def x_hi(b):
                    A(xh[:, 4 * b:4 * b + 4, :], xt[:, b], ACT.Copy).then_inc(xh_s, 1)

                def blk(e, b, gb, split):
                    act.wait_ge(gu_done, gb * 2 + 1)
                    A(sg[:, 0, :], gu[0][:, 0, :], ACT.Silu).then_inc(sg_s, 1)
                    split(0, 1)
                    act.wait_ge(ht_done, gb * 2 + 1)
                    A(hh[:, 0, :], ht[0][:], ACT.Copy).then_inc(hh_s, 1)
                    split(2)
                    act.wait_ge(gu_done, gb * 2 + 2)
                    A(sg[:, 1, :], gu[1][:, 0, :], ACT.Silu).then_inc(sg_s, 1)
                    act.wait_ge(t_done, gb * 2 + 4)
                    x_hi(0)
                    act.wait_ge(ht_done, gb * 2 + 2)
                    A(hh[:, 1, :], ht[1][:], ACT.Copy).then_inc(hh_s, 1)
                    act.wait_ge(t_done, gb * 2 + 5)
                    x_hi(1)
                    split(3)
                    act.wait_ge(y_done, gb + 1)
                    act.wait_ge(scat, gb * 16 + 48)
                    A(yb[:], fl(yp[:]), ACT.Copy, scale=self.wt_tab[:, bass.ds(e * NT + b, 1)]).then_inc(y_ready, 1)
                    split(4, 5)

                def expert(e, j, nth, more):
                    nb, base = plan(act, e)

                    def split(*pieces):
                        for i in pieces if more else ():
                            hi((j + 2) % BUFS, nth + (j + 2) // BUFS, i)

                    blk(e, 0, base, split)
                    with act.If(nb > 1):
                        with act.Fori(1, nb) as b:
                            blk(e, b, base + b, lambda *pieces: None)

                for i in range(PIECES):
                    hi(0, 0, i)
                act.wait_ge(init, 2)
                act.wait_ge(t_done, 3)
                x_hi(0)
                x_hi(1)
                for i in range(PIECES):
                    hi(1, 0, i)
                all_experts(act, expert)

            @block.vector
            def _(dve):
                v = nc.vector
                tt = v.tensor_tensor

                def lo(e, j, i):
                    _, r, h, l = piece(j, i)
                    dve.wait_ge(hi_s, e * PIECES + i + 1)
                    tt(l, r, h.bitcast(F32), ALU.subtract).then_inc(lo_s, 1)

                def x_lo(gb, b):
                    dve.wait_ge(xh_s, gb * 2 + b + 1)
                    s = slice(4 * b, 4 * b + 4)
                    tt(xl[:, s, :], xt[:, b], xh[:, s, :].bitcast(F32), ALU.subtract).then_inc(xl_s, 1)

                def hidden(gb, h):
                    dve.wait_ge(sg_s, gb * 2 + h + 1)
                    tt(hid[:, h, :], sg[:, h, :], gu[h][:, 1, :], ALU.mult).then_inc(hid_s, 1)

                def hidden_lo(gb, h):
                    dve.wait_ge(hh_s, gb * 2 + h + 1)
                    tt(hl[:, h, :], ht[h][:], hh[:, h, :].bitcast(F32), ALU.subtract).then_inc(hl_s, 1)

                def blk(gb, split):
                    hidden(gb, 0)
                    split(0, 1)
                    hidden_lo(gb, 0)
                    hidden(gb, 1)
                    x_lo(gb + 1, 0)
                    hidden_lo(gb, 1)
                    x_lo(gb + 1, 1)
                    split(2, 3, 4, 5)

                def expert(e, j, nth, more):
                    nb, base = plan(dve, e)

                    def split(*pieces):
                        for i in pieces if more else ():
                            lo(e + 2, (j + 2) % BUFS, i)

                    blk(base, split)
                    with dve.If(nb > 1):
                        with dve.Fori(1, nb) as b:
                            blk(base + b, lambda *pieces: None)

                for i in range(PIECES):
                    lo(0, 0, i)
                x_lo(0, 0)
                x_lo(0, 1)
                for i in range(PIECES):
                    lo(1, 1, i)
                all_experts(dve, expert)

    def final_norm(self):
        nc, sb, a = self.nc, self.sb, self.a
        with ExitStack() as ctx:
            y = [sb(ctx, f"y2_{i}", [P, D]) for i in range(NT)]
            g_b = sb(ctx, "ln2_g_b", [P, D])
            b_b = sb(ctx, "ln2_b_b", [P, D])
            stats = [sb(ctx, f"ln2_stats{i}", [P, 2, 6]) for i in range(NT)]
            mv = [sb(ctx, f"ln2_mv{i}", [P, 2]) for i in range(NT)]
            rs = [sb(ctx, f"ln2_rs{i}", [P, 1]) for i in range(NT)]
            y_in = [self.sems(ctx, f"y2_in{i}") for i in range(NT)]
            par_in, st, sq, rc, nrm, fin, out = self.sems(ctx, "ln2_par", "ln2_st", "ln2_sq", "ln2_rc", "ln2_nrm",
                                                          "ln2_fin", "ln2_out")
            block = ctx.enter_context(nc.Block())

            @block.sync
            def _(sp):
                for i in range(NT):
                    sp.dma_start(y[i][:], self.y_d[i * P:(i + 1) * P, :]).then_inc(y_in[i], 16)
                    if i == 0:
                        sp.dma_start(g_b[:], a["ln2_g"][0, :].partition_broadcast(P)).then_inc(par_in, 16)
                        sp.dma_start(b_b[:], a["ln2_b"][0, :].partition_broadcast(P)).then_inc(par_in, 16)
                for i in range(NT):
                    sp.wait_ge(fin, i + 1)
                    sp.dma_start(a["out"][0, i * P:(i + 1) * P, :], y[i][:]).then_inc(out, 16)
                sp.wait_ge(out, NT * 16)

            @block.scalar
            def _(act):
                for i in range(NT):
                    act.wait_ge(st, i * 3 + 3)
                    nc.scalar.activation(rs[i][:], mv[i][:, 1:2], ACT.Sqrt, bias=self.eps[:]).then_inc(sq, 1)

            @block.vector
            def _(dve):
                v = nc.vector
                for i in range(NT + 1):
                    if i < NT:
                        dve.wait_ge(y_in[i], 16)
                        self.norm_stats(dve, y[i], stats[i], mv[i], st, i * 3)
                    if i >= 1:
                        n = i - 1
                        dve.wait_ge(sq, n + 1)
                        v.reciprocal(rs[n][:], rs[n][:]).then_inc(rc, 1)
                        dve.wait_ge(rc, n + 1)
                        dve.wait_ge(st, n * 3 + 3)
                        v.tensor_scalar(y[n][:], y[n][:], mv[n][:, 0:1], rs[n][:], ALU.subtract, ALU.mult).then_inc(nrm, 1)
                        dve.wait_ge(par_in, 32)
                        dve.wait_ge(nrm, 2 * n + 1)
                        v.tensor_tensor(y[n][:], y[n][:], g_b[:], ALU.mult).then_inc(nrm, 1)

            @block.gpsimd
            def _(pool):
                for n in range(NT):
                    pool.wait_ge(nrm, 2 * n + 2)
                    nc.gpsimd.tensor_tensor(y[n][:], y[n][:], b_b[:], ALU.add).then_inc(fin, 1)


_INS = ["x", "w_in", "conv_qkv", "a_log", "dt_bias", "o_norm_g", "w_oa", "dw_w", "dw_b", "cln_g", "cln_b",
        "w_ob", "w_o", "ln1_g", "ln1_b", "w_router", "router_bias", "w_gate_e", "w_up_e", "w_down_e",
        "w_sh_gate", "w_sh_up", "w_sh_down", "ln2_g", "ln2_b"]


def decoder_layer(nc, *aps, upto=99):
    a = dict(zip(_INS + ["out"], aps))
    ctx = ExitStack()
    with ctx:
        k = Kernel(nc, a)
        k.ctx = ctx
        k.constants()
        with ExitStack() as xctx:
            k.x_hi = k.sb(xctx, "x_hi", [P, KT, S], F32R)
            k.x_lo = k.sb(xctx, "x_lo", [P, KT, S], F32R)
            k.load_x()
            k.end_stage()

            k.glu()
            k.end_stage()
            if upto < 3:
                return
            k.delta_net()
            k.end_stage()
            if upto < 4:
                return
            k.branches()
            k.end_stage()
        if upto < 5:
            return
        k.plan = k.sb(ctx, "plan", [1, E, 2], I32)
        with ExitStack() as tctx:
            with ExitStack() as xctx:
                k.x1_hi = k.sb(xctx, "x1_hi", [P, KT, S], F32R)
                k.x1_lo = k.sb(xctx, "x1_lo", [P, KT, S], F32R)
                k.mix_norm()
                k.end_stage()
                if upto < 6:
                    return
                k.shared_and_route()
                k.end_stage()
            if upto < 7:
                return
            k.tok_tab = k.sb(tctx, "tok_tab", [P, E * NT], U32)
            k.wt_tab = k.sb(tctx, "wt_tab", [P, E * NT])
            k.block_tables()
            k.end_stage()
            if upto < 8:
                return
            k.experts()
            k.end_stage()
        k.final_norm()


def kernel(**inputs):
    import numpy as np
    import concourse.bacc as bacc
    from concourse.bass_utils import run_bass_kernel_spmd

    nc = bacc.Bacc("TRN2", target_bir_lowering=False, num_devices=1)
    arrays, args = {}, []
    for name in _INS:
        arr = np.ascontiguousarray(inputs[name])
        arrays[f"in_{name}_dram"] = arr
        args.append(nc.dram_tensor(f"in_{name}_dram", arr.shape, mybir.dt.from_np(arr.dtype),
                                   kind="ExternalInput").ap())
    args.append(nc.dram_tensor("out_0_dram", (1, S, D), F32, kind="ExternalOutput").ap())
    decoder_layer(nc, *args)
    r = run_bass_kernel_spmd(nc, [arrays], core_ids=[0])
    return r.results[0]["out_0_dram"]
```
